# Optimizing a Trainium2 kernel written in Bass

```python
import jax, jax.numpy as jnp
from jax import lax
import numpy as np

D_MODEL = 1024
BATCH = 1
SEQ = 1024
DEPTH = 2
DEC_BATCH = 8
DEC_SEQ = 16
PAST_LEN = 1024

CHUNK = 64
N_MIXERS = 2
N_ATT_LAYERS = (DEPTH + 1) // 2
N_MLP_LAYERS = DEPTH // 2
N_HEADS = 8
QK_NOPE_DIM = 128
QK_ROPE_DIM = 64
V_HEAD_DIM = 128
Q_LORA_RANK = 384
KV_LORA_RANK = 256
ROPE_THETA = 10000.0
Q_BLOCK = 128
SGU_CHUNK = 128
SGU_WIDTH = D_MODEL
SGU_GROUPS = 8
SGU_GROUP_DIM = SGU_WIDTH // SGU_GROUPS
D_FF = 4 * D_MODEL
EPS = 1e-6

kernel_name = 'hybrid_mla_chunkmlp_streaming_step'

def rmsnorm(x, g):
    xf = x.astype(jnp.float32)
    y = xf * lax.rsqrt(jnp.mean(xf * xf, axis=-1, keepdims=True) + EPS)
    return (y * g.astype(jnp.float32)).astype(x.dtype)

def rope(x, pos):
    half = QK_ROPE_DIM // 2
    inv = 1.0 / (ROPE_THETA ** (jnp.arange(half, dtype=jnp.float32) / half))
    ang = pos.astype(jnp.float32)[:, None] * inv[None, :]
    shape = (1, pos.shape[0]) + (1,) * (x.ndim - 3) + (half,)
    cos = jnp.cos(ang).reshape(shape)
    sin = jnp.sin(ang).reshape(shape)
    xf = x.astype(jnp.float32)
    x1, x2 = xf[..., :half], xf[..., half:]
    return jnp.concatenate([x1 * cos - x2 * sin, x2 * cos + x1 * sin], axis=-1).astype(x.dtype)

def ada_modulation(c, w, b):
    m = jax.nn.silu(c) @ w + b
    return jnp.split(m, 6, axis=-1)

def modulated_norm(x, g, shift, scale):
    return rmsnorm(x, g) * (1 + scale[:, None, :]) + shift[:, None, :]

def mla_project(h, pos, p):
    w_in, g_qa, g_kva, w_q_up, g_qn, g_qr, g_kr = p['w_in'], p['g_qa'], p['g_kva'], p['w_q_up'], p['g_qn'], p['g_qr'], p['g_kr']
    B, T, _ = h.shape
    a = h @ w_in
    cq, ckv, kr = jnp.split(a, [Q_LORA_RANK, Q_LORA_RANK + KV_LORA_RANK], axis=-1)
    cq = rmsnorm(cq, g_qa)
    ckv = rmsnorm(ckv, g_kva)
    q = (cq @ w_q_up).reshape(B, T, N_HEADS, QK_NOPE_DIM + QK_ROPE_DIM)
    qn = rmsnorm(q[..., :QK_NOPE_DIM], g_qn)
    qr = rope(rmsnorm(q[..., QK_NOPE_DIM:], g_qr), pos)
    kr = rope(rmsnorm(kr, g_kr), pos)
    return qn, qr, ckv, kr

def mla_keys(ckv, w_uk, g_kn):
    return rmsnorm(jnp.einsum('bkl,lhd->bkhd', ckv, w_uk), g_kn)

def mla_attend(qn, qr, kn, kr, ckv, q_pos, k_pos):
    scale = (QK_NOPE_DIM + QK_ROPE_DIM) ** -0.5
    s = jnp.einsum('bqhd,bkhd->bhqk', qn, kn) + jnp.einsum('bqhr,bkr->bhqk', qr, kr)
    s = s.astype(jnp.float32) * scale
    visible = (k_pos[None, :] // CHUNK) <= (q_pos[:, None] // CHUNK)
    s = jnp.where(visible[None, None], s, jnp.finfo(jnp.float32).min)
    pr = jax.nn.softmax(s, axis=-1).astype(ckv.dtype)
    return jnp.einsum('bhqk,bkl->bqhl', pr, ckv)

def mla_out(o_lat, w_uv, w_o):
    B, T = o_lat.shape[:2]
    o = jnp.einsum('bqhl,lhd->bqhd', o_lat, w_uv).reshape(B, T, N_HEADS * V_HEAD_DIM)
    return o @ w_o

def mla_prompt_mixer(h, pos, p):
    qn, qr, ckv, kr = mla_project(h, pos, p)
    kn = mla_keys(ckv, p['w_uk'], p['g_kn'])
    B, T = h.shape[:2]
    nb = T // Q_BLOCK
    qn_b = qn.reshape(B, nb, Q_BLOCK, N_HEADS, QK_NOPE_DIM).swapaxes(0, 1)
    qr_b = qr.reshape(B, nb, Q_BLOCK, N_HEADS, QK_ROPE_DIM).swapaxes(0, 1)
    pos_b = pos.reshape(nb, Q_BLOCK)
    o = lax.map(lambda a: mla_attend(a[0], a[1], kn, kr, ckv, a[2], pos), (qn_b, qr_b, pos_b))
    o = o.swapaxes(0, 1).reshape(B, T, N_HEADS, KV_LORA_RANK)
    return mla_out(o, p['w_uv'], p['w_o']), ckv, kr

def mla_sample_mixer(h, pos, past_ckv, past_kpe, p):
    qn, qr, ckv_new, kr_new = mla_project(h, pos, p)
    ckv_all = jnp.concatenate([past_ckv, ckv_new], axis=1)
    kr_all = jnp.concatenate([past_kpe, kr_new], axis=1)
    kn = mla_keys(ckv_all, p['w_uk'], p['g_kn'])
    k_pos = jnp.arange(ckv_all.shape[1])
    o = mla_attend(qn, qr, kn, kr_all, ckv_all, pos, k_pos)
    return mla_out(o, p['w_uv'], p['w_o']), ckv_new, kr_new

def sgu_mix(u, v, w_s, b_s, idx):
    ii = jnp.arange(SGU_CHUNK)
    mask = (ii[None, :] // CHUNK) <= (ii[:, None] // CHUNK)
    w = jnp.where(mask[None], w_s, 0)
    w = w[:, idx[:, None], idx[None, :]]
    bias = b_s[:, idx].T[None, None, :, :, None]
    mixed = jnp.einsum('gij,bnjgc->bnigc', w, v) + bias
    return u * mixed

def chunk_mlp_mixer(h, idx, p):
    B, T, _ = h.shape
    Tc = idx.shape[0]
    n = T // Tc
    z = jax.nn.gelu(h @ p['w_in'])
    u, v = jnp.split(z, 2, axis=-1)
    v = rmsnorm(v, p['g_v'])
    shp = (B, n, Tc, SGU_GROUPS, SGU_GROUP_DIM)
    g = sgu_mix(u.reshape(shp), v.reshape(shp), p['w_s'], p['b_s'], idx).reshape(B, T, SGU_WIDTH)
    return g @ p['w_o'], v

def sq_relu_ffn(h, w1, w2):
    return jnp.square(jax.nn.relu(h @ w1)) @ w2

def setup_inputs(seed: int = 0) -> dict:
    key = jax.random.key(seed)
    ks = iter(jax.random.split(key, 48))

    def nrm(shape, scale):
        return jax.random.normal(next(ks), shape, jnp.float32) * scale

    def gain(shape):
        return 1.0 + nrm(shape, 0.05)

    NA, NB = N_ATT_LAYERS, N_MLP_LAYERS
    return {
        'x_prompt': nrm((BATCH, SEQ, D_MODEL), 1.0),
        'x_sample': nrm((DEC_BATCH, DEC_SEQ, D_MODEL), 1.0),
        'cache_ckv': nrm((NA, DEC_BATCH, PAST_LEN, KV_LORA_RANK), 1.0),
        'cache_kpe': nrm((NA, DEC_BATCH, PAST_LEN, QK_ROPE_DIM), 1.0),
        'c_prompt': nrm((BATCH, D_MODEL), 1.0),
        'c_sample': nrm((DEC_BATCH, D_MODEL), 1.0),
        'ada_w': nrm((DEPTH, D_MODEL, 6 * D_MODEL), 0.5 * D_MODEL ** -0.5),
        'ada_b': nrm((DEPTH, 6 * D_MODEL), 0.02),
        'norm1_g': gain((DEPTH, D_MODEL)),
        'norm2_g': gain((DEPTH, D_MODEL)),
        'ffn_w1': nrm((DEPTH, D_MODEL, D_FF), D_MODEL ** -0.5),
        'ffn_w2': nrm((DEPTH, D_FF, D_MODEL), D_FF ** -0.5),
        'mla_w_in': nrm((NA, D_MODEL, Q_LORA_RANK + KV_LORA_RANK + QK_ROPE_DIM), D_MODEL ** -0.5),
        'mla_g_qa': gain((NA, Q_LORA_RANK)),
        'mla_g_kva': gain((NA, KV_LORA_RANK)),
        'mla_w_q_up': nrm((NA, Q_LORA_RANK, N_HEADS * (QK_NOPE_DIM + QK_ROPE_DIM)), Q_LORA_RANK ** -0.5),
        'mla_w_uk': nrm((NA, KV_LORA_RANK, N_HEADS, QK_NOPE_DIM), KV_LORA_RANK ** -0.5),
        'mla_w_uv': nrm((NA, KV_LORA_RANK, N_HEADS, V_HEAD_DIM), KV_LORA_RANK ** -0.5),
        'mla_g_qn': gain((NA, QK_NOPE_DIM)),
        'mla_g_qr': gain((NA, QK_ROPE_DIM)),
        'mla_g_kn': gain((NA, QK_NOPE_DIM)),
        'mla_g_kr': gain((NA, QK_ROPE_DIM)),
        'mla_w_o': nrm((NA, N_HEADS * V_HEAD_DIM, D_MODEL), (N_HEADS * V_HEAD_DIM) ** -0.5),
        'cm_w_in': nrm((NB, D_MODEL, 2 * SGU_WIDTH), D_MODEL ** -0.5),
        'cm_g_v': gain((NB, SGU_WIDTH)),
        'cm_w_s': nrm((NB, SGU_GROUPS, SGU_CHUNK, SGU_CHUNK), SGU_CHUNK ** -0.5),
        'cm_b_s': gain((NB, SGU_GROUPS, SGU_CHUNK)),
        'cm_w_o': nrm((NB, SGU_WIDTH, D_MODEL), SGU_WIDTH ** -0.5),
    }

def reference(x_prompt, x_sample, cache_ckv, cache_kpe, c_prompt, c_sample,
              ada_w, ada_b, norm1_g, norm2_g, ffn_w1, ffn_w2,
              mla_w_in, mla_g_qa, mla_g_kva, mla_w_q_up, mla_w_uk, mla_w_uv,
              mla_g_qn, mla_g_qr, mla_g_kn, mla_g_kr, mla_w_o,
              cm_w_in, cm_g_v, cm_w_s, cm_b_s, cm_w_o):
    seq_p = x_prompt.shape[1]
    seq_s = x_sample.shape[1]
    past = cache_ckv.shape[2]
    pos_p = jnp.arange(seq_p)
    pos_s = past + jnp.arange(seq_s)
    idx_p = jnp.arange(SGU_CHUNK)
    idx_s = (past + jnp.arange(seq_s)) % SGU_CHUNK

    x_p, x_s = x_prompt, x_sample
    ckv_p_l, kpe_p_l, ckv_s_l, kpe_s_l, v_s_l = [], [], [], [], []
    for i in range(DEPTH):
        sh1_p, sc1_p, gt1_p, sh2_p, sc2_p, gt2_p = ada_modulation(c_prompt, ada_w[i], ada_b[i])
        sh1_s, sc1_s, gt1_s, sh2_s, sc2_s, gt2_s = ada_modulation(c_sample, ada_w[i], ada_b[i])
        h_p = modulated_norm(x_p, norm1_g[i], sh1_p, sc1_p)
        h_s = modulated_norm(x_s, norm1_g[i], sh1_s, sc1_s)
        if i % N_MIXERS == 0:
            a = i // N_MIXERS
            p = {'w_in': mla_w_in[a], 'g_qa': mla_g_qa[a], 'g_kva': mla_g_kva[a], 'w_q_up': mla_w_q_up[a],
                 'w_uk': mla_w_uk[a], 'w_uv': mla_w_uv[a], 'g_qn': mla_g_qn[a], 'g_qr': mla_g_qr[a],
                 'g_kn': mla_g_kn[a], 'g_kr': mla_g_kr[a], 'w_o': mla_w_o[a]}
            m_p, ckv_p, kpe_p = mla_prompt_mixer(h_p, pos_p, p)
            m_s, ckv_s, kpe_s = mla_sample_mixer(h_s, pos_s, cache_ckv[a], cache_kpe[a], p)
            ckv_p_l.append(ckv_p)
            kpe_p_l.append(kpe_p)
            ckv_s_l.append(ckv_s)
            kpe_s_l.append(kpe_s)
        else:
            b = i // N_MIXERS
            p = {'w_in': cm_w_in[b], 'g_v': cm_g_v[b], 'w_s': cm_w_s[b], 'b_s': cm_b_s[b], 'w_o': cm_w_o[b]}
            m_p, _ = chunk_mlp_mixer(h_p, idx_p, p)
            m_s, v_s = chunk_mlp_mixer(h_s, idx_s, p)
            v_s_l.append(v_s)
        x_p = x_p + gt1_p[:, None, :] * m_p
        x_s = x_s + gt1_s[:, None, :] * m_s
        f_p = sq_relu_ffn(modulated_norm(x_p, norm2_g[i], sh2_p, sc2_p), ffn_w1[i], ffn_w2[i])
        f_s = sq_relu_ffn(modulated_norm(x_s, norm2_g[i], sh2_s, sc2_s), ffn_w1[i], ffn_w2[i])
        x_p = x_p + gt2_p[:, None, :] * f_p
        x_s = x_s + gt2_s[:, None, :] * f_s

    return (x_p, x_s, jnp.stack(ckv_p_l), jnp.stack(kpe_p_l), jnp.stack(ckv_s_l), jnp.stack(kpe_s_l), jnp.stack(v_s_l))


_drawn_inputs = setup_inputs


def setup_inputs(seed=0):
    import zlib

    import numpy as np

    out = dict(_drawn_inputs(seed))
    spreads = {}
    factors = {'cache_ckv': 3.66,
     'cache_kpe': 6.95,
     'mla_g_qa': 8.0,
     'mla_g_qn': 8.0,
     'mla_g_qr': 8.0,
     'mla_g_kn': 8.0,
     'cm_b_s': 5.901}
    for name, (base, spread) in spreads.items():
        noise = np.random.default_rng([zlib.crc32(name.encode()), seed]).standard_normal(out[name].shape)
        drawn = base * np.exp(spread * noise) if base else spread * noise
        out[name] = __import__('jax').numpy.asarray(drawn.astype(out[name].dtype))
    for name, factor in factors.items():
        out[name] = (out[name] * factor).astype(out[name].dtype)
    return out
```

```python
from contextlib import ExitStack

import numpy as np
import concourse.bass as bass
from concourse import mybir

F32 = mybir.dt.float32
F32R = mybir.dt.float32r
BF16 = mybir.dt.bfloat16
ALU = mybir.AluOpType
ACT = mybir.ActivationFunctionType
AX = mybir.AxisListType

P = 128
D = 1024
KT = D // P
SEQ = 1024
NB = 8
TS = 16
TT = SEQ // P + 1
NTOK = TT * P
SAMPLE = TT - 1
H = 8
DN, DR = 128, 64
QL, KL = 384, 256
A_W = QL + KL + DR
PAST = 1024
FF = 4096
FT = FF // P
G = 8
EPS = 1e-6
SCALE = (DN + DR) ** -0.5
SHIFT1, SCALE1, GATE1, SHIFT2, SCALE2, GATE2 = range(6)


class Phase:

    semaphores = []

    def __init__(self, nc, name):
        self.nc, self.name, self.stack = nc, name, ExitStack()

    def __enter__(self):
        return self

    def __exit__(self, *a):
        self.stack.close()

    @classmethod
    def recycle_semaphores(cls, nc):
        nc.clear_and_free_semaphores(cls.semaphores)
        cls.semaphores = []
        nc.all_engine_barrier()

    def sb(self, name, shape, dt=F32):
        return self.stack.enter_context(self.nc.sbuf_tensor(f"{self.name}_{name}", list(shape), dt))

    def sem(self, name):
        sem = self.nc.alloc_semaphore(f"{self.name}_{name}")
        Phase.semaphores.append(sem)
        return sem

    def sems(self, name, n):
        return [self.sem(f"{name}{i}") for i in range(n)]


class Steps:

    def __init__(self, eng, sem):
        self.eng, self.sem, self.n, self.base = eng, sem, 0, 0

    def then(self, ins):
        self.n += 1
        ins.then_inc(self.sem, 1)

    def done(self):
        self.eng.wait_ge(self.sem, self.base + self.n)

    def run(self, ins):
        self.then(ins)
        self.done()


def mm3(pe, out, a_hi, a_lo, b_hi, b_lo, first, last):
    pe.matmul(out, a_hi, b_hi, start=first, stop=False)
    pe.matmul(out, a_hi, b_lo, start=False, stop=False)
    return pe.matmul(out, a_lo, b_hi, start=False, stop=last)


def f(ap):
    return ap.bitcast(F32)


def table_row(mod, layer, part, tile):
    base = mod[layer, 0, part * D:(part + 1) * D]
    if tile != SAMPLE:
        return [(0, P, base.partition_broadcast(P))]
    return [(b * TS, TS, mod[layer, 1 + b, part * D:(part + 1) * D].partition_broadcast(TS))
            for b in range(NB)]


TABLE_DMAS = {False: 1, True: NB}


def load_table(eng, dst, mod, layer, part, tile, sem):
    for p0, n, src in table_row(mod, layer, part, tile):
        eng.dma_start(dst[p0:p0 + n, :], src).then_inc(sem, 16)


def ada_phase(nc, psum, io, layer):
    RING = 3
    with Phase(nc, f"ada{layer}") as ph:
        c_cols = ph.sb("c_cols", [P, KT, 1 + NB])
        c_silu = ph.sb("c_silu", [P, KT, 32])
        w = ph.sb("w", [P, RING, 6 * D])
        bias = ph.sb("bias", [P, 3, 512])
        gain = ph.sb("gain", [P, 3, 512])
        mod = ph.sb("mod", [P, 3, 512])
        c_in = ph.sem("c_in")
        c_zero = ph.sem("c_zero")
        c_ready = ph.sem("c_ready")
        tab_zero = ph.sem("tab_zero")
        tab_in = ph.sem("tab_in")
        w_in = ph.sems("w_in", RING)
        w_used = ph.sem("w_used")
        dve_step = ph.sem("dve_step")
        mod_ready = ph.sem("mod_ready")
        mod_out = ph.sem("mod_out")

        scale_chunks = [(2 * part + half, g, half) for part, g in ((SCALE1, 0), (SCALE2, 1)) for half in range(2)]

        with nc.Block() as block:
            @block.sync
            def _(sp):
                sp.dma_start(c_cols[:], io["c_cols"]).then_inc(c_in, 16)
                for k in range(KT):
                    if k >= RING:
                        sp.wait_ge(w_used, k - RING + 1)
                    sp.dma_start(w[:, k % RING, :], io["ada_w"][layer, k]).then_inc(w_in[k % RING], 16)
                sp.wait_ge(mod_ready, 1)
                for j in range(4):
                    sp.dma_start(io["mod"][layer].rearrange("b (k j n) -> j b k n", j=4, n=512)[j],
                                 mod[32 * j:32 * j + 1 + NB, :, :]).then_inc(mod_out, 16)
                sp.wait_ge(mod_out, 64)

            @block.gpsimd
            def _(pool):
                pool.memset(bias[:], 0.0)
                pool.memset(gain[:], 1.0).then_inc(tab_zero, 1)
                pool.memset(c_silu[:], 0.0).then_inc(c_zero, 1)
                pool.wait_ge(tab_zero, 1)
                for j in range(4):
                    src = io["ada_b"][layer].rearrange("(k j n) -> j k n", j=4, n=512)[j]
                    pool.dma_start(bias[32 * j:32 * j + 1 + NB, :, :],
                                   src.partition_broadcast(1 + NB)).then_inc(tab_in, 16)
                for n, g, half in scale_chunks:
                    pool.dma_start(gain[32 * (n % 4):32 * (n % 4) + 1 + NB, n // 4, :],
                                   io["norm_g"][layer, g, half * 512:(half + 1) * 512].partition_broadcast(1 + NB)
                                   ).then_inc(tab_in, 16)

            @block.scalar
            def _(act):
                act.wait_ge(c_in, 16)
                act.wait_ge(c_zero, 1)
                act.activation(c_silu[:, :, 0:1 + NB], c_cols[:], ACT.Silu).then_inc(c_ready, 1)

            @block.tensor
            def _(pe):
                pe.wait_ge(c_ready, 1)
                for k in range(KT):
                    pe.wait_ge(w_in[k % RING], 16 * (k // RING + 1))
                    for bank in range(3):
                        for j in range(4):
                            n = 4 * bank + j
                            mm = pe.matmul(psum[32 * j:32 * j + 32, bank, :], c_silu[:, k, :],
                                           w[:, k % RING, n * 512:(n + 1) * 512],
                                           start=(k == 0), stop=(k == KT - 1), tile_position=(0, 32 * j))
                    mm.then_inc(w_used, 1)

            @block.vector
            def _(dve):
                step = Steps(dve, dve_step)
                dve.wait_ge(tab_in, 16 * (4 + len(scale_chunks)))
                for n, _, _ in scale_chunks:
                    q, bank = 32 * (n % 4), n // 4
                    step.then(dve.tensor_scalar(bias[q:q + 32, bank, :], bias[q:q + 32, bank, :], 1.0, None, ALU.add))
                step.done()
                dve.wait_ge(w_used, KT)
                step.run(dve.tensor_tensor(mod[:], psum[:, 0:3, :], bias[:], ALU.add))
                dve.tensor_tensor(mod[:], mod[:], gain[:], ALU.mult).then_inc(mod_ready, 1)


def latent_phase(nc, psum, io, ident, cqT, ckvT, krT):
    QT = QL // P
    WR = 6
    with Phase(nc, "lat") as ph:
        w_hi = ph.sb("w_hi", [P, KT, A_W], F32R)
        w_lo = ph.sb("w_lo", [P, KT, A_W], F32R)
        w_raw = ph.sb("w_raw", [P, WR, A_W])
        x = ph.sb("x", [P, 2, D])
        junk = ph.sb("junk", [P, D])
        junk3 = ph.sb("junk3", [P, A_W])
        xn = ph.sb("xn", [P, D])
        h = ph.sb("h", [P, 2, D])
        hT_hi = [ph.sb(f"hT_hi{i}", [P, KT, P], F32R) for i in range(2)]
        hT_lo = [ph.sb(f"hT_lo{i}", [P, KT, P], F32R) for i in range(2)]
        scale_t = ph.sb("scale_t", [P, D])
        shift_t = ph.sb("shift_t", [P, D])
        gains = ph.sb("gains", [P, A_W])
        cos = ph.sb("cos", [P, TT, DR])
        sin = ph.sb("sin", [P, TT, DR])
        inv_n = ph.sb("inv_n", [P, 3])
        eps3 = ph.sb("eps3", [P, 3])
        power = ph.sb("power", [P, 3])
        ss = ph.sb("ss", [P, 2])
        ms = ph.sb("ms", [P, 2])
        rstd = ph.sb("rstd", [P, 2])
        ss3 = ph.sb("ss3", [P, 2, 3])
        ms3 = ph.sb("ms3", [P, 2, 3])
        r3 = ph.sb("r3", [P, 2, 3])
        cq = ph.sb("cq", [P, 2, QL])
        ckv = ph.sb("ckv", [P, 2, KL])
        krn = ph.sb("krn", [P, DR])
        kr_cos = ph.sb("kr_cos", [P, DR])
        kr_sin = ph.sb("kr_sin", [P, DR])
        kr = ph.sb("kr", [P, 2, 2 * DR])

        raw_in = ph.sems("raw_in", WR)
        w_hi_ready, w_ready = ph.sem("w_hi_ready"), ph.sem("w_ready")
        x_in = ph.sems("x_in", 2)
        tab_in, stab_in, const_in = ph.sem("tab_in"), ph.sem("stab_in"), ph.sem("const_in")
        const_set = ph.sem("const_set")
        ss_ready, rstd_ready, h_ready = ph.sem("ss_ready"), ph.sem("rstd_ready"), ph.sem("h_ready")
        hT_raw, hT_hi_ready, hT_ready = ph.sem("hT_raw"), ph.sem("hT_hi_ready"), ph.sem("hT_ready")
        a_ready, ss3_ready, r3_ready = ph.sem("a_ready"), ph.sem("ss3_ready"), ph.sem("r3_ready")
        lat_ready, latT_raw = ph.sem("lat_ready"), ph.sem("latT_raw")
        latT_hi_ready, latT_ready = ph.sem("latT_hi_ready"), ph.sem("latT_ready")
        dve_step, pool_step = ph.sem("dve_step"), ph.sem("pool_step")
        stored = ph.sems("stored", 2)
        N_CONST = 5

        def a_bank(t):
            return 2 + 2 * (t % 2)

        with nc.Block() as block:
            @block.sync
            def _(sp):
                sp.dma_start(x[:, 0, :], io["x"][0]).then_inc(x_in[0], 16)
                load_table(sp, scale_t, io["mod"], 0, SCALE1, 0, tab_in)
                load_table(sp, shift_t, io["mod"], 0, SHIFT1, 0, tab_in)
                sp.dma_start(x[:, 1, :], io["x"][1]).then_inc(x_in[1], 16)
                for i, (dst, src) in enumerate((
                        (gains[:, 0:QL], io["g_qa"].partition_broadcast(P)),
                        (gains[:, QL:QL + KL], io["g_kva"].partition_broadcast(P)),
                        (gains[:, QL + KL:], io["g_kr"].partition_broadcast(P)),
                        (cos[:], io["cos"]), (sin[:], io["sin"]))):
                    sp.dma_start(dst, src).then_inc(const_in, 16)
                for k in range(KT):
                    if k >= WR:
                        sp.wait_ge(w_ready, k - WR + 1)
                    sp.dma_start(w_raw[:, k % WR, :], io["w_in"][k]).then_inc(raw_in[k % WR], 16)
                for t in range(2, TT + 3):
                    if t < TT:
                        sp.wait_ge(h_ready, t - 1)
                        sp.dma_start(x[:, t % 2, :], io["x"][t]).then_inc(x_in[t % 2], 16)
                    if t == SAMPLE:
                        sp.wait_ge(h_ready, SAMPLE)
                        load_table(sp, scale_t, io["mod"], 0, SCALE1, SAMPLE, stab_in)
                        load_table(sp, shift_t, io["mod"], 0, SHIFT1, SAMPLE, stab_in)
                    if t >= 3:
                        u = t - 3
                        sp.wait_ge(lat_ready, u + 1)
                        sp.dma_start(io["ckv_new"][u], ckv[:, u % 2, :]).then_inc(stored[u % 2], 16)
                        sp.dma_start(io["kpe_new"][u], kr[:, u % 2, 0:DR]).then_inc(stored[u % 2], 16)
                sp.wait_ge(stored[0], 32 * ((TT + 1) // 2))
                sp.wait_ge(stored[1], 32 * (TT // 2))

            @block.gpsimd
            def _(pool):
                step = Steps(pool, pool_step)
                pool.memset(inv_n[:, 0:1], 1.0 / QL)
                pool.memset(inv_n[:, 1:2], 1.0 / KL)
                pool.memset(inv_n[:, 2:3], 1.0 / DR)
                pool.memset(eps3[:], EPS)
                pool.memset(power[:], -0.5).then_inc(const_set, 1)
                pool.wait_ge(const_set, 1)

                def rms(t):
                    pool.wait_ge(ss_ready, t + 1)
                    c = slice(t % 2, t % 2 + 1)
                    step.run(pool.tensor_scalar(ms[:, c], ss[:, c], 1.0 / D, EPS, ALU.mult, ALU.add))
                    if t >= 2:
                        pool.wait_ge(h_ready, t - 1)
                    pool.tensor_tensor(rstd[:, c], ms[:, c], power[:, 0:1], ALU.pow).then_inc(rstd_ready, 1)

                def rms3(t):
                    pool.wait_ge(ss3_ready, t + 1)
                    step.run(pool.tensor_tensor(ms3[:, t % 2, :], ss3[:, t % 2, :], inv_n[:], ALU.mult))
                    step.run(pool.tensor_tensor(ms3[:, t % 2, :], ms3[:, t % 2, :], eps3[:], ALU.add))
                    if t >= 2:
                        pool.wait_ge(lat_ready, t - 1)
                    pool.tensor_tensor(r3[:, t % 2, :], ms3[:, t % 2, :], power[:], ALU.pow).then_inc(r3_ready, 1)

                for slot in range(-2, TT + 1):
                    if 0 <= slot - 1 < TT:
                        rms3(slot - 1)
                    if 0 <= slot + 2 < TT:
                        rms(slot + 2)

            @block.scalar
            def _(act):
                def squares(t):
                    act.wait_ge(x_in[t % 2], 16 * (t // 2 + 1))
                    if t >= 2:
                        act.wait_ge(rstd_ready, t - 1)
                    if t >= 1:
                        act.wait_ge(ss_ready, t)
                    act.activation(junk[:], x[:, t % 2, :], ACT.Square,
                                   accum_out=ss[:, t % 2:t % 2 + 1]).then_inc(ss_ready, 1)

                def w_split(k):
                    act.wait_ge(raw_in[k % WR], 16 * (k // WR + 1))
                    act.activation(w_hi[:, k, :], w_raw[:, k % WR, :], ACT.Copy).then_inc(w_hi_ready, 1)

                def hT_split(t):
                    for half in range(2):
                        act.wait_ge(hT_raw, 2 * t + half + 1)
                        if t >= 2:
                            act.wait_ge(a_ready, t - 1)
                        act.activation(hT_hi[t % 2][:, 4 * half:4 * half + 4, :],
                                       psum[:, half, :].rearrange("p (k n) -> p k n", k=4),
                                       ACT.Copy).then_inc(hT_hi_ready, 1)

                def post(t):
                    act.wait_ge(a_ready, t + 1)
                    if t >= 2:
                        act.wait_ge(r3_ready, t - 1)
                    if t >= 1:
                        act.wait_ge(ss3_ready, t)
                    b = a_bank(t)
                    for n, (c0, c1, src) in enumerate(((0, QL, psum[:, b, 0:QL]), (QL, QL + KL, psum[:, b + 1, 0:KL]),
                                                       (QL + KL, A_W, psum[:, b + 1, KL:KL + DR]))):
                        last = act.activation(junk3[:, c0:c1], src, ACT.Square, accum_out=ss3[:, t % 2, n:n + 1])
                    last.then_inc(ss3_ready, 1)

                def latT_split(t):
                    cols = slice(t * P, (t + 1) * P)
                    act.wait_ge(latT_raw, t + 1)
                    act.activation(cqT[0][:, :, cols], psum[:, 6, 0:QL].rearrange("p (k n) -> p k n", k=QT), ACT.Copy)
                    act.activation(ckvT[0][:, :, cols], psum[:, 7, 0:KL].rearrange("p (k n) -> p k n", k=2), ACT.Copy)
                    act.activation(krT[0][:, cols], psum[:, 7, KL:KL + P], ACT.Copy).then_inc(latT_hi_ready, 1)

                for slot in range(-2, TT + 2):
                    if 0 <= slot - 1 < TT:
                        post(slot - 1)
                    if 0 <= slot + 1 < TT:
                        hT_split(slot + 1)
                    if 0 <= slot + 2 < TT:
                        squares(slot + 2)
                    if slot == -2:
                        for k in range(KT):
                            w_split(k)
                    if 0 <= slot - 2 < TT:
                        latT_split(slot - 2)

            @block.vector
            def _(dve):
                step = Steps(dve, dve_step)

                def norm(t):
                    if t == 0:
                        dve.wait_ge(tab_in, 32)
                    if t == SAMPLE:
                        dve.wait_ge(stab_in, 32 * NB)
                    dve.wait_ge(rstd_ready, t + 1)
                    step.run(dve.scalar_tensor_tensor(xn[:], x[:, t % 2, :], rstd[:, t % 2:t % 2 + 1],
                                                      scale_t[:], ALU.mult, ALU.mult))
                    if t >= 2:
                        dve.wait_ge(hT_raw, 2 * t - 2)
                    dve.tensor_tensor(h[:, t % 2, :], xn[:], shift_t[:], ALU.add).then_inc(h_ready, 1)

                def w_split(k):
                    dve.wait_ge(w_hi_ready, k + 1)
                    dve.tensor_tensor(w_lo[:, k, :], w_raw[:, k % WR, :], f(w_hi[:, k, :]), ALU.subtract
                                      ).then_inc(w_ready, 1)

                def hT_split(t):
                    for half in range(2):
                        dve.wait_ge(hT_hi_ready, 2 * t + half + 1)
                        ks = slice(4 * half, 4 * half + 4)
                        dve.tensor_tensor(hT_lo[t % 2][:, ks, :], psum[:, half, :].rearrange("p (k n) -> p k n", k=4),
                                          f(hT_hi[t % 2][:, ks, :]), ALU.subtract).then_inc(hT_ready, 1)

                def post(t):
                    b, s = a_bank(t), t % 2
                    if t == 0:
                        dve.wait_ge(const_in, 16 * N_CONST)
                    dve.wait_ge(r3_ready, t + 1)
                    if t >= 2:
                        dve.wait_ge(latT_raw, t - 1)
                        dve.wait_ge(stored[s], 32 * (t // 2))
                    dve.scalar_tensor_tensor(cq[:, s, :], psum[:, b, 0:QL], r3[:, s, 0:1], gains[:, 0:QL],
                                             ALU.mult, ALU.mult)
                    dve.scalar_tensor_tensor(ckv[:, s, :], psum[:, b + 1, 0:KL], r3[:, s, 1:2],
                                             gains[:, QL:QL + KL], ALU.mult, ALU.mult)
                    step.run(dve.scalar_tensor_tensor(krn[:], psum[:, b + 1, KL:KL + DR], r3[:, s, 2:3],
                                                      gains[:, QL + KL:], ALU.mult, ALU.mult))
                    hr = DR // 2
                    step.then(dve.tensor_tensor(kr_cos[:], krn[:], cos[:, t, :], ALU.mult))
                    step.then(dve.tensor_tensor(kr_sin[:, 0:hr], krn[:, hr:], sin[:, t, 0:hr], ALU.mult))
                    step.run(dve.tensor_tensor(kr_sin[:, hr:], krn[:, 0:hr], sin[:, t, hr:], ALU.mult))
                    for i in range(2):
                        last = dve.tensor_tensor(kr[:, s, i * DR:(i + 1) * DR], kr_cos[:], kr_sin[:], ALU.add)
                    last.then_inc(lat_ready, 1)

                def latT_split(t):
                    cols = slice(t * P, (t + 1) * P)
                    dve.wait_ge(latT_hi_ready, t + 1)
                    dve.tensor_tensor(cqT[1][:, :, cols], psum[:, 6, 0:QL].rearrange("p (k n) -> p k n", k=QT),
                                      f(cqT[0][:, :, cols]), ALU.subtract)
                    dve.tensor_tensor(ckvT[1][:, :, cols], psum[:, 7, 0:KL].rearrange("p (k n) -> p k n", k=2),
                                      f(ckvT[0][:, :, cols]), ALU.subtract)
                    dve.tensor_tensor(krT[1][:, cols], psum[:, 7, KL:KL + P], f(krT[0][:, cols]),
                                      ALU.subtract).then_inc(latT_ready, 1)

                for slot in range(-2, TT + 2):
                    if 0 <= slot + 1 < TT:
                        hT_split(slot + 1)
                    if 0 <= slot - 1 < TT:
                        post(slot - 1)
                    if 0 <= slot + 2 < TT:
                        norm(slot + 2)
                    if slot == -2:
                        for k in range(KT):
                            w_split(k)
                    if 0 <= slot - 2 < TT:
                        latT_split(slot - 2)

            @block.tensor
            def _(pe):
                def transposes(t):
                    pe.wait_ge(h_ready, t + 1)
                    if t >= 1:
                        pe.wait_ge(hT_ready, 2 * t)
                    for k in range(KT):
                        mm = pe.transpose(psum[:, k // 4, (k % 4) * P:(k % 4 + 1) * P],
                                          h[:, t % 2, k * P:(k + 1) * P], ident[:])
                        if k % 4 == 3:
                            mm.then_inc(hT_raw, 1)

                def product(t):
                    pe.wait_ge(hT_ready, 2 * t + 2)
                    if t >= 2:
                        pe.wait_ge(lat_ready, t - 1)
                    for n, (c0, c1) in enumerate(((0, QL), (QL, A_W))):
                        for k in range(KT):
                            if t == 0 and n == 0:
                                pe.wait_ge(w_ready, k + 1)
                            mm = mm3(pe, psum[:, a_bank(t) + n, 0:c1 - c0],
                                     hT_hi[t % 2][:, k, :], hT_lo[t % 2][:, k, :],
                                     w_hi[:, k, c0:c1], w_lo[:, k, c0:c1], k == 0, k == KT - 1)
                    mm.then_inc(a_ready, 1)

                def latT(t):
                    pe.wait_ge(lat_ready, t + 1)
                    if t >= 1:
                        pe.wait_ge(latT_ready, t)
                    for k in range(QT):
                        pe.transpose(psum[:, 6, k * P:(k + 1) * P], cq[:, t % 2, k * P:(k + 1) * P], ident[:])
                    for k in range(2):
                        pe.transpose(psum[:, 7, k * P:(k + 1) * P], ckv[:, t % 2, k * P:(k + 1) * P], ident[:])
                    pe.transpose(psum[:, 7, 2 * P:3 * P], kr[:, t % 2, :], ident[:]).then_inc(latT_raw, 1)

                for slot in range(-1, TT + 1):
                    if 0 <= slot + 1 < TT:
                        transposes(slot + 1)
                    if 0 <= slot < TT:
                        product(slot)
                    if 0 <= slot - 1 < TT:
                        latT(slot - 1)


def project_phase(nc, psum, io, ident, layer, x_from, hT):
    N_TAB = 3
    with Phase(nc, f"proj{layer}") as ph:
        w_hi = ph.sb("w_hi", [P, KT, D], F32R)
        w_lo = ph.sb("w_lo", [P, KT, D], F32R)
        w_raw = ph.sb("w_raw", [P, 2, D])
        m = ph.sb("m", [P, 2, KT, P])
        m_hi = [ph.sb(f"m_hi{i}", [P, KT, P], F32R) for i in range(2)]
        m_lo = [ph.sb(f"m_lo{i}", [P, KT, P], F32R) for i in range(2)]
        gate_t, scale_t, shift_t = ph.sb("gate_t", [P, D]), ph.sb("scale_t", [P, D]), ph.sb("shift_t", [P, D])
        x = ph.sb("x", [P, 2, D])
        upd = ph.sb("upd", [P, D])
        xn = ph.sb("xn", [P, D])
        h = ph.sb("h", [P, 2, D])
        ss, ms, rstd = ph.sb("ss", [P, 2]), ph.sb("ms", [P, 2]), ph.sb("rstd", [P, 2])
        power = ph.sb("power", [P, 1])
        junk = psum[:, 6:8, :]

        raw_in, m_in, x_in = ph.sems("raw_in", 2), ph.sems("m_in", 2), ph.sems("x_in", 2)
        tab_in, stab_in = ph.sem("tab_in"), ph.sem("stab_in")
        w_hi_ready, w_ready = ph.sem("w_hi_ready"), ph.sem("w_ready")
        m_hi_ready, m_ready, o_ready = ph.sem("m_hi_ready"), ph.sem("m_ready"), ph.sem("o_ready")
        upd_ready, x_ready, x_stored = ph.sem("upd_ready"), ph.sem("x_ready"), ph.sems("x_stored", 2)
        ss_ready, rstd_ready, xn_ready = ph.sem("ss_ready"), ph.sem("rstd_ready"), ph.sem("xn_ready")
        h_ready, hT_raw = ph.sem("h_ready"), ph.sem("hT_raw")
        hT_hi_ready, hT_ready = ph.sem("hT_hi_ready"), ph.sem("hT_ready")
        const_set, pool_step = ph.sem("const_set"), ph.sem("pool_step")

        def o_bank(t):
            return 2 + 2 * (t % 2)

        with nc.Block() as block:
            @block.sync
            def _(sp):
                def load_m(t):
                    if t >= 2:
                        sp.wait_ge(m_ready, t - 1)
                    sp.dma_start(m[:, t % 2], io["mixT"].rearrange("k p n -> p k n")[:, :, t * P:(t + 1) * P]
                                 ).then_inc(m_in[t % 2], 16)

                def load_x(t):
                    if t >= 2:
                        sp.wait_ge(xn_ready, t - 1)
                        sp.wait_ge(x_stored[t % 2], 16 * (t // 2))
                    sp.dma_start(x[:, t % 2, :], x_from[t]).then_inc(x_in[t % 2], 16)

                def store_x(t):
                    sp.wait_ge(x_ready, t + 1)
                    sp.dma_start(io["x_res"][t], x[:, t % 2, :]).then_inc(x_stored[t % 2], 16)

                def load_w(k):
                    if k >= 2:
                        sp.wait_ge(w_ready, k - 1)
                    sp.dma_start(w_raw[:, k % 2, :], io[f"w_o{layer}"][k]).then_inc(raw_in[k % 2], 16)

                load_m(0)
                for k in range(KT):
                    load_w(k)
                    if k == 1:
                        load_m(1)
                        load_x(0)
                        load_x(1)
                        load_table(sp, gate_t, io["mod"], layer, GATE1, 0, tab_in)
                        load_table(sp, scale_t, io["mod"], layer, SCALE2, 0, tab_in)
                        load_table(sp, shift_t, io["mod"], layer, SHIFT2, 0, tab_in)
                for t in range(TT):
                    if t + 2 < TT:
                        load_m(t + 2)
                    if t == SAMPLE:
                        sp.wait_ge(h_ready, SAMPLE)
                        load_table(sp, gate_t, io["mod"], layer, GATE1, SAMPLE, stab_in)
                        load_table(sp, scale_t, io["mod"], layer, SCALE2, SAMPLE, stab_in)
                        load_table(sp, shift_t, io["mod"], layer, SHIFT2, SAMPLE, stab_in)
                    store_x(t)
                    if t + 2 < TT:
                        load_x(t + 2)
                sp.wait_ge(x_stored[0], 16 * ((TT + 1) // 2))
                sp.wait_ge(x_stored[1], 16 * (TT // 2))

            @block.scalar
            def _(act):
                def w_split(k):
                    act.wait_ge(raw_in[k % 2], 16 * (k // 2 + 1))
                    act.activation(w_hi[:, k, :], w_raw[:, k % 2, :], ACT.Copy).then_inc(w_hi_ready, 1)

                def m_split(t):
                    act.wait_ge(m_in[t % 2], 16 * (t // 2 + 1))
                    if t >= 2:
                        act.wait_ge(o_ready, t - 1)
                    act.activation(m_hi[t % 2][:], m[:, t % 2], ACT.Copy).then_inc(m_hi_ready, 1)

                def squares(t):
                    act.wait_ge(x_ready, t + 1)
                    if t >= 2:
                        act.wait_ge(rstd_ready, t - 1)
                    if t >= 1:
                        act.wait_ge(ss_ready, t)
                    act.activation(junk, x[:, t % 2, :].rearrange("p (a n) -> p a n", a=2), ACT.Square,
                                   accum_out=ss[:, t % 2:t % 2 + 1]).then_inc(ss_ready, 1)

                def hT_split(t):
                    for half in range(2):
                        act.wait_ge(hT_raw, 2 * t + half + 1)
                        act.activation(hT[0][:, 4 * half:4 * half + 4, t * P:(t + 1) * P],
                                       psum[:, half, :].rearrange("p (k n) -> p k n", k=4),
                                       ACT.Copy).then_inc(hT_hi_ready, 1)

                m_split(0)
                for k in range(KT):
                    w_split(k)
                for slot in range(TT + 2):
                    if slot + 1 < TT:
                        m_split(slot + 1)
                    if 0 <= slot - 1 < TT:
                        squares(slot - 1)
                    if 0 <= slot - 2 < TT:
                        hT_split(slot - 2)

            @block.gpsimd
            def _(pool):
                step = Steps(pool, pool_step)
                pool.memset(power[:], -0.5).then_inc(const_set, 1)
                pool.wait_ge(const_set, 1)
                for t in range(TT):
                    c = slice(t % 2, t % 2 + 1)
                    pool.wait_ge(x_in[t % 2], 16 * (t // 2 + 1))
                    pool.wait_ge(upd_ready, t + 1)
                    pool.tensor_tensor(x[:, t % 2, :], x[:, t % 2, :], upd[:], ALU.add).then_inc(x_ready, 1)
                    pool.wait_ge(ss_ready, t + 1)
                    step.run(pool.tensor_scalar(ms[:, c], ss[:, c], 1.0 / D, EPS, ALU.mult, ALU.add))
                    if t >= 2:
                        pool.wait_ge(xn_ready, t - 1)
                    pool.tensor_tensor(rstd[:, c], ms[:, c], power[:], ALU.pow).then_inc(rstd_ready, 1)

            @block.vector
            def _(dve):
                def w_split(k):
                    dve.wait_ge(w_hi_ready, k + 1)
                    dve.tensor_tensor(w_lo[:, k, :], w_raw[:, k % 2, :], f(w_hi[:, k, :]), ALU.subtract
                                      ).then_inc(w_ready, 1)

                def m_split(t):
                    dve.wait_ge(m_hi_ready, t + 1)
                    dve.tensor_tensor(m_lo[t % 2][:], m[:, t % 2], f(m_hi[t % 2][:]), ALU.subtract).then_inc(m_ready, 1)

                def update(t):
                    if t == 0:
                        dve.wait_ge(tab_in, 16 * N_TAB)
                    if t == SAMPLE:
                        dve.wait_ge(stab_in, 16 * N_TAB * NB)
                    dve.wait_ge(o_ready, t + 1)
                    if t >= 1:
                        dve.wait_ge(x_ready, t)
                    dve.tensor_tensor(upd[:].rearrange("p (a n) -> p a n", a=2), psum[:, o_bank(t):o_bank(t) + 2, :],
                                      gate_t[:].rearrange("p (a n) -> p a n", a=2), ALU.mult).then_inc(upd_ready, 1)

                def norm(t):
                    dve.wait_ge(rstd_ready, t + 1)
                    if t >= 1:
                        dve.wait_ge(h_ready, t)
                    dve.scalar_tensor_tensor(xn[:], x[:, t % 2, :], rstd[:, t % 2:t % 2 + 1], scale_t[:],
                                             ALU.mult, ALU.mult).then_inc(xn_ready, 1)
                    dve.wait_ge(xn_ready, t + 1)
                    if t >= 2:
                        dve.wait_ge(hT_raw, 2 * t - 2)
                    dve.tensor_tensor(h[:, t % 2, :], xn[:], shift_t[:], ALU.add).then_inc(h_ready, 1)

                def hT_split(t):
                    for half in range(2):
                        dve.wait_ge(hT_hi_ready, 2 * t + half + 1)
                        part = (slice(None), slice(4 * half, 4 * half + 4), slice(t * P, (t + 1) * P))
                        dve.tensor_tensor(hT[1][part], psum[:, half, :].rearrange("p (k n) -> p k n", k=4),
                                          f(hT[0][part]), ALU.subtract).then_inc(hT_ready, 1)

                m_split(0)
                for k in range(KT):
                    w_split(k)
                for slot in range(TT + 2):
                    if 0 <= slot - 1 < TT:
                        update(slot - 1)
                    if slot + 1 < TT:
                        m_split(slot + 1)
                    if 0 <= slot - 1 < TT:
                        norm(slot - 1)
                    if 0 <= slot - 2 < TT:
                        hT_split(slot - 2)

            @block.tensor
            def _(pe):
                def product(t):
                    pe.wait_ge(m_ready, t + 1)
                    if t >= 2:
                        pe.wait_ge(upd_ready, t - 1)
                    for half in range(2):
                        for k in range(KT):
                            if t == 0 and half == 0:
                                pe.wait_ge(w_ready, k + 1)
                            cols = slice(half * 512, half * 512 + 512)
                            mm = mm3(pe, psum[:, o_bank(t) + half, :], m_hi[t % 2][:, k, :], m_lo[t % 2][:, k, :],
                                     w_hi[:, k, cols], w_lo[:, k, cols], k == 0, k == KT - 1)
                    mm.then_inc(o_ready, 1)

                def transposes(t):
                    pe.wait_ge(h_ready, t + 1)
                    if t >= 1:
                        pe.wait_ge(hT_ready, 2 * t)
                    for k in range(KT):
                        mm = pe.transpose(psum[:, k // 4, (k % 4) * P:(k % 4 + 1) * P],
                                          h[:, t % 2, k * P:(k + 1) * P], ident[:])
                        if k % 4 == 3:
                            mm.then_inc(hT_raw, 1)

                for slot in range(TT + 2):
                    if 0 <= slot - 2 < TT:
                        transposes(slot - 2)
                    if slot < TT:
                        product(slot)


def ffn_phase(nc, psum, io, layer, hT, x_to):
    SF = 2
    SLABS = FT // SF
    GT = 3
    GN = NTOK // GT
    U = SF * GT
    V = 2 * TT
    H_BANKS, F_BANKS, UPDS = 2, 6, 3
    with Phase(nc, f"ffn{layer}") as ph:
        x = ph.sb("x", [P, TT, D])
        gate_t = ph.sb("gate_t", [P, 2, D])
        raw = ph.sb("raw", [P, 2 * SF, D])
        w1_hi = [ph.sb(f"w1_hi{i}", [P, KT, P], F32R) for i in range(SF)]
        w1_lo = [ph.sb(f"w1_lo{i}", [P, KT, P], F32R) for i in range(SF)]
        w2_hi = [ph.sb(f"w2_hi{i}", [P, D], F32R) for i in range(SF)]
        w2_lo = [ph.sb(f"w2_lo{i}", [P, D], F32R) for i in range(SF)]
        relu = ph.sb("relu", [P, 2, GN])
        sq = ph.sb("sq", [P, 2, GN])
        s_hi = ph.sb("s_hi", [P, SF, NTOK], F32R)
        s_lo = ph.sb("s_lo", [P, SF, NTOK], F32R)
        upd = ph.sb("upd", [P, UPDS, 512])

        raw_in = ph.sems("raw_in", 2 * SF)
        x_in, tab_in = ph.sem("x_in"), ph.sem("tab_in")
        w1_hi_ready, w1_ready = ph.sem("w1_hi_ready"), ph.sem("w1_ready")
        w2_hi_ready, w2_ready = ph.sem("w2_hi_ready"), ph.sem("w2_ready")
        hid_ready = ph.sem("hid_ready")
        relu_ready = ph.sem("relu_ready")
        sq_ready = ph.sem("sq_ready")
        s_hi_ready = ph.sem("s_hi_ready")
        s_ready = ph.sem("s_ready")
        f_ready = ph.sem("f_ready")
        upd_ready = ph.sem("upd_ready")
        added = ph.sem("added")
        stored = ph.sem("stored")

        with nc.Block() as block:
            @block.sync
            def _(sp):
                def load_w1(s, i):
                    sp.dma_start(raw[:, i, :].rearrange("p (k n) -> p k n", k=KT), io["w1"][layer, s * SF + i]
                                 ).then_inc(raw_in[i], 16)

                def load_w2(s, i):
                    sp.dma_start(raw[:, SF + i, :], io["w2"][layer, s * SF + i]).then_inc(raw_in[SF + i], 16)

                for i in range(SF):
                    load_w1(0, i)
                for i in range(SF):
                    load_w2(0, i)
                load_table(sp, gate_t[:, 0, :], io["mod"], layer, GATE2, 0, tab_in)
                load_table(sp, gate_t[:, 1, :], io["mod"], layer, GATE2, SAMPLE, tab_in)
                sp.dma_start(x[:], io["x_res"].rearrange("t p n -> p t n")).then_inc(x_in, 16)
                with sp.Fori(0, SLABS - 1) as s:
                    for i in range(SF):
                        sp.wait_ge(w1_ready, s * SF + (i + 1))
                        load_w1(s + 1, i)
                    for i in range(SF):
                        sp.wait_ge(w2_ready, s * SF + (i + 1))
                        load_w2(s + 1, i)
                for t in range(TT):
                    sp.wait_ge(added, V * SLABS + 2 * (t + 1))
                    sp.dma_start(x_to[t], x[:, t, :]).then_inc(stored, 16)
                sp.wait_ge(stored, 16 * TT)

            @block.scalar
            def _(act):
                def split_w1(s, i):
                    act.wait_ge(raw_in[i], s * 16 + 16)
                    act.activation(w1_hi[i][:], raw[:, i, :].rearrange("p (k n) -> p k n", k=KT),
                                   ACT.Copy).then_inc(w1_hi_ready, 1)

                def slab(s, last):
                    act.wait_ge(f_ready, s * V + 1)
                    for i in range(SF):
                        act.wait_ge(raw_in[SF + i], s * 16 + 16)
                        act.activation(w2_hi[i][:], raw[:, SF + i, :], ACT.Copy).then_inc(w2_hi_ready, 1)

                    def square_hi(u):
                        act.wait_ge(sq_ready, s * U + (2 + u + 1))
                        act.activation(s_hi[:, u // GT, (u % GT) * GN:(u % GT + 1) * GN], sq[:, u % 2, :],
                                       ACT.Copy).then_inc(s_hi_ready, 1)

                    for u in range(U):
                        act.wait_ge(hid_ready, s * U + (u + 1))
                        act.wait_ge(sq_ready, s * U + (u + 1))
                        act.activation(relu[:, u % 2, :], psum[:, u % H_BANKS, 0:GN], ACT.Relu
                                       ).then_inc(relu_ready, 1)
                        if u >= 1:
                            square_hi(u - 1)
                    square_hi(U - 1)
                    if not last:
                        for i in range(SF):
                            act.wait_ge(hid_ready, s * U + GT * (i + 1))
                            split_w1(s + 1, i)

                act.sem_inc(relu_ready, H_BANKS)
                for i in range(SF):
                    split_w1(0, i)
                with act.Fori(0, SLABS - 1) as s:
                    slab(s, False)
                slab(SLABS - 1, True)

            @block.vector
            def _(dve):
                def split_w1(s, i):
                    dve.wait_ge(w1_hi_ready, s * SF + (i + 1))
                    dve.tensor_tensor(w1_lo[i][:], raw[:, i, :].rearrange("p (k n) -> p k n", k=KT),
                                      f(w1_hi[i][:]), ALU.subtract).then_inc(w1_ready, 1)

                def slab(s, last):
                    for i in range(SF):
                        dve.wait_ge(w2_hi_ready, s * SF + (i + 1))
                        dve.tensor_tensor(w2_lo[i][:], raw[:, SF + i, :], f(w2_hi[i][:]), ALU.subtract
                                          ).then_inc(w2_ready, 1)

                    def square_lo(u):
                        dve.wait_ge(s_hi_ready, s * U + (u + 1))
                        part = (slice(None), u // GT, slice((u % GT) * GN, (u % GT + 1) * GN))
                        dve.tensor_tensor(s_lo[part], sq[:, u % 2, :], f(s_hi[part]), ALU.subtract
                                          ).then_inc(s_ready, 1)

                    for u in range(U):
                        dve.wait_ge(relu_ready, s * U + (H_BANKS + u + 1))
                        dve.wait_ge(s_ready, s * U + (u + 1))
                        dve.tensor_tensor(sq[:, u % 2, :], relu[:, u % 2, :], relu[:, u % 2, :], ALU.mult
                                          ).then_inc(sq_ready, 1)
                        if u >= 1:
                            square_lo(u - 1)
                    square_lo(U - 1)
                    for v in range(V):
                        t, half = v // 2, v % 2
                        dve.wait_ge(f_ready, s * V + (1 + v + 1))
                        dve.wait_ge(added, s * V + (V + v + 1 - UPDS))
                        dve.tensor_tensor(upd[:, v % UPDS, :], psum[:, H_BANKS + v % F_BANKS, :],
                                          gate_t[:, int(t == SAMPLE), half * 512:half * 512 + 512], ALU.mult
                                          ).then_inc(upd_ready, 1)
                        if not last and v in (2, 5):
                            split_w1(s + 1, (v - 2) // 3)

                dve.sem_inc(sq_ready, 2)
                dve.sem_inc(s_ready, 2)
                dve.sem_inc(upd_ready, F_BANKS)
                for i in range(SF):
                    split_w1(0, i)
                dve.wait_ge(tab_in, 16 * (1 + NB))
                with dve.Fori(0, SLABS - 1) as s:
                    slab(s, False)
                slab(SLABS - 1, True)

            @block.gpsimd
            def _(pool):
                pool.sem_inc(added, V)
                pool.wait_ge(x_in, 16)
                with pool.Fori(0, SLABS) as s:
                    for v in range(V):
                        part = x[:, v // 2, (v % 2) * 512:(v % 2) * 512 + 512]
                        pool.wait_ge(upd_ready, s * V + (F_BANKS + v + 1))
                        pool.wait_ge(added, s * V + (v + 1))
                        pool.tensor_tensor(part, part, upd[:, v % UPDS, :], ALU.add).then_inc(added, 1)

            @block.tensor
            def _(pe):
                def slab(s):
                    for u in range(U):
                        i, g = u // GT, u % GT
                        pe.wait_ge(w1_ready, s * SF + (i + 1))
                        pe.wait_ge(relu_ready, s * U + (u + 1))
                        for k in range(KT):
                            mm = mm3(pe, psum[:, u % H_BANKS, 0:GN], w1_hi[i][:, k, :], w1_lo[i][:, k, :],
                                     hT[0][:, k, g * GN:(g + 1) * GN], hT[1][:, k, g * GN:(g + 1) * GN],
                                     k == 0, k == KT - 1)
                        mm.then_inc(hid_ready, 1)
                    for v in range(V):
                        t, half = v // 2, v % 2
                        pe.wait_ge(s_ready, s * U + (2 + U - GT + t // GT + 1))
                        pe.wait_ge(w2_ready, s * SF + SF)
                        pe.wait_ge(upd_ready, s * V + (v + 1))
                        for i in range(SF):
                            toks, cols = slice(t * P, (t + 1) * P), slice(half * 512, half * 512 + 512)
                            mm = mm3(pe, psum[:, H_BANKS + v % F_BANKS, :], s_hi[:, i, toks], s_lo[:, i, toks],
                                     w2_hi[i][:, cols], w2_lo[i][:, cols], i == 0, i == SF - 1)
                        mm.then_inc(f_ready, 1)

                pe.sem_inc(f_ready, 1)
                with pe.Fori(0, SLABS) as s:
                    slab(s)


def prompt_attention_phase(nc, psum, io, ident, cqT, ckvT, krT):
    PAIRS = H // 2
    QT = QL // P
    T = SEQ // P
    GR = T // 2
    N = 2 * 2 * GR
    GN = 2 * GR
    QW = 2 * (DN + DR)

    def unit(n):
        return n // (2 * GR), n // 2 % GR, n % 2

    def key_tiles(n):
        return 2 * unit(n)[1] + 2

    chunks = [[(k, min(k + 4, key_tiles(n))) for k in range(0, key_tiles(n), 4)] for n in range(N)]
    before = [sum(len(c) for c in chunks[:n]) for n in range(N + 1)]
    C = before[N]
    assert C % 2 == 0

    with Phase(nc, "patt") as ph:
        q_raw, kv_raw = ph.sb("q_raw", [P, QT, QW]), ph.sb("kv_raw", [P, 2, 512])
        wq_hi, wq_lo = ph.sb("wq_hi", [P, QT, QW], F32R), ph.sb("wq_lo", [P, QT, QW], F32R)
        wkv_hi, wkv_lo = ph.sb("wkv_hi", [P, 2, 512], F32R), ph.sb("wkv_lo", [P, 2, 512], F32R)
        g_qn, g_qr, g_kn = ph.sb("g_qn", [P, DN]), ph.sb("g_qr", [P, DR]), ph.sb("g_kn", [P, DN])
        cos, sin = ph.sb("cos", [P, TT, DR]), ph.sb("sin", [P, TT, DR])
        ident_bf, mask = ph.sb("ident_bf", [P, P], BF16), ph.sb("mask", [P, 2, 2 * P], BF16)
        junk = ph.sb("junk", [P, QW + 2 * DN])
        inv_n, eps, power = ph.sb("inv_n", [P, 6]), ph.sb("eps", [P, 6]), ph.sb("power", [P, 6])
        ss, ms, rs = ph.sb("ss", [P, 2, 6]), ph.sb("ms", [P, 2, 6]), ph.sb("rs", [P, 2, 6])
        q_tok = ph.sb("q_tok", [P, 2, 4, P])
        k_tok = ph.sb("k_tok", [P, 2, 2, DN])
        qr, qr_cos, qr_sin = ph.sb("qr", [P, 2, DR]), ph.sb("qr_cos", [P, 2, DR]), ph.sb("qr_sin", [P, 2, DR])
        qT_hi = ph.sb("qT_hi", [P, 4, SEQ], F32R)
        qT_lo = ph.sb("qT_lo", [P, 2, SEQ], F32R)
        kT_hi, kT_lo = ph.sb("kT_hi", [P, 2, SEQ], F32R), ph.sb("kT_lo", [P, 2, SEQ], F32R)
        v_hi, v_lo = ph.sb("v_hi", [P, T, 2 * DN], F32R), ph.sb("v_lo", [P, T, 2 * DN], F32R)
        mx, neg, total, inv = (ph.sb(n, [P, 2]) for n in ("mx", "neg", "total", "inv"))
        pr = ph.sb("pr", [P, 2, SEQ])
        pT_hi = [ph.sb(f"pT_hi{i}", [P, T, 2 * P], F32R) for i in range(2)]
        pT_lo = [ph.sb(f"pT_lo{i}", [P, T, 2 * P], F32R) for i in range(2)]
        o = ph.sb("o", [P, 2, 2 * P])

        const_in, const_set = ph.sem("const_in"), ph.sem("const_set")
        raw_in = ph.sem("raw_in")
        w_hi_ready, w_ready = ph.sem("w_hi_ready"), ph.sem("w_ready")
        proj_ready = ph.sem("proj_ready")
        ss_ready = ph.sem("ss_ready")
        r_ready = ph.sem("r_ready")
        v_hi_ready = ph.sem("v_hi_ready")
        tok_ready = ph.sem("tok_ready")
        tokT_raw = ph.sem("tokT_raw")
        tokT_hi_ready = ph.sem("tokT_hi_ready")
        tokT_ready = ph.sem("tokT_ready")
        s_ready = ph.sem("s_ready")
        max_ready = ph.sem("max_ready")
        exp_ready = ph.sem("exp_ready")
        pr_ready = ph.sem("pr_ready")
        pT_raw = ph.sem("pT_raw")
        pT_hi_ready = ph.sem("pT_hi_ready")
        pT_ready = ph.sem("pT_ready")
        pv_ready = ph.sem("pv_ready")
        o_ready = ph.sem("o_ready")
        stored = ph.sems("stored", 2)
        dve_step, pool_step = ph.sem("dve_step"), ph.sem("pool_step")

        def flat(bank, width):
            return psum[:, bank:bank + 2, :].rearrange("p a n -> p (a n)")[:, 0:width]

        with nc.Block() as block:
            @block.sync
            def _(sp):
                for i in range(2):
                    sp.sem_inc(stored[i], 16)
                for dst, src in ((g_qn, "g_qn"), (g_qr, "g_qr"), (g_kn, "g_kn")):
                    sp.dma_start(dst[:], io[src].partition_broadcast(P)).then_inc(const_in, 16)
                for dst, src in ((cos, "cos"), (sin, "sin"), (ident_bf, "ident_bf"), (mask, "mask")):
                    sp.dma_start(dst[:], io[src]).then_inc(const_in, 16)
                with sp.Fori(0, PAIRS) as p:
                    for g in range(GN):
                        j, grp = g // GR, g % GR
                        sp.wait_ge(o_ready, p * GN + (2 + g + 1))
                        sp.dma_start(io["mixT"][p * 2 + j, :, 2 * P * grp:2 * P * (grp + 1)], o[:, g % 2, :]
                                     ).then_inc(stored[g % 2], 16)
                for i in range(2):
                    sp.wait_ge(stored[i], 16 + 16 * PAIRS * GN // 2)

            @block.gpsimd
            def _(pool):
                def load(p):
                    pool.dma_start(q_raw[:], io["w_q_pair"][p]).then_inc(raw_in, 16)
                    pool.dma_start(kv_raw[:], io["w_kv_pair"][p]).then_inc(raw_in, 16)

                def pair(p, step):
                    for t in range(T):
                        s = t % 2
                        pool.wait_ge(ss_ready, p * T + (1 + t + 1))
                        step.run(pool.tensor_tensor(ms[:, s, :], ss[:, s, :], inv_n[:], ALU.mult))
                        step.run(pool.tensor_tensor(ms[:, s, :], ms[:, s, :], eps[:], ALU.add))
                        pool.wait_ge(tok_ready, p * T + (t + 2))
                        pool.tensor_tensor(rs[:, s, :], ms[:, s, :], power[:], ALU.pow).then_inc(r_ready, 1)

                load(0)
                pool.sem_inc(r_ready, 2)
                pool.memset(inv_n[:, 0:2], 1.0 / DN)
                pool.memset(inv_n[:, 2:4], 1.0 / DR)
                pool.memset(inv_n[:, 4:6], 1.0 / DN)
                pool.memset(eps[:], EPS)
                pool.memset(power[:], -0.5).then_inc(const_set, 1)
                pool.wait_ge(const_set, 1)
                step = Steps(pool, pool_step)
                with pool.Fori(0, PAIRS - 1) as p:
                    step.n, step.base = 0, p * (2 * T)
                    pair(p, step)
                    pool.wait_ge(w_ready, p * 2 + 2)
                    load(p + 1)
                step.n, step.base = 0, (PAIRS - 1) * 2 * T
                pair(PAIRS - 1, step)

            @block.scalar
            def _(act):
                def tile(p, t):
                    b, s = 2 * (t % 3), t % 2
                    act.wait_ge(proj_ready, p * T + (1 + t + 1))
                    act.wait_ge(r_ready, p * T + (t + 1))
                    act.wait_ge(ss_ready, p * T + (t + 1))
                    q, kv = psum[:, b, :], psum[:, b + 1, :]
                    HW = DN + DR
                    act.activation(v_hi[:, t, :], kv[:, 2 * DN:], ACT.Copy).then_inc(v_hi_ready, 1)
                    for n, (src, c) in enumerate((
                            (q[:, 0:DN], 0), (q[:, HW:HW + DN], HW), (q[:, DN:HW], DN), (q[:, HW + DN:2 * HW], HW + DN),
                            (kv[:, 0:DN], QW), (kv[:, DN:2 * DN], QW + DN))):
                        last = act.activation(junk[:, c:c + src.shape[1]], src, ACT.Square, accum_out=ss[:, s, n:n + 1])
                    last.then_inc(ss_ready, 1)

                def tileT(p, t):
                    b, toks = 6, slice(t * P, (t + 1) * P)
                    act.wait_ge(tokT_raw, p * T + (2 + t + 1))
                    act.activation(qT_hi[:, :, toks], psum[:, b, :].rearrange("p (k n) -> p k n", k=4), ACT.Copy)
                    act.activation(kT_hi[:, :, toks], psum[:, b + 1, 0:2 * P].rearrange("p (k n) -> p k n", k=2),
                                   ACT.Copy).then_inc(tokT_hi_ready, 1)

                def exps(p, n):
                    s, width = n % 2, key_tiles(n) * P
                    act.wait_ge(max_ready, p * N + (n + 1))
                    act.wait_ge(pT_raw, p * C + (1 + before[max(n - 1, 0)]))
                    act.activation(pr[:, s, 0:width], flat(2 * s, width), ACT.Exp, bias=neg[:, s:s + 1], scale=SCALE,
                                   accum_out=total[:, s:s + 1]).then_inc(exp_ready, 1)

                def probsT(p, n):
                    g, i = n // 2, n % 2
                    for c, (k0, k1) in enumerate(chunks[n]):
                        m = before[n] + c
                        act.wait_ge(pT_raw, p * C + (1 + m + 1))
                        act.wait_ge(pv_ready, p * GN + (g + 1))
                        act.activation(pT_hi[g % 2][:, k0:k1, i * P:(i + 1) * P],
                                       psum[:, 4 + m % 2, 0:(k1 - k0) * P].rearrange("p (k n) -> p k n", n=P),
                                       ACT.Copy).then_inc(pT_hi_ready, 1)

                def out(p, g):
                    act.wait_ge(pv_ready, p * GN + (2 + g + 1))
                    act.wait_ge(stored[g % 2], p * (16 * GN // 2) + 16 * (g // 2 + 1))
                    act.activation(o[:, g % 2, :], psum[:, 6 + g % 2, 0:2 * P], ACT.Copy).then_inc(o_ready, 1)

                act.sem_inc(ss_ready, 1)
                act.sem_inc(exp_ready, 2)
                act.sem_inc(o_ready, 2)
                with act.Fori(0, PAIRS) as p:
                    act.wait_ge(raw_in, p * 32 + 32)
                    act.wait_ge(proj_ready, p * T + 1)
                    act.activation(wq_hi[:], q_raw[:], ACT.Copy).then_inc(w_hi_ready, 1)
                    act.activation(wkv_hi[:], kv_raw[:], ACT.Copy).then_inc(w_hi_ready, 1)
                    for t in range(T + 2):
                        if t < T:
                            tile(p, t)
                        if t >= 2:
                            tileT(p, t - 2)
                    for n in range(N + 1):
                        if n < N:
                            exps(p, n)
                        if n >= 1:
                            probsT(p, n - 1)
                        if n >= 4 and n % 2 == 0:
                            out(p, n // 2 - 2)
                    out(p, GN - 1)

            @block.vector
            def _(dve):
                def tile(p, t, step):
                    b, s, HW, hr = 2 * (t % 3), t % 2, DN + DR, DR // 2
                    dve.wait_ge(r_ready, p * T + (2 + t + 1))
                    dve.wait_ge(tokT_raw, p * T + (t + 1))
                    for j in range(2):
                        q, k = psum[:, b, j * HW:(j + 1) * HW], psum[:, b + 1, j * DN:(j + 1) * DN]
                        dve.scalar_tensor_tensor(qr[:, j, :], q[:, DN:], rs[:, s, 2 + j:3 + j], g_qr[:],
                                                 ALU.mult, ALU.mult)
                        dve.scalar_tensor_tensor(q_tok[:, s, j, :], q[:, 0:DN], rs[:, s, j:j + 1], g_qn[:],
                                                 ALU.mult, ALU.mult)
                        last = dve.scalar_tensor_tensor(k_tok[:, s, j, :], k, rs[:, s, 4 + j:5 + j], g_kn[:],
                                                        ALU.mult, ALU.mult)
                    step.run(last)
                    cos_t = cos[:, t, :].unsqueeze(1).to_broadcast([P, 2, DR])
                    sin_t = sin[:, t, :].unsqueeze(1).to_broadcast([P, 2, DR])
                    dve.tensor_tensor(qr_cos[:], qr[:], cos_t, ALU.mult)
                    dve.tensor_tensor(qr_sin[:, :, 0:hr], qr[:, :, hr:], sin_t[:, :, 0:hr], ALU.mult)
                    step.run(dve.tensor_tensor(qr_sin[:, :, hr:], qr[:, :, 0:hr], sin_t[:, :, hr:], ALU.mult))
                    for i in range(2):
                        dve.tensor_tensor(q_tok[:, s, 2:4, i * DR:(i + 1) * DR], qr_cos[:], qr_sin[:], ALU.add)
                    dve.wait_ge(v_hi_ready, p * T + (t + 1))
                    dve.tensor_tensor(v_lo[:, t, :], psum[:, b + 1, 2 * DN:], f(v_hi[:, t, :]), ALU.subtract
                                      ).then_inc(tok_ready, 1)

                def tileT(p, t):
                    b, toks = 6, slice(t * P, (t + 1) * P)
                    dve.wait_ge(tokT_hi_ready, p * T + (t + 1))
                    q = psum[:, b, :].rearrange("p (k n) -> p k n", k=4)
                    dve.tensor_tensor(qT_lo[:, :, toks], q[:, 0:2, :], f(qT_hi[:, 0:2, toks]), ALU.subtract)
                    dve.tensor_tensor(qT_hi[DR:, 2:4, toks], q[DR:, 2:4, :], f(qT_hi[DR:, 2:4, toks]), ALU.subtract)
                    dve.tensor_tensor(kT_lo[:, :, toks], psum[:, b + 1, 0:2 * P].rearrange("p (k n) -> p k n", k=2),
                                      f(kT_hi[:, :, toks]), ALU.subtract).then_inc(tokT_ready, 1)

                def maxes(p, n, step):
                    s, width = n % 2, key_tiles(n) * P
                    dve.wait_ge(s_ready, p * N + (n + 1))
                    dve.wait_ge(exp_ready, p * N + (n + 1))
                    step.run(dve.reduce_max(mx[:, s:s + 1], flat(2 * s, width), AX.X))
                    dve.tensor_scalar(neg[:, s:s + 1], mx[:, s:s + 1], -SCALE, None, ALU.mult).then_inc(max_ready, 1)

                def normalise(p, n, step):
                    s, width = n % 2, key_tiles(n) * P
                    dve.wait_ge(exp_ready, p * N + (2 + n + 1))
                    step.run(dve.reciprocal(inv[:, s:s + 1], total[:, s:s + 1]))
                    dve.tensor_scalar(pr[:, s, 0:width], pr[:, s, 0:width], inv[:, s:s + 1], None, ALU.mult
                                      ).then_inc(pr_ready, 1)

                def probsT(p, n):
                    g, i = n // 2, n % 2
                    for c, (k0, k1) in enumerate(chunks[n]):
                        m = before[n] + c
                        part = (slice(None), slice(k0, k1), slice(i * P, (i + 1) * P))
                        dve.wait_ge(pT_hi_ready, p * C + (m + 1))
                        dve.tensor_tensor(pT_lo[g % 2][part],
                                          psum[:, 4 + m % 2, 0:(k1 - k0) * P].rearrange("p (k n) -> p k n", n=P),
                                          f(pT_hi[g % 2][part]), ALU.subtract).then_inc(pT_ready, 1)

                dve.sem_inc(tok_ready, 3)
                dve.sem_inc(tokT_ready, 2)
                dve.sem_inc(pT_ready, 2)
                dve.wait_ge(const_in, 16 * 7)
                step = Steps(dve, dve_step)
                with dve.Fori(0, PAIRS) as p:
                    step.n, step.base = 0, p * (2 * T + 2 * N)
                    dve.wait_ge(w_hi_ready, p * 2 + 1)
                    dve.tensor_tensor(wq_lo[:], q_raw[:], f(wq_hi[:]), ALU.subtract).then_inc(w_ready, 1)
                    dve.wait_ge(w_hi_ready, p * 2 + 2)
                    dve.tensor_tensor(wkv_lo[:], kv_raw[:], f(wkv_hi[:]), ALU.subtract).then_inc(w_ready, 1)
                    for t in range(T + 2):
                        if t >= 2:
                            tileT(p, t - 2)
                        if t < T:
                            tile(p, t, step)
                    for n in range(N + 1):
                        if n < N:
                            maxes(p, n, step)
                            normalise(p, n, step)
                        if n >= 1:
                            probsT(p, n - 1)
                    assert step.n == 2 * T + 2 * N

            @block.tensor
            def _(pe):
                def proj(p, t):
                    b, toks = 2 * (t % 3), slice(t * P, (t + 1) * P)
                    pe.wait_ge(tok_ready, p * T + (t + 1))
                    if t == 0:
                        pe.wait_ge(w_ready, p * 2 + 1)
                    for k in range(QT):
                        mm3(pe, psum[:, b, 0:QW], cqT[0][:, k, toks], cqT[1][:, k, toks],
                            wq_hi[:, k, :], wq_lo[:, k, :], k == 0, k == QT - 1)
                    if t == 0:
                        pe.wait_ge(w_ready, p * 2 + 2)
                    for k in range(2):
                        mm = mm3(pe, psum[:, b + 1, :], ckvT[0][:, k, toks], ckvT[1][:, k, toks],
                                 wkv_hi[:, k, :], wkv_lo[:, k, :], k == 0, k == 1)
                    mm.then_inc(proj_ready, 1)

                def tokT(p, t):
                    b, s = 6, t % 2
                    pe.wait_ge(tok_ready, p * T + (3 + t + 1))
                    pe.wait_ge(tokT_ready, p * T + (t + 2))
                    if t == 0:
                        pe.wait_ge(o_ready, p * GN + 2)
                    for k in range(4):
                        pe.transpose(psum[:, b, k * P:(k + 1) * P], q_tok[:, s, k, :], ident[:])
                    for k in range(2):
                        mm = pe.transpose(psum[:, b + 1, k * P:(k + 1) * P], k_tok[:, s, k, :], ident[:])
                    mm.then_inc(tokT_raw, 1)

                def scores(p, n):
                    j, g, i = unit(n)
                    width, toks = key_tiles(n) * P, slice((2 * g + i) * P, (2 * g + i + 1) * P)
                    pe.wait_ge(exp_ready, p * N + (n + 1))
                    for c in range(0, width, 512):
                        keys = slice(c, min(c + 512, width))
                        bank = 2 * (n % 2) + c // 512
                        out = psum[:, bank, 0:keys.stop - c]
                        mm3(pe, out, qT_hi[:, j, toks], qT_lo[:, j, toks], kT_hi[:, j, keys], kT_lo[:, j, keys],
                            True, False)
                        if keys.stop == width:
                            m0 = width - 2 * P - c
                            pe.matmul(psum[:, bank, m0:m0 + 2 * P], ident_bf[:], mask[:, i, :], start=False, stop=False)
                        pe.matmul(out, qT_hi[:, 2 + j, toks], krT[0][:, keys], start=False, stop=False)
                        mm = pe.matmul(out, qT_hi[:, 2 + j, toks], krT[1][:, keys], start=False, stop=True)
                    mm.then_inc(s_ready, 1)

                def probsT(p, n):
                    pe.wait_ge(pr_ready, p * N + (n + 1))
                    for c, (k0, k1) in enumerate(chunks[n]):
                        m = before[n] + c
                        pe.wait_ge(pT_ready, p * C + (m + 1))
                        for k in range(k0, k1):
                            mm = pe.transpose(psum[:, 4 + m % 2, (k - k0) * P:(k - k0 + 1) * P],
                                              pr[:, n % 2, k * P:(k + 1) * P], ident[:])
                        mm.then_inc(pT_raw, 1)

                def values(p, g):
                    j, s = g // GR, g % 2
                    pe.wait_ge(pT_ready, p * C + (2 + before[2 * g + 2]))
                    pe.wait_ge(o_ready, p * GN + (g + 1))
                    tiles = key_tiles(2 * g)
                    for k in range(tiles):
                        mm = mm3(pe, psum[:, 6 + s, 0:2 * P], v_hi[:, k, j * DN:(j + 1) * DN],
                                 v_lo[:, k, j * DN:(j + 1) * DN], pT_hi[s][:, k, :], pT_lo[s][:, k, :],
                                 k == 0, k == tiles - 1)
                    mm.then_inc(pv_ready, 1)

                pe.sem_inc(proj_ready, 1)
                pe.sem_inc(tokT_raw, 2)
                pe.sem_inc(pT_raw, 1)
                pe.sem_inc(pv_ready, 2)
                pe.wait_ge(const_in, 16 * 7)
                with pe.Fori(0, PAIRS) as p:
                    for t in range(T + 1):
                        if t < T:
                            proj(p, t)
                        if t >= 2:
                            tokT(p, t - 2)
                    scores(p, 0)
                    tokT(p, T - 1)
                    for n in range(N):
                        if n == 1:
                            pe.wait_ge(tokT_ready, p * T + (2 + T))
                        if n + 1 < N:
                            scores(p, n + 1)
                        probsT(p, n)
                        if n >= 2 and n % 2 == 0:
                            values(p, n // 2 - 1)
                    values(p, GN - 1)


def sample_query_phase(nc, psum, io, ident, cqT, ckvT, krT, wuk, qe, qrT, s_new):
    QT, HW, hr = QL // P, DN + DR, DR // 2
    toks = slice(SAMPLE * P, NTOK)
    with Phase(nc, "sq") as ph:
        wq_raw = ph.sb("wq_raw", [P, QT, H * HW])
        wq_hi, wq_lo = ph.sb("wq_hi", [P, QT, H * HW], F32R), ph.sb("wq_lo", [P, QT, H * HW], F32R)
        wuk_raw = ph.sb("wuk_raw", [P, 2, D])
        wukT = ph.sb("wukT", [P, H, KL])
        g_qn, g_kn, g_qr = ph.sb("g_qn", [P, DN]), ph.sb("g_kn", [P, DN]), ph.sb("g_qr", [P, DR])
        gg = ph.sb("gg", [P, DN])
        cos, sin = ph.sb("cos", [P, DR]), ph.sb("sin", [P, DR])
        sq = ph.sb("sq", [P, 4, 2 * HW])
        inv_n, eps, power = ph.sb("inv_n", [P, 3 * H]), ph.sb("eps", [P, 3 * H]), ph.sb("power", [P, 3 * H])
        ss, ms, rs = ph.sb("ss", [P, 3, H]), ph.sb("ms", [P, 3, H]), ph.sb("rs", [P, 3, H])
        qn = ph.sb("qn", [P, H, DN])
        qr, qr_cos, qr_sin = ph.sb("qr", [P, H, DR]), ph.sb("qr_cos", [P, H, DR]), ph.sb("qr_sin", [P, H, DR])
        qnT = ph.sb("qnT", [P, H, P])
        qe_f = ph.sb("qe_f", [P, 2, NB, H, TS])
        kr_f, ckv_f = ph.sb("kr_f", [P, P]), ph.sb("ckv_f", [P, 2, P])
        rn_wide, rn_keys = ph.sb("rn_wide", [P, H, TS]), ph.sb("rn_keys", [P, P])
        s_nope = ph.sb("s_nope", [P, P])

        wq_in, wuk_in, wukT_in, const_in = ph.sem("wq_in"), ph.sem("wuk_in"), ph.sem("wukT_in"), ph.sem("const_in")
        const_set = ph.sem("const_set")
        w_hi, w_ready = ph.sem("w_hi"), ph.sem("w_ready")
        q_ready, sq_ready, ss_ready, r_ready = ph.sem("q_ready"), ph.sem("sq_ready"), ph.sem("ss_ready"), ph.sem("r_ready")
        qtok_ready, qT_raw, qT_ready = ph.sem("qtok_ready"), ph.sem("qT_raw"), ph.sem("qT_ready")
        qe_raw, qe_f_ready, qe_ready = ph.sem("qe_raw"), ph.sem("qe_f_ready"), ph.sem("qe_ready")
        k_ready, ksq_ready, kss_ready, kr_ready = ph.sem("k_ready"), ph.sem("ksq_ready"), ph.sem("kss_ready"), ph.sem("kr_ready")
        lat_f_ready, wide_ready, s_raw, done = ph.sem("lat_f_ready"), ph.sem("wide_ready"), ph.sem("s_raw"), ph.sem("done")
        dve_step, pool_step = ph.sem("dve_step"), ph.sem("pool_step")

        with nc.Block() as block:
            @block.sync
            def _(sp):
                sp.dma_start(wq_raw[:], io["w_q"]).then_inc(wq_in, 16)
                sp.dma_start(wuk_raw[:], io["w_uk"]).then_inc(wuk_in, 16)
                sp.dma_start(wukT[:], io["w_ukT"]).then_inc(wukT_in, 16)
                for dst, src in ((g_qn, "g_qn"), (g_kn, "g_kn"), (g_qr, "g_qr")):
                    sp.dma_start(dst[:], io[src].partition_broadcast(P)).then_inc(const_in, 16)
                for dst, src in ((cos, "cos"), (sin, "sin")):
                    sp.dma_start(dst[:], io[src][:, SAMPLE, :]).then_inc(const_in, 16)

            @block.gpsimd
            def _(pool):
                step = Steps(pool, pool_step)
                pool.memset(inv_n[:, 0:H], 1.0 / DN)
                pool.memset(inv_n[:, H:2 * H], 1.0 / DR)
                pool.memset(inv_n[:, 2 * H:], 1.0 / DN)
                pool.memset(eps[:], EPS)
                pool.memset(power[:], -0.5).then_inc(const_set, 1)
                pool.wait_ge(const_set, 1)
                pool.memset(qrT[DR:, :, :], 0.0).then_inc(const_set, 1)
                pool.wait_ge(const_set, 2)

                def rms(parts, signal):
                    a, b = parts.start * H, parts.stop * H
                    flat = [t[:].rearrange("p a h -> p (a h)")[:, a:b] for t in (ss, ms, rs)]
                    step.run(pool.tensor_tensor(flat[1], flat[0], inv_n[:, a:b], ALU.mult))
                    step.run(pool.tensor_tensor(flat[1], flat[1], eps[:, a:b], ALU.add))
                    pool.tensor_tensor(flat[2], flat[1], power[:, a:b], ALU.pow).then_inc(signal, 1)

                pool.wait_ge(ss_ready, 1)
                rms(slice(0, 2), r_ready)
                pool.wait_ge(kss_ready, 1)
                rms(slice(2, 3), kr_ready)

            @block.scalar
            def _(act):
                act.wait_ge(wq_in, 16)
                act.activation(wq_hi[:], wq_raw[:], ACT.Copy).then_inc(w_hi, 1)
                act.wait_ge(wuk_in, 16)
                act.activation(wuk[0][:], wuk_raw[:], ACT.Copy).then_inc(w_hi, 1)
                act.wait_ge(q_ready, 1)
                act.activation(sq[:], psum[:, 0:4, 0:2 * HW], ACT.Square).then_inc(sq_ready, 1)
                act.wait_ge(k_ready, 1)
                act.wait_ge(ss_ready, 1)
                act.activation(sq[:, 0:2, :], psum[:, 4:6, 0:384], ACT.Square)
                act.activation(sq[:, 2, 0:256], psum[:, 6, 0:256], ACT.Square).then_inc(ksq_ready, 1)
                act.wait_ge(qT_raw, 1)
                act.activation(qnT[:], psum[:, 4:6, :].rearrange("p a (h n) -> p (a h) n", n=P), ACT.Copy)
                act.activation(qrT[0:DR, :, :].rearrange("p b (h t) -> p b h t", t=TS),
                               psum[0:DR, 6:8, :].rearrange("p a (h b t) -> p b (a h) t", b=NB, t=TS),
                               ACT.Copy).then_inc(qT_ready, 1)
                act.wait_ge(qe_raw, 1)
                for k in range(2):
                    last = act.activation(qe_f[:, k], psum[:, 2 * k:2 * k + 2, :].rearrange(
                        "p a (h b t) -> p b (a h) t", b=NB, t=TS), ACT.Copy)
                last.then_inc(qe_f_ready, 1)
                act.wait_ge(qe_f_ready, 1)
                act.activation(qe[0][:], qe_f[:].rearrange("p k b h t -> p k b (h t)"), ACT.Copy).then_inc(qe_ready, 1)

            @block.vector
            def _(dve):
                step = Steps(dve, dve_step)
                dve.wait_ge(w_hi, 1)
                dve.tensor_tensor(wq_lo[:], wq_raw[:], f(wq_hi[:]), ALU.subtract).then_inc(w_ready, 1)
                dve.wait_ge(w_hi, 2)
                dve.tensor_tensor(wuk[1][:], wuk_raw[:], f(wuk[0][:]), ALU.subtract).then_inc(w_ready, 1)
                dve.tensor_tensor(ckv_f[:], f(ckvT[0][:, :, toks]), f(ckvT[1][:, :, toks]), ALU.add)
                dve.tensor_tensor(kr_f[:], f(krT[0][:, toks]), f(krT[1][:, toks]), ALU.add).then_inc(lat_f_ready, 1)
                dve.wait_ge(const_in, 16 * 5)
                step.then(dve.tensor_tensor(gg[:], g_qn[:], g_kn[:], ALU.mult))
                dve.wait_ge(sq_ready, 1)
                heads = sq[:].rearrange("p a (j x) -> p a j x", j=2)
                dve.reduce_sum(ss[:, 0, :].rearrange("p (a j) -> p a j", j=2), heads[:, :, :, 0:DN], AX.X)
                dve.reduce_sum(ss[:, 1, :].rearrange("p (a j) -> p a j", j=2), heads[:, :, :, DN:], AX.X
                               ).then_inc(ss_ready, 1)
                dve.wait_ge(r_ready, 1)
                q = psum[:, 0:4, 0:2 * HW].rearrange("p a (j x) -> p a j x", j=2)

                def per_head(t, width):
                    return t.rearrange("p (a j) -> p a j", j=2).unsqueeze(3).to_broadcast([P, 4, 2, width])

                dve.tensor_tensor(qn[:].rearrange("p (a j) x -> p a j x", j=2), q[:, :, :, 0:DN],
                                  per_head(rs[:, 0, :], DN), ALU.mult)
                step.run(dve.tensor_tensor(qr[:].rearrange("p (a j) x -> p a j x", j=2), q[:, :, :, DN:],
                                           per_head(rs[:, 1, :], DR), ALU.mult))
                step.then(dve.tensor_tensor(qn[:], qn[:], gg[:].unsqueeze(1).to_broadcast([P, H, DN]), ALU.mult))
                step.run(dve.tensor_tensor(qr[:], qr[:], g_qr[:].unsqueeze(1).to_broadcast([P, H, DR]), ALU.mult))
                cos_h = cos[:].unsqueeze(1).to_broadcast([P, H, DR])
                sin_h = sin[:].unsqueeze(1).to_broadcast([P, H, DR])
                dve.tensor_tensor(qr_cos[:], qr[:], cos_h, ALU.mult)
                dve.tensor_tensor(qr_sin[:, :, 0:hr], qr[:, :, hr:], sin_h[:, :, 0:hr], ALU.mult)
                step.run(dve.tensor_tensor(qr_sin[:, :, hr:], qr[:, :, 0:hr], sin_h[:, :, hr:], ALU.mult))
                dve.tensor_tensor(qr[:], qr_cos[:], qr_sin[:], ALU.add).then_inc(qtok_ready, 1)
                dve.wait_ge(ksq_ready, 1)
                dve.reduce_sum(ss[:, 2, :], sq[:].rearrange("p a n -> p (a n)")[:, 0:D].rearrange(
                    "p (h x) -> p h x", x=DN), AX.X).then_inc(kss_ready, 1)
                dve.wait_ge(kr_ready, 1)
                dve.tensor_copy(rn_wide[:], rs[:, 2, :].unsqueeze(2).to_broadcast([P, H, TS])).then_inc(wide_ready, 1)
                dve.wait_ge(qe_ready, 1)
                dve.tensor_tensor(qe[1][:], qe_f[:].rearrange("p k b h t -> p k b (h t)"), f(qe[0][:]), ALU.subtract)
                dve.wait_ge(s_raw, 1)
                step.run(dve.tensor_copy(rn_keys[:], psum[:, 4, 0:P]))
                step.run(dve.tensor_tensor(s_nope[:], psum[:, 5, 0:P], rn_keys[:], ALU.mult))
                dve.tensor_tensor(s_new[:], psum[:, 6, 0:P], s_nope[:], ALU.add).then_inc(done, 1)

            @block.tensor
            def _(pe):
                pe.wait_ge(w_ready, 1)
                for c in range(4):
                    cols = slice(c * 2 * HW, (c + 1) * 2 * HW)
                    for k in range(QT):
                        mm = mm3(pe, psum[:, c, 0:2 * HW], cqT[0][:, k, toks], cqT[1][:, k, toks],
                                 wq_hi[:, k, cols], wq_lo[:, k, cols], k == 0, k == QT - 1)
                mm.then_inc(q_ready, 1)
                pe.wait_ge(w_ready, 2)
                for c, (c0, c1) in enumerate(((0, 384), (384, 768), (768, D))):
                    for k in range(2):
                        mm = mm3(pe, psum[:, 4 + c, 0:c1 - c0], ckvT[0][:, k, toks], ckvT[1][:, k, toks],
                                 wuk[0][:, k, c0:c1], wuk[1][:, k, c0:c1], k == 0, k == 1)
                mm.then_inc(k_ready, 1)
                pe.wait_ge(qtok_ready, 1)
                pe.wait_ge(ksq_ready, 1)
                for h in range(H):
                    pe.transpose(psum[:, 4 + h // 4, (h % 4) * P:(h % 4 + 1) * P], qn[:, h, :], ident[:])
                    mm = pe.transpose(psum[0:DR, 6 + h // 4, (h % 4) * P:(h % 4 + 1) * P], qr[:, h, :], ident[:])
                mm.then_inc(qT_raw, 1)
                pe.wait_ge(qT_ready, 1)
                pe.wait_ge(wukT_in, 16)
                for k in range(2):
                    for h in range(H):
                        mm = pe.matmul(psum[:, 2 * k + h // 4, (h % 4) * P:(h % 4 + 1) * P],
                                       wukT[:, h, k * P:(k + 1) * P], qnT[:, h, :], start=True, stop=True)
                mm.then_inc(qe_raw, 1)
                pe.wait_ge(wide_ready, 1)
                pe.matmul(psum[:, 4, 0:P], rn_wide[:].rearrange("p h t -> p (h t)"), ident[:], start=True, stop=True)
                pe.wait_ge(qe_f_ready, 1)
                pe.wait_ge(lat_f_ready, 1)
                for b in range(NB):
                    own = slice(b * TS, (b + 1) * TS)
                    for k in range(2):
                        pe.matmul(psum[:, 5, own], qe_f[:, k, b].rearrange("p h t -> p (h t)"), ckv_f[:, k, own],
                                  start=(k == 0), stop=(k == 1))
                    mm = pe.matmul(psum[:, 6, own], qrT[:, b, :], kr_f[:, own], start=True, stop=True)
                mm.then_inc(s_raw, 1)


def sample_attention_phase(nc, psum, io, ident, wuk, qe, qrT, s_new):
    T = PAST // P
    CW = 384
    LAST = D - 2 * CW
    KEYS = PAST + TS
    PT, SB = 7, 6
    with Phase(nc, "satt") as ph:
        lT_raw = ph.sb("lT_raw", [P, 2, PAST])
        lT_hi, lT_lo = ph.sb("lT_hi", [P, 2, PAST], F32R), ph.sb("lT_lo", [P, 2, PAST], F32R)
        kpeT = ph.sb("kpeT", [P, PAST])
        l_raw = ph.sb("l_raw", [P, T, KL])
        l_hi, l_lo = ph.sb("l_hi", [P, T, KL], F32R), ph.sb("l_lo", [P, T, KL], F32R)
        l_new = ph.sb("l_new", [P, NB, KL])
        wc_hi, wc_lo = ph.sb("wc_hi", [P, 2, CW], F32R), ph.sb("wc_lo", [P, 2, CW], F32R)
        sq = ph.sb("sq", [P, 2, D])
        ss, ms, rn = ph.sb("ss", [P, 2, H]), ph.sb("ms", [P, 2, H]), ph.sb("rn", [P, 2, H])
        power, inv_n, eps = ph.sb("power", [P, H]), ph.sb("inv_n", [P, H]), ph.sb("eps", [P, H])
        st_nope = ph.sb("st_nope", [P, H, TS])
        st = ph.sb("st", [P, 2, P])
        s = ph.sb("s", [P, KEYS])
        pr = ph.sb("pr", [P, (T + 1) * P])
        mx, neg, total, inv = (ph.sb(n, [P, 1]) for n in ("mx", "neg", "total", "inv"))
        pT_hi, pT_lo = ph.sb("pT_hi", [P, T, P], F32R), ph.sb("pT_lo", [P, T, P], F32R)
        pT_new = ph.sb("pT_new", [P, P])
        o = ph.sb("o", [P, KL])
        oT = ph.sb("oT", [P, 2, H, NB, TS])
        wuv = ph.sb("wuv", [P, 2, H * DN])
        out = ph.sb("out", [P, H, P])

        const_in, const_set, wc_set = ph.sem("const_in"), ph.sem("const_set"), ph.sem("wc_set")
        l_new_in = ph.sem("l_new_in")
        lT_in, kpe_in, l_in = ph.sems("lT_in", 4), ph.sems("kpe_in", 4), ph.sems("l_in", 4)
        lT_hi_ready, lT_ready = ph.sem("lT_hi_ready"), ph.sem("lT_ready")
        wc_ready = ph.sem("wc_ready")
        k_ready = ph.sem("k_ready")
        sq_ready = ph.sem("sq_ready")
        ss_ready = ph.sem("ss_ready")
        rn_ready = ph.sem("rn_ready")
        st_ready = ph.sem("st_ready")
        sb_raw = ph.sem("sb_raw")
        s_ready = ph.sem("s_ready")
        max_ready = ph.sem("max_ready")
        exp_ready = ph.sem("exp_ready")
        inv_ready = ph.sem("inv_ready")
        l_hi_ready, l_ready = ph.sem("l_hi_ready"), ph.sem("l_ready")
        pT_raw = ph.sem("pT_raw")
        pT_hi_ready, pT_ready = ph.sem("pT_hi_ready"), ph.sem("pT_ready")
        pv_ready = ph.sem("pv_ready")
        o_ready, oT_raw = ph.sem("o_ready"), ph.sem("oT_raw")
        oT_ready = ph.sem("oT_ready")
        out_raw, out_ready, stored = ph.sem("out_raw"), ph.sem("out_ready"), ph.sem("stored")
        dve_step, pool_step = ph.sem("dve_step"), ph.sem("pool_step")

        def quarter(q):
            return slice(q * PAST // 4, (q + 1) * PAST // 4)

        def banks(t):
            return 3 * (t % 2)

        def streams(eng, body, tail):
            body(0, False, True)
            with eng.Fori(1, NB - 1) as b:
                body(b, True, True)
            body(NB - 1, True, False)
            tail(NB - 1)

        with nc.Block() as block:
            @block.sync
            def _(sp):
                def load_lT(b, q):
                    sp.dma_start(lT_raw[:, :, quarter(q)], io["cacheT"][b, :, :, quarter(q)]).then_inc(lT_in[q], 16)

                def load_kpe(b, q):
                    sp.dma_start(kpeT[0:DR, quarter(q)], io["kpeT"][b, :, quarter(q)]).then_inc(kpe_in[q], 16)

                for q in range(4):
                    load_lT(0, q)
                    load_kpe(0, q)
                sp.dma_start(wuv[:], io["w_uv"]).then_inc(const_in, 16)
                with sp.Fori(0, NB - 1) as b:
                    for q in range(4):
                        sp.wait_ge(lT_ready, b * T + (2 * q + 2))
                        load_lT(b + 1, q)
                        sp.wait_ge(k_ready, b * T + (8 + 2 * q + 2))
                        load_kpe(b + 1, q)
                sp.wait_ge(out_ready, 2)
                sp.dma_start(io["mixT"].rearrange("k p n -> p k n")[:, :, SEQ:], out[:]).then_inc(stored, 16)
                sp.wait_ge(stored, 16)

            @block.gpsimd
            def _(pool):
                def load_l(b, q):
                    pool.dma_start(l_raw[:, 2 * q:2 * q + 2, :], io["cache"][b, :, 2 * q:2 * q + 2, :]
                                   ).then_inc(l_in[q], 16)

                def rms(b, t, step):
                    c = t % 2
                    pool.wait_ge(ss_ready, b * T + (2 + t + 1))
                    step.run(pool.tensor_tensor(ms[:, c, :], ss[:, c, :], inv_n[:], ALU.mult))
                    step.run(pool.tensor_tensor(ms[:, c, :], ms[:, c, :], eps[:], ALU.add))
                    pool.wait_ge(st_ready, b * T + (t + 1))
                    pool.tensor_tensor(rn[:, c, :], ms[:, c, :], power[:], ALU.pow).then_inc(rn_ready, 1)

                def tail(b, q):
                    pool.wait_ge(l_hi_ready, b * 4 + (q + 1))
                    part = (slice(None), slice(2 * q, 2 * q + 2))
                    pool.tensor_tensor(l_lo[part], l_raw[part], f(l_hi[part]), ALU.subtract).then_inc(l_ready, 1)

                def body(b, prev, nxt):
                    step = Steps(pool, pool_step)
                    step.base = b * (2 * T)
                    for t in range(T):
                        if prev and t < 4:
                            tail(b - 1, t)
                            pool.wait_ge(l_ready, b * 4 + (t + 1 - 4))
                            load_l(b, t)
                        rms(b, t, step)

                pool.memset(l_new[:], 0.0)
                pool.memset(pr[:, KEYS:], 0.0)
                pool.memset(inv_n[:], 1.0 / DN)
                pool.memset(eps[:], EPS)
                pool.memset(power[:], -0.5).then_inc(const_set, 1)
                pool.wait_ge(const_set, 1)
                pool.memset(kpeT[DR:, :], 0.0).then_inc(const_set, 1)
                pool.wait_ge(const_set, 2)
                for q in range(4):
                    load_l(0, q)
                pool.dma_start(l_new[0:TS, :, :], io["ckv_new"][SAMPLE].rearrange("(b t) l -> t b l", t=TS)
                               ).then_inc(l_new_in, 16)
                streams(pool, body, lambda b: [tail(b, q) for q in range(4)])

            @block.scalar
            def _(act):
                def lT_split(b, t):
                    if t % 2 == 0:
                        act.wait_ge(lT_in[t // 2], b * 16 + 16)
                    act.wait_ge(k_ready, b * T + (t + 1))
                    keys = slice(t * P, (t + 1) * P)
                    act.activation(lT_hi[:, :, keys], lT_raw[:, :, keys], ACT.Copy).then_inc(lT_hi_ready, 1)

                def squares(b, t):
                    act.wait_ge(k_ready, b * T + (8 + t + 1))
                    act.wait_ge(ss_ready, b * T + (t + 1))
                    k, c = banks(t), t % 2
                    act.activation(sq[:, c, 2 * CW:], psum[:, k + 2, 0:LAST], ACT.Square)
                    act.activation(sq[:, c, 0:2 * CW].rearrange("p (a n) -> p a n", a=2), psum[:, k:k + 2, 0:CW],
                                   ACT.Square).then_inc(sq_ready, 1)

                def evict_scores(b, half):
                    act.wait_ge(sb_raw, b * T + (2 + 4 * half + 4))
                    act.wait_ge(exp_ready, b + 1)
                    act.activation(s[:, half * 512:half * 512 + 512], psum[:, SB, :], ACT.Copy).then_inc(s_ready, 1)

                def before(b, slot):
                    if slot < 4:
                        part = (slice(None), slice(2 * slot, 2 * slot + 2))
                        act.wait_ge(l_in[slot], b * 16 + 16)
                        act.wait_ge(pv_ready, b + 1)
                        act.activation(l_hi[part], l_raw[part], ACT.Copy).then_inc(l_hi_ready, 1)
                    if slot == 2:
                        act.wait_ge(max_ready, b + 1)
                        act.wait_ge(pT_raw, b * 3 + 1)
                        act.activation(pr[:, 0:KEYS], s[:], ACT.Exp, bias=neg[:], scale=SCALE,
                                       accum_out=total[:]).then_inc(exp_ready, 1)
                    if slot in (3, 4):
                        c = slot - 3
                        act.wait_ge(pT_raw, b * 3 + (1 + c + 1))
                        act.activation(pT_hi[:, 4 * c:4 * c + 4, :], psum[:, PT, :].rearrange("p (k n) -> p k n", n=P),
                                       ACT.Copy).then_inc(pT_hi_ready, 1)
                    if slot == 5:
                        act.wait_ge(pT_raw, b * 3 + 4)
                        act.activation(pT_new[:], psum[:, PT, 0:P], ACT.Copy).then_inc(pT_hi_ready, 1)
                    if slot == 7:
                        act.wait_ge(pv_ready, b + 2)
                        act.wait_ge(inv_ready, b + 1)
                        act.activation(o[:], psum[:, PT, 0:KL], ACT.Copy, scale=inv[:]).then_inc(o_ready, 1)

                def after(b, slot):
                    if slot == 1:
                        evict_scores(b, 1)
                    if slot == 7:
                        act.wait_ge(oT_raw, b + 1)
                        for k in range(2):
                            last = act.activation(oT[:, k, :, b, :], psum[:, PT, k * P:(k + 1) * P].rearrange(
                                "p (h t) -> p h t", t=TS), ACT.Copy)
                        last.then_inc(oT_ready, 1)

                def body(b, prev, nxt):
                    for t in range(T):
                        if t + 2 < T:
                            lT_split(b, t + 2)
                        elif nxt:
                            lT_split(b + 1, t + 2 - T)
                        if prev:
                            before(b - 1, t)
                        squares(b, t)
                        if prev:
                            after(b - 1, t)
                        if t == 5:
                            evict_scores(b, 0)

                def tail(b):
                    for slot in range(T):
                        before(b, slot)
                        after(b, slot)

                act.sem_inc(s_ready, 1)
                act.sem_inc(exp_ready, 1)
                act.sem_inc(oT_ready, 1)
                act.activation(wc_hi[:, :, 0:LAST], f(wuk[0][:, :, 2 * CW:]), ACT.Copy).then_inc(wc_set, 1)
                lT_split(0, 0)
                lT_split(0, 1)
                act.wait_ge(const_set, 2)
                streams(act, body, tail)
                act.wait_ge(out_raw, 1)
                for half in range(2):
                    act.activation(out[:, 4 * half:4 * half + 4, :], psum[:, half, :].rearrange("p (h n) -> p h n", n=P),
                                   ACT.Copy).then_inc(out_ready, 1)

            @block.vector
            def _(dve):
                def lT_split(b, t):
                    keys = slice(t * P, (t + 1) * P)
                    dve.wait_ge(lT_hi_ready, b * T + (t + 1))
                    dve.tensor_tensor(lT_lo[:, :, keys], lT_raw[:, :, keys], f(lT_hi[:, :, keys]), ALU.subtract
                                      ).then_inc(lT_ready, 1)

                def place_queries(b):
                    dve.wait_ge(k_ready, b * T + 8)
                    dve.tensor_copy(wc_hi[:, :, LAST:], f(qe[0][:, :, b, :]))
                    dve.tensor_copy(wc_lo[:, :, LAST:], f(qe[1][:, :, b, :])).then_inc(wc_ready, 1)

                def sums(b, t):
                    dve.wait_ge(sq_ready, b * T + (t + 1))
                    dve.reduce_sum(ss[:, t % 2, :], sq[:, t % 2, :].rearrange("p (h x) -> p h x", x=DN), AX.X
                                   ).then_inc(ss_ready, 1)

                def scores(b, t, step):
                    bank = psum[:, banks(t) + 2, :]
                    dve.wait_ge(rn_ready, b * T + (t + 1))
                    step.run(dve.tensor_tensor(st_nope[:], bank[:, LAST:CW].rearrange("p (h t) -> p h t", t=TS),
                                               rn[:, t % 2, :].unsqueeze(2).to_broadcast([P, H, TS]), ALU.mult))
                    dve.wait_ge(sb_raw, b * T + (t + 1))
                    dve.tensor_tensor(st[:, t % 2, :], bank[:, CW:CW + P], st_nope[:].rearrange("p h t -> p (h t)"),
                                      ALU.add).then_inc(st_ready, 1)

                def tail(b, slot, step):
                    if slot == 2:
                        dve.wait_ge(s_ready, b * 2 + 3)
                        step.run(dve.tensor_copy(s[:, PAST:], s_new[:, bass.ts(b, TS)]))
                        step.run(dve.reduce_max(mx[:], s[:], AX.X))
                        dve.tensor_scalar(neg[:], mx[:], -SCALE, None, ALU.mult).then_inc(max_ready, 1)
                    if slot == 3:
                        dve.wait_ge(exp_ready, b + 2)
                        dve.reciprocal(inv[:], total[:]).then_inc(inv_ready, 1)
                    if slot in (3, 4):
                        c = slot - 3
                        part = (slice(None), slice(4 * c, 4 * c + 4))
                        dve.wait_ge(pT_hi_ready, b * 3 + (c + 1))
                        dve.tensor_tensor(pT_lo[part], psum[:, PT, :].rearrange("p (k n) -> p k n", n=P), f(pT_hi[part]),
                                          ALU.subtract).then_inc(pT_ready, 1)

                def body(b, prev, nxt):
                    step = Steps(dve, dve_step)
                    step.base = b * (T + 2) - (2 if prev else 0)
                    for t in range(T):
                        if t + 2 < T:
                            lT_split(b, t + 2)
                        elif nxt:
                            lT_split(b + 1, t + 2 - T)
                        if prev:
                            tail(b - 1, t, step)
                        if t == T - 1 and nxt:
                            place_queries(b + 1)
                        sums(b, t)
                        scores(b, t, step)

                def last_tail(b):
                    step = Steps(dve, dve_step)
                    step.base = b * (T + 2) + T
                    for slot in range(T):
                        tail(b, slot, step)

                dve.sem_inc(ss_ready, 2)
                dve.sem_inc(st_ready, 2)
                dve.tensor_copy(wc_lo[:, :, 0:LAST], f(wuk[1][:, :, 2 * CW:])).then_inc(wc_set, 1)
                place_queries(0)
                lT_split(0, 0)
                lT_split(0, 1)
                streams(dve, body, last_tail)

            @block.tensor
            def _(pe):
                def keys(b, t):
                    k, tile = banks(t), slice(t * P, (t + 1) * P)
                    pe.wait_ge(lT_ready, b * T + (t + 1))
                    pe.wait_ge(st_ready, b * T + (t + 1))
                    for c in range(3):
                        if c == 2 and t == 0:
                            pe.wait_ge(wc_ready, b + 1)
                        for i in range(2):
                            hi, lo = (w[:, i, c * CW:(c + 1) * CW] for w in wuk) if c < 2 else (wc_hi[:, i, :], wc_lo[:, i, :])
                            mm3(pe, psum[:, k + c, 0:CW], lT_hi[:, i, tile], lT_lo[:, i, tile], hi, lo, i == 0, i == 1)
                    if t % 2 == 0:
                        pe.wait_ge(kpe_in[t // 2], b * 16 + 16)
                    pe.matmul(psum[:, k + 2, CW:CW + P], kpeT[:, tile], qrT[:, b, :], start=True, stop=True
                              ).then_inc(k_ready, 1)

                def turn(b, t):
                    pe.wait_ge(st_ready, b * T + (2 + t + 1))
                    if t % 4 == 0:
                        pe.wait_ge(s_ready, b * 2 + (t // 4 + 1))
                    pe.transpose(psum[:, SB, (t % 4) * P:(t % 4 + 1) * P], st[:, t % 2, :], ident[:]).then_inc(sb_raw, 1)

                def before(b, slot):
                    if slot in (3, 4, 5):
                        c = slot - 3
                        if c == 0:
                            pe.wait_ge(exp_ready, b + 2)
                            pe.wait_ge(oT_ready, b + 1)
                        else:
                            pe.wait_ge(pT_ready, b * 2 + c)
                        for k in range(4 * c, min(4 * c + 4, T + 1)):
                            mm = pe.transpose(psum[:, PT, (k % 4) * P:(k % 4 + 1) * P], pr[:, k * P:(k + 1) * P], ident[:])
                        mm.then_inc(pT_raw, 1)
                    if slot == 6:
                        pe.wait_ge(pT_hi_ready, b * 3 + 3)
                        pe.wait_ge(l_ready, b * 4 + 4)
                        for k in range(T):
                            mm3(pe, psum[:, PT, 0:KL], pT_hi[:, k, :], pT_lo[:, k, :], l_hi[:, k, :], l_lo[:, k, :],
                                k == 0, False)
                        pe.matmul(psum[:, PT, 0:KL], pT_new[:], l_new[:, b, :], start=False, stop=True
                                  ).then_inc(pv_ready, 1)

                def after(b, slot):
                    if slot < 2:
                        turn(b, T - 2 + slot)
                    if slot == 7:
                        pe.wait_ge(o_ready, b + 1)
                        for k in range(2):
                            mm = pe.transpose(psum[:, PT, k * P:(k + 1) * P], o[:, k * P:(k + 1) * P], ident[:])
                        mm.then_inc(oT_raw, 1)

                def body(b, prev, nxt):
                    for t in range(T):
                        if prev:
                            before(b - 1, t)
                        keys(b, t)
                        if prev:
                            after(b - 1, t)
                        if t >= 2:
                            turn(b, t - 2)

                def tail(b):
                    for slot in range(T):
                        before(b, slot)
                        after(b, slot)

                pe.sem_inc(k_ready, 8)
                pe.sem_inc(sb_raw, 2)
                pe.sem_inc(pT_raw, 1)
                pe.sem_inc(pv_ready, 1)
                pe.wait_ge(const_set, 2)
                pe.wait_ge(wc_set, 2)
                pe.wait_ge(const_in, 16)
                pe.wait_ge(l_new_in, 16)
                streams(pe, body, tail)
                pe.wait_ge(oT_ready, 1 + NB)
                for h in range(H):
                    for k in range(2):
                        mm = pe.matmul(psum[:, h // 4, (h % 4) * P:(h % 4 + 1) * P], wuv[:, k, h * DN:(h + 1) * DN],
                                       oT[:, k, h].rearrange("p b t -> p (b t)"), start=(k == 0), stop=(k == 1))
                mm.then_inc(out_raw, 1)


def gating_phase(nc, psum, io, ident):
    CHUNKS = (2, 3, 0, 1)
    with Phase(nc, "gate") as ph:
        w_hi, w_lo = ph.sb("w_hi", [P, KT, 2 * D], F32R), ph.sb("w_lo", [P, KT, 2 * D], F32R)
        w_raw = ph.sb("w_raw", [P, 2, D])
        x = ph.sb("x", [P, 3, D])
        hT_hi = [ph.sb(f"hT_hi{i}", [P, KT, P], F32R) for i in range(2)]
        hT_lo = [ph.sb(f"hT_lo{i}", [P, KT, P], F32R) for i in range(2)]
        scale_t, shift_t, g_v = ph.sb("scale_t", [P, D]), ph.sb("shift_t", [P, D]), ph.sb("g_v", [P, D])
        z = ph.sb("z", [P, 2, 2 * D])
        ws = ph.sb("ws", [P, 2, G, P])
        bs = ph.sb("bs", [P, 2, G])
        gT = ph.sb("gT", [P, KT, P])
        junk = ph.sb("junk", [P, D], BF16)
        ss, ms, rstd = ph.sb("ss", [P, 2]), ph.sb("ms", [P, 2]), ph.sb("rstd", [P, 2])
        vss, vms, vr = ph.sb("vss", [P, 2]), ph.sb("vms", [P, 2]), ph.sb("vr", [P, 2])
        power = ph.sb("power", [P, 1])

        raw_in, x_in = ph.sems("raw_in", 2), ph.sems("x_in", 3)
        tab_in, stab_in, const_in = ph.sem("tab_in"), ph.sem("stab_in"), ph.sem("const_in")
        ws_in, ws_zero, blocks_in, ws_ready = ph.sem("ws_in"), ph.sem("ws_zero"), ph.sem("blocks_in"), ph.sem("ws_ready")
        const_set = ph.sem("const_set")
        w_hi_ready, w_ready = ph.sem("w_hi_ready"), ph.sem("w_ready")
        ss_ready, rstd_ready, xn_ready, h_ready = (ph.sem(n) for n in ("ss_ready", "rstd_ready", "xn_ready", "h_ready"))
        hT_raw, hT_hi_ready, hT_ready = ph.sem("hT_raw"), ph.sem("hT_hi_ready"), ph.sem("hT_ready")
        z_raw, z_ready = ph.sem("z_raw"), ph.sem("z_ready")
        vss_ready, vr_ready, v_ready = ph.sem("vss_ready"), ph.sem("vr_ready"), ph.sem("v_ready")
        mix_raw, g_ready, gT_raw, gT_ready = (ph.sem(n) for n in ("mix_raw", "g_ready", "gT_raw", "gT_ready"))
        gT_stored, v_stored = ph.sem("gT_stored"), ph.sem("v_stored")
        pool_step = ph.sem("pool_step")

        with nc.Block() as block:
            @block.sync
            def _(sp):
                def load_x(t):
                    if t >= 3:
                        sp.wait_ge(hT_raw, 2 * (t - 2))
                    sp.dma_start(x[:, t % 3, :], io["x_mid"][t]).then_inc(x_in[t % 3], 16)

                load_x(0)
                load_table(sp, scale_t, io["mod"], 1, SCALE1, 0, tab_in)
                load_table(sp, shift_t, io["mod"], 1, SHIFT1, 0, tab_in)
                for n in range(2 * KT):
                    if n >= 2:
                        sp.wait_ge(w_ready, n - 1)
                    half, k = 1 - n // KT, n % KT
                    sp.dma_start(w_raw[:, n % 2, :], io["cm_w_in"][k, :, half * D:(half + 1) * D]
                                 ).then_inc(raw_in[n % 2], 16)
                    if n == 2:
                        load_x(1)
                        load_x(2)
                        sp.dma_start(ws[:, 0], io["w_sT"]).then_inc(ws_in, 16)
                        sp.dma_start(bs[:, 0, :], io["b_sT"]).then_inc(const_in, 16)
                        for b in range(NB):
                            sp.dma_start(bs[b * TS:(b + 1) * TS, 1, :], io["b_sT"][0:TS, :]).then_inc(const_in, 16)
                        sp.dma_start(g_v[:], io["cm_g_v"].partition_broadcast(P)).then_inc(const_in, 16)
                    if n == 6:
                        sp.wait_ge(ws_zero, 1)
                        for b in range(NB):
                            rows = slice(b * TS, (b + 1) * TS)
                            sp.dma_start(ws[rows, 1, :, rows], io["w_sT"][0:TS, :, 0:TS]).then_inc(blocks_in, 16)
                for t in range(TT + 2):
                    if 3 <= t + 1 < TT:
                        load_x(t + 1)
                    if t == SAMPLE - 1:
                        sp.wait_ge(h_ready, SAMPLE)
                        load_table(sp, scale_t, io["mod"], 1, SCALE1, SAMPLE, stab_in)
                        load_table(sp, shift_t, io["mod"], 1, SHIFT1, SAMPLE, stab_in)
                    if t >= 2:
                        u = t - 2
                        sp.wait_ge(gT_ready, 2 * u + 2)
                        sp.dma_start(io["mixT"].rearrange("k p n -> p k n")[:, :, u * P:(u + 1) * P], gT[:]
                                     ).then_inc(gT_stored, 16)
                    if t == SAMPLE + 1:
                        sp.wait_ge(v_ready, TT)
                        sp.dma_start(io["v_new"], z[:, SAMPLE % 2, D:]).then_inc(v_stored, 16)
                sp.wait_ge(gT_stored, 16 * TT)
                sp.wait_ge(v_stored, 16)

            @block.gpsimd
            def _(pool):
                step = Steps(pool, pool_step)
                pool.memset(power[:], -0.5).then_inc(const_set, 1)
                pool.wait_ge(const_set, 1)

                def rms(t):
                    c = slice(t % 2, t % 2 + 1)
                    pool.wait_ge(ss_ready, t + 1)
                    step.run(pool.tensor_scalar(ms[:, c], ss[:, c], 1.0 / D, EPS, ALU.mult, ALU.add))
                    if t >= 2:
                        pool.wait_ge(xn_ready, t - 1)
                    pool.tensor_tensor(rstd[:, c], ms[:, c], power[:], ALU.pow).then_inc(rstd_ready, 1)

                def v_rms(t):
                    c = slice(t % 2, t % 2 + 1)
                    pool.wait_ge(vss_ready, t + 1)
                    step.run(pool.tensor_scalar(vms[:, c], vss[:, c], 1.0 / D, EPS, ALU.mult, ALU.add))
                    if t >= 2:
                        pool.wait_ge(v_ready, t - 1)
                    pool.tensor_tensor(vr[:, c], vms[:, c], power[:], ALU.pow).then_inc(vr_ready, 1)

                rms(0)
                pool.memset(ws[:, 1], 0.0).then_inc(ws_zero, 1)
                pool.wait_ge(ws_in, 16)
                pool.wait_ge(ws_zero, 1)
                pool.memset(ws[64:, 0, :, 0:64], 0.0).then_inc(ws_ready, 1)
                pool.wait_ge(ws_ready, 1)
                for slot in range(-1, TT + 1):
                    if 0 <= slot < TT:
                        v_rms(slot)
                    if 0 <= slot + 2 < TT:
                        rms(slot + 2)

            @block.scalar
            def _(act):
                def squares(t):
                    act.wait_ge(x_in[t % 3], 16 * (t // 3 + 1))
                    if t >= 2:
                        act.wait_ge(rstd_ready, t - 1)
                    if t >= 1:
                        act.wait_ge(ss_ready, t)
                    if t >= 2:
                        act.wait_ge(vss_ready, t - 1)
                    act.activation(junk[:], x[:, t % 3, :], ACT.Square, accum_out=ss[:, t % 2:t % 2 + 1]
                                   ).then_inc(ss_ready, 1)

                def w_split(n):
                    half, k = 1 - n // KT, n % KT
                    act.wait_ge(raw_in[n % 2], 16 * (n // 2 + 1))
                    act.activation(w_hi[:, k, half * D:(half + 1) * D], w_raw[:, n % 2, :], ACT.Copy).then_inc(w_hi_ready, 1)

                def hT_split(t):
                    for half in range(2):
                        act.wait_ge(hT_raw, 2 * t + half + 1)
                        if t >= 2:
                            act.wait_ge(z_raw, 4 * (t - 1))
                        act.activation(hT_hi[t % 2][:, 4 * half:4 * half + 4, :],
                                       psum[:, half, :].rearrange("p (k n) -> p k n", k=4),
                                       ACT.Copy).then_inc(hT_hi_ready, 1)

                def gelu(t, n):
                    act.wait_ge(z_raw, 4 * t + n + 1)
                    c = CHUNKS[n]
                    if n == 0 and t >= 2:
                        act.wait_ge(mix_raw, t - 1)
                    if n == 2 and t >= 2:
                        act.wait_ge(gT_raw, 2 * (t - 1))
                    act.activation(z[:, t % 2, c * 512:(c + 1) * 512], psum[:, 2 + n, :], ACT.Gelu_apprx_tanh
                                   ).then_inc(z_ready, 1)

                def v_squares(t):
                    act.wait_ge(z_ready, 4 * t + 2)
                    if t >= 2:
                        act.wait_ge(vr_ready, t - 1)
                    act.wait_ge(ss_ready, min(t + 2, TT))
                    act.activation(junk[:], z[:, t % 2, D:], ACT.Square,
                                   accum_out=vss[:, t % 2:t % 2 + 1]).then_inc(vss_ready, 1)

                def gT_out(t):
                    for half in range(2):
                        act.wait_ge(gT_raw, 2 * t + half + 1)
                        if t >= 1:
                            act.wait_ge(gT_stored, 16 * t)
                        act.activation(gT[:, 4 * half:4 * half + 4, :],
                                       psum[:, half, :].rearrange("p (k n) -> p k n", k=4), ACT.Copy
                                       ).then_inc(gT_ready, 1)

                squares(0)
                for n in range(2):
                    w_split(n)
                hT_split(0)
                for n in range(2, 2 * KT):
                    w_split(n)
                    if n == 4:
                        squares(1)
                for slot in range(TT + 2):
                    if slot < TT:
                        gelu(slot, 0)
                        gelu(slot, 1)
                        v_squares(slot)
                    if 0 <= slot - 2 < TT:
                        gT_out(slot - 2)
                    if slot < TT:
                        gelu(slot, 2)
                    if slot + 1 < TT:
                        hT_split(slot + 1)
                    if slot < TT:
                        gelu(slot, 3)
                    if slot + 2 < TT:
                        squares(slot + 2)

            @block.vector
            def _(dve):
                def norm(t):
                    if t == 0:
                        dve.wait_ge(tab_in, 32)
                    if t == SAMPLE:
                        dve.wait_ge(stab_in, 32 * NB)
                    dve.wait_ge(rstd_ready, t + 1)
                    dve.scalar_tensor_tensor(x[:, t % 3, :], x[:, t % 3, :], rstd[:, t % 2:t % 2 + 1], scale_t[:],
                                             ALU.mult, ALU.mult).then_inc(xn_ready, 1)
                    dve.wait_ge(xn_ready, t + 1)
                    dve.tensor_tensor(x[:, t % 3, :], x[:, t % 3, :], shift_t[:], ALU.add).then_inc(h_ready, 1)

                def w_split(n):
                    half, k = 1 - n // KT, n % KT
                    cols = slice(half * D, (half + 1) * D)
                    dve.wait_ge(w_hi_ready, n + 1)
                    dve.tensor_tensor(w_lo[:, k, cols], w_raw[:, n % 2, :], f(w_hi[:, k, cols]), ALU.subtract
                                      ).then_inc(w_ready, 1)

                def hT_split(t):
                    for half in range(2):
                        dve.wait_ge(hT_hi_ready, 2 * t + half + 1)
                        ks = slice(4 * half, 4 * half + 4)
                        dve.tensor_tensor(hT_lo[t % 2][:, ks, :], psum[:, half, :].rearrange("p (k n) -> p k n", k=4),
                                          f(hT_hi[t % 2][:, ks, :]), ALU.subtract).then_inc(hT_ready, 1)

                def norm_v(t):
                    if t == 0:
                        dve.wait_ge(const_in, 16 * (2 + NB))
                    dve.wait_ge(vr_ready, t + 1)
                    v = z[:, t % 2, D:]
                    dve.scalar_tensor_tensor(v, v, vr[:, t % 2:t % 2 + 1], g_v[:], ALU.mult, ALU.mult).then_inc(v_ready, 1)

                def gated(t):
                    dve.wait_ge(mix_raw, t + 1)
                    dve.wait_ge(z_ready, 4 * t + 4)
                    for g in range(G):
                        u = z[:, t % 2, g * P:(g + 1) * P]
                        last = dve.scalar_tensor_tensor(u, psum[:, 6 + g // 4, (g % 4) * P:(g % 4 + 1) * P],
                                                        bs[:, int(t == SAMPLE), g:g + 1], u, ALU.add, ALU.mult)
                    last.then_inc(g_ready, 1)

                norm(0)
                for n in range(2):
                    w_split(n)
                hT_split(0)
                for n in range(2, 2 * KT):
                    w_split(n)
                    if n == 8:
                        norm(1)
                for slot in range(TT + 1):
                    if slot < TT:
                        norm_v(slot)
                    if slot + 1 < TT:
                        hT_split(slot + 1)
                    if 0 <= slot - 1 < TT:
                        gated(slot - 1)
                    if slot + 2 < TT:
                        norm(slot + 2)

            @block.tensor
            def _(pe):
                def transposes(t):
                    pe.wait_ge(h_ready, t + 1)
                    if t >= 1:
                        pe.wait_ge(hT_ready, 2 * t)
                    if t >= 3:
                        pe.wait_ge(gT_ready, 2 * (t - 2))
                    for k in range(KT):
                        mm = pe.transpose(psum[:, k // 4, (k % 4) * P:(k % 4 + 1) * P],
                                          x[:, t % 3, k * P:(k + 1) * P], ident[:])
                        if k % 4 == 3:
                            mm.then_inc(hT_raw, 1)

                def product(t, n):
                    c = CHUNKS[n]
                    cols = slice(c * 512, (c + 1) * 512)
                    pe.wait_ge(hT_ready, 2 * t + 2)
                    if t >= 1:
                        pe.wait_ge(z_ready, 4 * (t - 1) + n + 1)
                    for k in range(KT):
                        if t == 0:
                            pe.wait_ge(w_ready, (n // 2) * KT + k + 1)
                        mm = mm3(pe, psum[:, 2 + n, :], hT_hi[t % 2][:, k, :], hT_lo[t % 2][:, k, :],
                                 w_hi[:, k, cols], w_lo[:, k, cols], k == 0, k == KT - 1)
                    mm.then_inc(z_raw, 1)

                def mix(t):
                    if t == 0:
                        pe.wait_ge(ws_ready, 1)
                        pe.wait_ge(blocks_in, 16 * NB)
                    pe.wait_ge(v_ready, t + 1)
                    if t >= 1:
                        pe.wait_ge(g_ready, t)
                    for g in range(G):
                        mm = pe.matmul(psum[:, 6 + g // 4, (g % 4) * P:(g % 4 + 1) * P], ws[:, int(t == SAMPLE), g, :],
                                       z[:, t % 2, D + g * P:D + (g + 1) * P], start=True, stop=True)
                    mm.then_inc(mix_raw, 1)

                def turn(t):
                    pe.wait_ge(g_ready, t + 1)
                    if t + 1 < TT:
                        pe.wait_ge(hT_ready, min(2 * (t + 3), 2 * TT))
                    if t >= 1:
                        pe.wait_ge(gT_ready, 2 * t)
                    for k in range(KT):
                        mm = pe.transpose(psum[:, k // 4, (k % 4) * P:(k % 4 + 1) * P],
                                          z[:, t % 2, k * P:(k + 1) * P], ident[:])
                        if k % 4 == 3:
                            mm.then_inc(gT_raw, 1)

                transposes(0)
                for slot in range(TT + 2):
                    if slot < TT:
                        product(slot, 0)
                        product(slot, 1)
                    if 0 <= slot - 2 < TT:
                        turn(slot - 2)
                    if slot < TT:
                        product(slot, 2)
                    if slot + 1 < TT:
                        transposes(slot + 1)
                    if slot < TT:
                        product(slot, 3)
                    if 0 <= slot - 1 < TT:
                        mix(slot - 1)


def build_program(nc, io):
    Phase.semaphores = []
    with ExitStack() as ctx:
        psum = ctx.enter_context(nc.psum_tensor("psum", [P, 8, 512], F32))
        ident = ctx.enter_context(nc.sbuf_tensor("ident", [P, P], F32))
        load_constants(nc, io, ident)
        ada_phase(nc, psum, io, 0)
        ada_phase(nc, psum, io, 1)
        with ExitStack() as latents:
            def split(name, shape):
                return [latents.enter_context(nc.sbuf_tensor(f"{name}_{part}", shape, F32R)) for part in ("hi", "lo")]
            cqT = split("cqT", [P, QL // P, NTOK])
            ckvT = split("ckvT", [P, KL // P, NTOK])
            krT = split("krT", [P, NTOK])
            latent_phase(nc, psum, io, ident, cqT, ckvT, krT)
            prompt_attention_phase(nc, psum, io, ident, cqT, ckvT, krT)
            sample_phases(nc, psum, io, ident, cqT, ckvT, krT)
        Phase.recycle_semaphores(nc)
        mlp_half(nc, psum, io, ident, 0, io["x"], io["x_mid"])
        gating_phase(nc, psum, io, ident)
        mlp_half(nc, psum, io, ident, 1, io["x_mid"], io["y"])


def sample_phases(nc, psum, io, ident, cqT, ckvT, krT):
    with ExitStack() as ctx:
        def sb(name, shape, dt=F32):
            return ctx.enter_context(nc.sbuf_tensor(f"sample_{name}", shape, dt))
        wuk = [sb(f"wuk_{part}", [P, 2, D], F32R) for part in ("hi", "lo")]
        qe = [sb(f"qe_{part}", [P, 2, NB, P], F32R) for part in ("hi", "lo")]
        qrT = sb("qrT", [P, NB, P])
        s_new = sb("s_new", [P, P])
        sample_query_phase(nc, psum, io, ident, cqT, ckvT, krT, wuk, qe, qrT, s_new)
        sample_attention_phase(nc, psum, io, ident, wuk, qe, qrT, s_new)


def mlp_half(nc, psum, io, ident, layer, x_from, x_to):
    with ExitStack() as ctx:
        hT = [ctx.enter_context(nc.sbuf_tensor(f"h2T{layer}_{part}", [P, KT, NTOK], F32R)) for part in ("hi", "lo")]
        project_phase(nc, psum, io, ident, layer, x_from, hT)
        ffn_phase(nc, psum, io, layer, hT, x_to)


def load_constants(nc, io, ident):
    with Phase(nc, "const") as ph:
        loaded = ph.sem("loaded")
        with nc.Block() as block:
            @block.sync
            def _(sp):
                sp.dma_start(ident[:], io["ident"]).then_inc(loaded, 16)
                sp.wait_ge(loaded, 16)


SCRATCH = {
    "mod": (2, 1 + NB, 6 * D),
    "mixT": (KT, P, NTOK),
    "x_res": (TT, P, D),
    "x_mid": (TT, P, D),
}
OUTPUTS = {
    "y": (TT, P, D), "ckv_new": (TT, P, KL), "kpe_new": (TT, P, DR), "v_new": (P, D),
}


def lay_out(v):
    def a(name):
        return np.asarray(v[name])

    def rows(w):
        return w.reshape(-1, P, w.shape[-1])

    pair = 2 * (DN + DR)
    uk, uv = a("mla_w_uk")[0], a("mla_w_uv")[0]
    kv = np.concatenate([uk.reshape(2, P, 4, 2 * DN), uv.reshape(2, P, 4, 2 * DN)], axis=3)
    cq = a("mla_w_q_up")[0].reshape(QL // P, P, 4, pair)
    c = np.concatenate([a("c_prompt"), a("c_sample")])
    cache = a("cache_ckv")[0]
    out = {
        "x": np.concatenate([a("x_prompt").reshape(SEQ, D), a("x_sample").reshape(NB * TS, D)]).reshape(TT, P, D),
        "c_cols": c.T.reshape(KT, P, 1 + NB).transpose(1, 0, 2),
        "ada_w": a("ada_w").reshape(2, KT, P, 6 * D),
        "ada_b": a("ada_b"),
        "norm_g": np.stack([a("norm1_g"), a("norm2_g")], axis=1),
        "w1": a("ffn_w1").reshape(2, KT, P, FT, P).transpose(0, 3, 2, 1, 4),
        "w2": a("ffn_w2").reshape(2, FT, P, D),
        "w_in": rows(a("mla_w_in")[0]),
        "g_qa": a("mla_g_qa")[0], "g_kva": a("mla_g_kva")[0], "g_kr": a("mla_g_kr")[0],
        "g_qn": a("mla_g_qn")[0], "g_qr": a("mla_g_qr")[0], "g_kn": a("mla_g_kn")[0],
        "w_q_pair": cq.transpose(2, 1, 0, 3),
        "w_kv_pair": kv.transpose(2, 1, 0, 3),
        "w_q": rows(a("mla_w_q_up")[0]).transpose(1, 0, 2),
        "w_uk": uk.reshape(2, P, H * DN).transpose(1, 0, 2),
        "w_ukT": uk.transpose(2, 1, 0),
        "w_uv": uv.reshape(2, P, H * DN).transpose(1, 0, 2),
        "w_o0": rows(a("mla_w_o")[0]), "w_o1": rows(a("cm_w_o")[0]),
        "cache": cache.reshape(NB, PAST // P, P, KL).transpose(0, 2, 1, 3),
        "cacheT": cache.reshape(NB, PAST, 2, P).transpose(0, 3, 2, 1),
        "kpeT": a("cache_kpe")[0].transpose(0, 2, 1),
        "cm_w_in": rows(a("cm_w_in")[0]),
        "cm_g_v": a("cm_g_v")[0],
        "w_sT": a("cm_w_s")[0].transpose(2, 0, 1),
        "b_sT": a("cm_b_s")[0].T,
    }
    return {k: np.ascontiguousarray(x) for k, x in out.items()}


def constants():
    half = DR // 2
    pos = np.concatenate([np.arange(SEQ), np.tile(PAST + np.arange(TS), NB)]).astype(np.float32)
    inv = (np.float32(1.0) / (np.float32(10000.0) ** (np.arange(half, dtype=np.float32) / np.float32(half)))).astype(np.float32)
    ang = pos[:, None] * inv[None, :]
    cos, sin = np.cos(ang), np.sin(ang)

    def tiles(t):
        return np.ascontiguousarray(t.reshape(TT, P, DR).transpose(1, 0, 2)).astype(np.float32)

    r, key = np.arange(P)[:, None, None], np.arange(2 * P)[None, None, :]
    seen = key < P * np.arange(2)[None, :, None] + 64 * (r // 64 + 1)
    return {
        "ident": np.eye(P, dtype=np.float32),
        "ident_bf": np.eye(P, dtype=np.float32).astype(mybir.dt.np(BF16)),
        "mask": np.where(seen, 0.0, -1e30).astype(mybir.dt.np(BF16)),
        "cos": tiles(np.concatenate([cos, cos], axis=1)),
        "sin": tiles(np.concatenate([-sin, sin], axis=1)),
    }


def kernel(**inputs):
    from concourse import bacc
    from concourse.bass_utils import run_bass_kernel_spmd

    arrays = {**lay_out(inputs), **constants()}
    nc = bacc.Bacc("TRN2", target_bir_lowering=False, num_devices=1)
    io = {k: nc.dram_tensor(f"in_{k}", v.shape, mybir.dt.from_np(v.dtype), kind="ExternalInput").ap()
          for k, v in arrays.items()}
    io |= {k: nc.dram_tensor(f"out_{k}", s, F32, kind="ExternalOutput").ap() for k, s in OUTPUTS.items()}
    io |= {k: nc.dram_tensor(f"scratch_{k}", s, F32).ap() for k, s in SCRATCH.items()}
    build_program(nc, io)
    r = run_bass_kernel_spmd(nc, [{f"in_{k}": v for k, v in arrays.items()}], core_ids=[0]).results[0]
    y, ckv, kpe, v = (r[f"out_{k}"] for k in ("y", "ckv_new", "kpe_new", "v_new"))
    return (y[:SAMPLE].reshape(1, SEQ, D), y[SAMPLE].reshape(NB, TS, D),
            ckv[:SAMPLE].reshape(1, 1, SEQ, KL), kpe[:SAMPLE].reshape(1, 1, SEQ, DR),
            ckv[SAMPLE].reshape(1, NB, TS, KL), kpe[SAMPLE].reshape(1, NB, TS, DR),
            v.reshape(1, NB, TS, D))
```

```python
from contextlib import ExitStack

import numpy as np
import concourse.bass as bass
from concourse import mybir

F32 = mybir.dt.float32
F32R = mybir.dt.float32r
BF16 = mybir.dt.bfloat16
ALU = mybir.AluOpType
ACT = mybir.ActivationFunctionType
AX = mybir.AxisListType

P = 128
D = 1024
KT = D // P
SEQ = 1024
NB = 8
TS = 16
TT = SEQ // P + 1
NTOK = TT * P
SAMPLE = TT - 1
H = 8
DN, DR = 128, 64
QL, KL = 384, 256
A_W = QL + KL + DR
PAST = 1024
FF = 4096
FT = FF // P
G = 8
EPS = 1e-6
SCALE = (DN + DR) ** -0.5
SHIFT1, SCALE1, GATE1, SHIFT2, SCALE2, GATE2 = range(6)


class Phase:

    semaphores = []

    def __init__(self, nc, name):
        self.nc, self.name, self.stack = nc, name, ExitStack()

    def __enter__(self):
        return self

    def __exit__(self, *a):
        self.stack.close()

    @classmethod
    def recycle_semaphores(cls, nc):
        nc.clear_and_free_semaphores(cls.semaphores)
        cls.semaphores = []
        nc.all_engine_barrier()

    def sb(self, name, shape, dt=F32):
        return self.stack.enter_context(self.nc.sbuf_tensor(f"{self.name}_{name}", list(shape), dt))

    def sem(self, name):
        sem = self.nc.alloc_semaphore(f"{self.name}_{name}")
        Phase.semaphores.append(sem)
        return sem

    def sems(self, name, n):
        return [self.sem(f"{name}{i}") for i in range(n)]


class Steps:

    def __init__(self, eng, sem):
        self.eng, self.sem, self.n, self.base = eng, sem, 0, 0

    def then(self, ins):
        self.n += 1
        ins.then_inc(self.sem, 1)

    def done(self):
        self.eng.wait_ge(self.sem, self.base + self.n)

    def run(self, ins):
        self.then(ins)
        self.done()


def mm3(pe, out, a_hi, a_lo, b_hi, b_lo, first, last):
    pe.matmul(out, a_hi, b_hi, start=first, stop=False)
    pe.matmul(out, a_hi, b_lo, start=False, stop=False)
    return pe.matmul(out, a_lo, b_hi, start=False, stop=last)


def f(ap):
    return ap.bitcast(F32)


def table_row(mod, layer, part, tile):
    base = mod[layer, 0, part * D:(part + 1) * D]
    if tile != SAMPLE:
        return [(0, P, base.partition_broadcast(P))]
    return [(b * TS, TS, mod[layer, 1 + b, part * D:(part + 1) * D].partition_broadcast(TS))
            for b in range(NB)]


TABLE_DMAS = {False: 1, True: NB}


def load_table(eng, dst, mod, layer, part, tile, sem):
    for p0, n, src in table_row(mod, layer, part, tile):
        eng.dma_start(dst[p0:p0 + n, :], src).then_inc(sem, 16)


FRONT = 2 * D
ATT_N = 128
ATT_STEPS = (6 * D - FRONT) // (4 * ATT_N)
FFN_N = 96
FFN_STEPS = 6 * D // (4 * FFN_N)
HK = KT // 2
BIAS, PLUS, GAIN = range(3)


def mod_products(pe, out, c_silu, w, k0, ks, n, first, last):
    for k in range(ks):
        for j in range(4):
            mm = pe.matmul(out[32 * j:32 * j + 32, :], c_silu[:, k0 + k, :], w[:, k, j * n:(j + 1) * n],
                           start=(first and k == 0), stop=(last and k == ks - 1), tile_position=(0, 32 * j))
    return mm


def mod_finish(dve, step, mod, products, addend, tab):
    step.run(dve.tensor_tensor(mod, products, addend, ALU.add))
    step.run(dve.tensor_tensor(mod, mod, tab[:, PLUS, :], ALU.add))
    return dve.tensor_tensor(mod, mod, tab[:, GAIN, :], ALU.mult)


def mod_tables(src, n):
    return src.unsqueeze(1).to_broadcast([4, 32, 3, n])


def mod_store(eng, io, layer, n, step, mod, sem):
    rows = io["mod"][layer].rearrange("b (s j n) -> s j b n", j=4, n=n)
    for j in range(4):
        eng.dma_start(rows[step, j], mod[32 * j:32 * j + 1 + NB, :]).then_inc(sem, 16)


def latent_phase(nc, psum, io, ident, c_silu, cqT, ckvT, krT):
    QT = QL // P
    MOD_N = FRONT // 4
    RR = KT // 2
    tiles = [SAMPLE] + list(range(SAMPLE))
    with Phase(nc, "lat") as ph:
        w_hi = ph.sb("w_hi", [P, KT, A_W], F32R)
        w_lo = ph.sb("w_lo", [P, KT, A_W], F32R)
        raw = ph.sb("raw", [P, RR, FRONT])
        c_cols = ph.sb("c_cols", [P, KT, 1 + NB])
        mod_tab, mod = ph.sb("mod_tab", [P, 3, MOD_N]), ph.sb("mod", [P, MOD_N])
        sel = ph.sb("sel", [P, 2, 4, P])
        x = ph.sb("x", [P, 2, D])
        junk = ph.sb("junk", [P, D], BF16)
        junk3 = ph.sb("junk3", [P, A_W], BF16)
        xn = ph.sb("xn", [P, D])
        h = ph.sb("h", [P, 2, D])
        hT_hi = [ph.sb(f"hT_hi{i}", [P, KT, P], F32R) for i in range(2)]
        hT_lo = [ph.sb(f"hT_lo{i}", [P, KT, P], F32R) for i in range(2)]
        scale_t = ph.sb("scale_t", [P, D])
        shift_t = ph.sb("shift_t", [P, D])
        gains = ph.sb("gains", [P, A_W])
        cos = ph.sb("cos", [P, TT, DR])
        sin = ph.sb("sin", [P, TT, DR])
        inv_n = ph.sb("inv_n", [P, 3])
        eps3 = ph.sb("eps3", [P, 3])
        power = ph.sb("power", [P, 3])
        ss = ph.sb("ss", [P, 2])
        ms = ph.sb("ms", [P, 2])
        rstd = ph.sb("rstd", [P, 2])
        ss3 = ph.sb("ss3", [P, 2, 3])
        ms3 = ph.sb("ms3", [P, 2, 3])
        r3 = ph.sb("r3", [P, 2, 3])
        cq = ph.sb("cq", [P, 2, QL])
        ckv = ph.sb("ckv", [P, 2, KL])
        krn = ph.sb("krn", [P, DR])
        kr_cos = ph.sb("kr_cos", [P, DR])
        kr_sin = ph.sb("kr_sin", [P, DR])
        kr = ph.sb("kr", [P, 2, 2 * DR])

        raw_in = ph.sems("raw_in", RR)
        c_in, c_zero, c_ready = ph.sem("c_in"), ph.sem("c_zero"), ph.sem("c_ready")
        mod_tab_in, mod_w_used, mod_step = ph.sem("mod_tab_in"), ph.sem("mod_w_used"), ph.sem("mod_step")
        mod_ready = ph.sem("mod_ready")
        w_hi_ready, w_ready = ph.sem("w_hi_ready"), ph.sem("w_ready")
        x_in = ph.sems("x_in", 2)
        stab_ready, shift_raw, scale_raw, tab_ready = (
            ph.sem(n) for n in ("stab_ready", "shift_raw", "scale_raw", "tab_ready"))
        sel_in, const_in = ph.sem("sel_in"), ph.sem("const_in")
        const_set = ph.sem("const_set")
        ss_ready, rstd_ready, h_ready = ph.sem("ss_ready"), ph.sem("rstd_ready"), ph.sem("h_ready")
        hT_raw, hT_hi_ready, hT_ready = ph.sem("hT_raw"), ph.sem("hT_hi_ready"), ph.sem("hT_ready")
        a_ready, ss3_ready, r3_ready = ph.sem("a_ready"), ph.sem("ss3_ready"), ph.sem("r3_ready")
        lat_ready, latT_raw = ph.sem("lat_ready"), ph.sem("latT_raw")
        latT_hi_ready, latT_ready = ph.sem("latT_hi_ready"), ph.sem("latT_ready")
        dve_step, pool_step = ph.sem("dve_step"), ph.sem("pool_step")
        stored = ph.sems("stored", 2)
        N_CONST = 5

        def w_raw(k, n):
            return raw[:, k // 2, (k % 2) * A_W:(k % 2 + n) * A_W].rearrange("p (k n) -> p k n", k=n)

        def a_bank(t):
            return 2 + 2 * (t % 2)

        with nc.Block() as block:
            @block.sync
            def _(sp):
                sp.dma_start(c_cols[:], io["c_cols"]).then_inc(c_in, 16)
                sp.dma_start(x[:, 0, :], io["x"][tiles[0]]).then_inc(x_in[0], 16)
                for k in range(KT):
                    if k >= RR:
                        sp.wait_ge(mod_w_used, k - RR + 1)
                    sp.dma_start(raw[:, k % RR, :], io["ada_w_front"][k]).then_inc(raw_in[k % RR], 16)
                    if k == RR - 1:
                        sp.dma_start(mod_tab[:], mod_tables(io["ada_tab_front"], MOD_N)).then_inc(mod_tab_in, 16)
                        sp.dma_start(sel[:], io["mod_sel"]).then_inc(sel_in, 16)
                for i in range(RR):
                    sp.wait_ge(mod_w_used, RR + i + 1)
                    sp.dma_start(w_raw(2 * i, 2), io["w_in"][:, 2 * i:2 * i + 2, :]).then_inc(raw_in[i], 16)
                sp.dma_start(x[:, 1, :], io["x"][tiles[1]]).then_inc(x_in[1], 16)
                for i, (dst, src) in enumerate((
                        (gains[:, 0:QL], io["g_qa"].partition_broadcast(P)),
                        (gains[:, QL:QL + KL], io["g_kva"].partition_broadcast(P)),
                        (gains[:, QL + KL:], io["g_kr"].partition_broadcast(P)),
                        (cos[:], io["cos"]), (sin[:], io["sin"]))):
                    sp.dma_start(dst, src).then_inc(const_in, 16)
                for t in range(2, TT + 3):
                    if t < TT:
                        sp.wait_ge(h_ready, t - 1)
                        sp.dma_start(x[:, t % 2, :], io["x"][tiles[t]]).then_inc(x_in[t % 2], 16)
                    if t >= 3:
                        u = t - 3
                        sp.wait_ge(lat_ready, u + 1)
                        sp.dma_start(io["ckv_new"][tiles[u]], ckv[:, u % 2, :]).then_inc(stored[u % 2], 16)
                        sp.dma_start(io["kpe_new"][tiles[u]], kr[:, u % 2, 0:DR]).then_inc(stored[u % 2], 16)
                sp.wait_ge(stored[0], 32 * ((TT + 1) // 2))
                sp.wait_ge(stored[1], 32 * (TT // 2))

            @block.gpsimd
            def _(pool):
                step = Steps(pool, pool_step)
                pool.memset(c_silu[:], 0.0).then_inc(c_zero, 1)
                pool.memset(inv_n[:, 0:1], 1.0 / QL)
                pool.memset(inv_n[:, 1:2], 1.0 / KL)
                pool.memset(inv_n[:, 2:3], 1.0 / DR)
                pool.memset(eps3[:], EPS)
                pool.memset(power[:], -0.5).then_inc(const_set, 1)
                pool.wait_ge(const_set, 1)

                def rms(t):
                    pool.wait_ge(ss_ready, t + 1)
                    c = slice(t % 2, t % 2 + 1)
                    step.run(pool.tensor_scalar(ms[:, c], ss[:, c], 1.0 / D, EPS, ALU.mult, ALU.add))
                    if t >= 2:
                        pool.wait_ge(h_ready, t - 1)
                    pool.tensor_tensor(rstd[:, c], ms[:, c], power[:, 0:1], ALU.pow).then_inc(rstd_ready, 1)

                def rms3(t):
                    pool.wait_ge(ss3_ready, t + 1)
                    step.run(pool.tensor_tensor(ms3[:, t % 2, :], ss3[:, t % 2, :], inv_n[:], ALU.mult))
                    step.run(pool.tensor_tensor(ms3[:, t % 2, :], ms3[:, t % 2, :], eps3[:], ALU.add))
                    if t >= 2:
                        pool.wait_ge(lat_ready, t - 1)
                    pool.tensor_tensor(r3[:, t % 2, :], ms3[:, t % 2, :], power[:], ALU.pow).then_inc(r3_ready, 1)

                for slot in range(-2, TT + 1):
                    if 0 <= slot - 1 < TT:
                        rms3(slot - 1)
                    if 0 <= slot + 2 < TT:
                        rms(slot + 2)

            @block.scalar
            def _(act):
                def squares(t):
                    act.wait_ge(x_in[t % 2], 16 * (t // 2 + 1))
                    if t >= 2:
                        act.wait_ge(rstd_ready, t - 1)
                    if t >= 1:
                        act.wait_ge(ss_ready, t)
                    act.activation(junk[:], x[:, t % 2, :], ACT.Square,
                                   accum_out=ss[:, t % 2:t % 2 + 1]).then_inc(ss_ready, 1)

                def w_split(k):
                    act.wait_ge(raw_in[k // 2], 16 * 3)
                    act.activation(w_hi[:, k:k + 1, :], w_raw(k, 1), ACT.Copy).then_inc(w_hi_ready, 1)

                def hT_split(t):
                    for half in range(2):
                        act.wait_ge(hT_raw, 2 * t + half + 1)
                        if t >= 2:
                            act.wait_ge(a_ready, t - 1)
                        act.activation(hT_hi[t % 2][:, 4 * half:4 * half + 4, :],
                                       psum[:, half, :].rearrange("p (k n) -> p k n", k=4),
                                       ACT.Copy).then_inc(hT_hi_ready, 1)

                def post(t):
                    act.wait_ge(a_ready, t + 1)
                    if t >= 2:
                        act.wait_ge(r3_ready, t - 1)
                    if t >= 1:
                        act.wait_ge(ss3_ready, t)
                    b = a_bank(t)
                    for n, (c0, c1, src) in enumerate(((0, QL, psum[:, b, 0:QL]), (QL, QL + KL, psum[:, b + 1, 0:KL]),
                                                       (QL + KL, A_W, psum[:, b + 1, KL:KL + DR]))):
                        last = act.activation(junk3[:, c0:c1], src, ACT.Square, accum_out=ss3[:, t % 2, n:n + 1])
                    last.then_inc(ss3_ready, 1)

                def latT_split(t):
                    cols = slice(tiles[t] * P, (tiles[t] + 1) * P)
                    act.wait_ge(latT_raw, t + 1)
                    act.activation(cqT[0][:, :, cols], psum[:, 6, 0:QL].rearrange("p (k n) -> p k n", k=QT), ACT.Copy)
                    act.activation(ckvT[0][:, :, cols], psum[:, 7, 0:KL].rearrange("p (k n) -> p k n", k=2), ACT.Copy)
                    act.activation(krT[0][:, cols], psum[:, 7, KL:KL + P], ACT.Copy).then_inc(latT_hi_ready, 1)

                act.wait_ge(c_in, 16)
                act.wait_ge(c_zero, 1)
                act.activation(c_silu[:, :, 0:1 + NB], c_cols[:], ACT.Silu).then_inc(c_ready, 1)
                squares(0)
                for k in range(4):
                    w_split(k)
                act.wait_ge(shift_raw, 1)
                act.activation(shift_t[:].rearrange("p (a n) -> p a n", a=2), psum[:, 6:8, :], ACT.Copy
                               ).then_inc(tab_ready, 1)
                for k in range(4, 6):
                    w_split(k)
                hT_split(0)
                for k in range(6, KT):
                    w_split(k)
                act.wait_ge(scale_raw, 1)
                act.activation(scale_t[:].rearrange("p (a n) -> p a n", a=2), psum[:, 4:6, :], ACT.Copy
                               ).then_inc(tab_ready, 1)
                squares(1)
                squares(2)
                for slot in range(TT + 2):
                    if 0 <= slot - 1 < TT:
                        post(slot - 1)
                    if 0 <= slot + 1 < TT:
                        hT_split(slot + 1)
                    if 3 <= slot + 2 < TT:
                        squares(slot + 2)
                    if 0 <= slot - 2 < TT:
                        latT_split(slot - 2)

            @block.vector
            def _(dve):
                step = Steps(dve, dve_step)

                def norm(t):
                    if t == 0:
                        dve.wait_ge(stab_ready, 1)
                    if t == 1:
                        dve.wait_ge(tab_ready, 2)

                    def halves(a):
                        return a.rearrange("p (a n) -> p a n", a=2)
                    scale, shift = ((psum[:, 2:4, :], psum[:, 4:6, :]) if t == 0 else
                                    (halves(scale_t[:]), halves(shift_t[:])))
                    dve.wait_ge(rstd_ready, t + 1)
                    if t >= 1:
                        dve.wait_ge(h_ready, t)
                    step.run(dve.scalar_tensor_tensor(halves(xn[:]), halves(x[:, t % 2, :]), rstd[:, t % 2:t % 2 + 1],
                                                      scale, ALU.mult, ALU.mult))
                    if t == 0:
                        dve.wait_ge(stab_ready, 2)
                    if t >= 2:
                        dve.wait_ge(hT_raw, 2 * t - 2)
                    dve.tensor_tensor(halves(h[:, t % 2, :]), halves(xn[:]), shift, ALU.add).then_inc(h_ready, 1)

                def w_split(k):
                    dve.wait_ge(w_hi_ready, k + 1)
                    dve.tensor_tensor(w_lo[:, k:k + 1, :], w_raw(k, 1), f(w_hi[:, k:k + 1, :]), ALU.subtract
                                      ).then_inc(w_ready, 1)

                def hT_split(t):
                    for half in range(2):
                        dve.wait_ge(hT_hi_ready, 2 * t + half + 1)
                        ks = slice(4 * half, 4 * half + 4)
                        dve.tensor_tensor(hT_lo[t % 2][:, ks, :], psum[:, half, :].rearrange("p (k n) -> p k n", k=4),
                                          f(hT_hi[t % 2][:, ks, :]), ALU.subtract).then_inc(hT_ready, 1)

                def post(t):
                    b, s = a_bank(t), t % 2
                    if t == 0:
                        dve.wait_ge(const_in, 16 * N_CONST)
                    dve.wait_ge(r3_ready, t + 1)
                    if t >= 2:
                        dve.wait_ge(latT_raw, t - 1)
                        dve.wait_ge(stored[s], 32 * (t // 2))
                    dve.scalar_tensor_tensor(cq[:, s, :], psum[:, b, 0:QL], r3[:, s, 0:1], gains[:, 0:QL],
                                             ALU.mult, ALU.mult)
                    dve.scalar_tensor_tensor(ckv[:, s, :], psum[:, b + 1, 0:KL], r3[:, s, 1:2],
                                             gains[:, QL:QL + KL], ALU.mult, ALU.mult)
                    step.run(dve.scalar_tensor_tensor(krn[:], psum[:, b + 1, KL:KL + DR], r3[:, s, 2:3],
                                                      gains[:, QL + KL:], ALU.mult, ALU.mult))
                    hr = DR // 2
                    step.then(dve.tensor_tensor(kr_cos[:], krn[:], cos[:, tiles[t], :], ALU.mult))
                    step.then(dve.tensor_tensor(kr_sin[:, 0:hr], krn[:, hr:], sin[:, tiles[t], 0:hr], ALU.mult))
                    step.run(dve.tensor_tensor(kr_sin[:, hr:], krn[:, 0:hr], sin[:, tiles[t], hr:], ALU.mult))
                    for i in range(2):
                        last = dve.tensor_tensor(kr[:, s, i * DR:(i + 1) * DR], kr_cos[:], kr_sin[:], ALU.add)
                    last.then_inc(lat_ready, 1)

                def latT_split(t):
                    cols = slice(tiles[t] * P, (tiles[t] + 1) * P)
                    dve.wait_ge(latT_hi_ready, t + 1)
                    dve.tensor_tensor(cqT[1][:, :, cols], psum[:, 6, 0:QL].rearrange("p (k n) -> p k n", k=QT),
                                      f(cqT[0][:, :, cols]), ALU.subtract)
                    dve.tensor_tensor(ckvT[1][:, :, cols], psum[:, 7, 0:KL].rearrange("p (k n) -> p k n", k=2),
                                      f(ckvT[0][:, :, cols]), ALU.subtract)
                    dve.tensor_tensor(krT[1][:, cols], psum[:, 7, KL:KL + P], f(krT[0][:, cols]),
                                      ALU.subtract).then_inc(latT_ready, 1)

                dve.wait_ge(mod_tab_in, 16)
                dve.wait_ge(mod_w_used, KT)
                mod_finish(dve, Steps(dve, mod_step), mod[:], psum[:, 0, :], mod_tab[:, BIAS, :], mod_tab
                           ).then_inc(mod_ready, 1)
                for k in range(3):
                    w_split(k)
                norm(0)
                for k in range(3, 6):
                    w_split(k)
                hT_split(0)
                for k in range(6, KT):
                    w_split(k)
                norm(1)
                norm(2)
                for slot in range(TT + 2):
                    if 0 <= slot + 1 < TT:
                        hT_split(slot + 1)
                    if 0 <= slot - 1 < TT:
                        post(slot - 1)
                    if 3 <= slot + 2 < TT:
                        norm(slot + 2)
                    if 0 <= slot - 2 < TT:
                        latT_split(slot - 2)

            @block.tensor
            def _(pe):
                def transposes(t):
                    pe.wait_ge(h_ready, t + 1)
                    if t >= 1:
                        pe.wait_ge(hT_ready, 2 * t)
                    for k in range(KT):
                        mm = pe.transpose(psum[:, k // 4, (k % 4) * P:(k % 4 + 1) * P],
                                          h[:, t % 2, k * P:(k + 1) * P], ident[:])
                        if k % 4 == 3:
                            mm.then_inc(hT_raw, 1)

                def product(t):
                    pe.wait_ge(hT_ready, 2 * t + 2)
                    if t >= 2:
                        pe.wait_ge(lat_ready, t - 1)
                    if t == 1:
                        pe.wait_ge(tab_ready, 2)
                    for n, (c0, c1) in enumerate(((0, QL), (QL, A_W))):
                        for k in range(KT):
                            if t == 0 and n == 0:
                                pe.wait_ge(w_ready, k + 1)
                            mm = mm3(pe, psum[:, a_bank(t) + n, 0:c1 - c0],
                                     hT_hi[t % 2][:, k, :], hT_lo[t % 2][:, k, :],
                                     w_hi[:, k, c0:c1], w_lo[:, k, c0:c1], k == 0, k == KT - 1)
                    mm.then_inc(a_ready, 1)

                def latT(t):
                    pe.wait_ge(lat_ready, t + 1)
                    if t >= 1:
                        pe.wait_ge(latT_ready, t)
                    else:
                        pe.wait_ge(tab_ready, 1)
                    for k in range(QT):
                        pe.transpose(psum[:, 6, k * P:(k + 1) * P], cq[:, t % 2, k * P:(k + 1) * P], ident[:])
                    for k in range(2):
                        pe.transpose(psum[:, 7, k * P:(k + 1) * P], ckv[:, t % 2, k * P:(k + 1) * P], ident[:])
                    pe.transpose(psum[:, 7, 2 * P:3 * P], kr[:, t % 2, :], ident[:]).then_inc(latT_raw, 1)

                pe.wait_ge(c_ready, 1)
                for k in range(KT):
                    pe.wait_ge(raw_in[k % RR], 16 * (k // RR + 1))
                    mod_products(pe, psum[:, 0, :], c_silu, raw[:, k % RR:k % RR + 1, :], k, 1, MOD_N,
                                 k == 0, k == KT - 1).then_inc(mod_w_used, 1)
                def table(part, tokens, bank):
                    for half in range(2):
                        mm = pe.matmul(psum[:, bank + half, :], sel[:, tokens, 2 * part + half, :], mod[:],
                                       start=True, stop=True)
                    return mm

                PROMPT, STREAMS = range(2)
                pe.wait_ge(sel_in, 16)
                pe.wait_ge(mod_ready, 1)
                table(SCALE1, STREAMS, 2).then_inc(stab_ready, 1)
                table(SHIFT1, STREAMS, 4).then_inc(stab_ready, 1)
                table(SHIFT1, PROMPT, 6).then_inc(shift_raw, 1)
                transposes(0)
                table(SCALE1, PROMPT, 4).then_inc(scale_raw, 1)
                product(0)
                transposes(1)
                for slot in range(1, TT + 1):
                    if slot + 1 < TT:
                        transposes(slot + 1)
                    if slot < TT:
                        product(slot)
                    if 0 <= slot - 1 < TT:
                        latT(slot - 1)


def project_phase(nc, psum, io, ident, layer, x_from, hT):
    N_TAB = 3
    WR = 6
    tiles = [SAMPLE] + list(range(SAMPLE))
    with Phase(nc, f"proj{layer}") as ph:
        w_hi = ph.sb("w_hi", [P, KT, D], F32R)
        w_lo = ph.sb("w_lo", [P, KT, D], F32R)
        w_raw = ph.sb("w_raw", [P, WR - 3, D])
        m = ph.sb("m", [P, 2, KT, P])
        m_hi = [ph.sb(f"m_hi{i}", [P, KT, P], F32R) for i in range(2)]
        m_lo = [ph.sb(f"m_lo{i}", [P, KT, P], F32R) for i in range(2)]
        gate_t, scale_t, shift_t = ph.sb("gate_t", [P, D]), ph.sb("scale_t", [P, D]), ph.sb("shift_t", [P, D])
        x = ph.sb("x", [P, 2, D])
        upd = ph.sb("upd", [P, D])
        h = ph.sb("h", [P, 2, D])
        ss, ms, rstd = ph.sb("ss", [P, 2]), ph.sb("ms", [P, 2]), ph.sb("rstd", [P, 2])
        power = ph.sb("power", [P, 1])
        junk = psum[:, 6:8, :]
        raw = [w_raw[:, i, :] for i in range(WR - 3)] + [upd[:], h[:, 0, :], h[:, 1, :]]

        raw_in, m_in, x_in = ph.sems("raw_in", WR), ph.sems("m_in", 2), ph.sems("x_in", 2)
        gate_in, tab_in, stab_in = ph.sem("gate_in"), ph.sem("tab_in"), ph.sem("stab_in")
        w_hi_ready, w_ready = ph.sem("w_hi_ready"), ph.sem("w_ready")
        m_hi_ready, m_ready, o_ready = ph.sem("m_hi_ready"), ph.sem("m_ready"), ph.sem("o_ready")
        upd_ready, x_ready, x_stored = ph.sem("upd_ready"), ph.sem("x_ready"), ph.sems("x_stored", 2)
        ss_ready, rstd_ready, xn_ready = ph.sem("ss_ready"), ph.sem("rstd_ready"), ph.sem("xn_ready")
        h_ready, hT_raw = ph.sem("h_ready"), ph.sem("hT_raw")
        hT_hi_ready, hT_ready = ph.sem("hT_hi_ready"), ph.sem("hT_ready")
        const_set, pool_step = ph.sem("const_set"), ph.sem("pool_step")

        def o_bank(t):
            return 2 + 2 * (t % 2)

        def cols(t):
            return slice(tiles[t] * P, (tiles[t] + 1) * P)

        with nc.Block() as block:
            @block.sync
            def _(sp):
                def load_m(t):
                    if t >= 2:
                        sp.wait_ge(m_ready, t - 1)
                    sp.dma_start(m[:, t % 2], io["mixT"].rearrange("k p n -> p k n")[:, :, cols(t)]
                                 ).then_inc(m_in[t % 2], 16)

                def load_x(t):
                    if t >= 2:
                        sp.wait_ge(xn_ready, t - 1)
                        sp.wait_ge(x_stored[t % 2], 16 * (t // 2))
                    sp.dma_start(x[:, t % 2, :], x_from[tiles[t]]).then_inc(x_in[t % 2], 16)

                def store_x(t):
                    sp.wait_ge(x_ready, t + 1)
                    sp.dma_start(io["x_res"][tiles[t]], x[:, t % 2, :]).then_inc(x_stored[t % 2], 16)

                def load_w(k):
                    if k >= WR:
                        sp.wait_ge(w_ready, k - WR + 1)
                    sp.dma_start(raw[k % WR], io[f"w_o{layer}"][k]).then_inc(raw_in[k % WR], 16)

                load_m(0)
                for k in range(KT):
                    load_w(k)
                load_m(1)
                load_x(0)
                load_table(sp, gate_t, io["mod"], layer, GATE1, SAMPLE, stab_in)
                load_table(sp, scale_t, io["mod"], layer, SCALE2, SAMPLE, stab_in)
                load_table(sp, shift_t, io["mod"], layer, SHIFT2, SAMPLE, stab_in)
                load_x(1)
                load_m(2)
                for t in range(TT):
                    if t + 3 < TT:
                        load_m(t + 3)
                    if t == 0:
                        sp.wait_ge(upd_ready, 1)
                        load_table(sp, gate_t, io["mod"], layer, GATE1, 0, gate_in)
                        sp.wait_ge(h_ready, 1)
                        load_table(sp, scale_t, io["mod"], layer, SCALE2, 0, tab_in)
                        load_table(sp, shift_t, io["mod"], layer, SHIFT2, 0, tab_in)
                    store_x(t)
                    if t + 2 < TT:
                        load_x(t + 2)
                sp.wait_ge(x_stored[0], 16 * ((TT + 1) // 2))
                sp.wait_ge(x_stored[1], 16 * (TT // 2))

            @block.scalar
            def _(act):
                def w_split(k):
                    act.wait_ge(raw_in[k % WR], 16 * (k // WR + 1))
                    act.activation(w_hi[:, k, :], raw[k % WR], ACT.Copy).then_inc(w_hi_ready, 1)

                def m_split(t):
                    act.wait_ge(m_in[t % 2], 16 * (t // 2 + 1))
                    if t >= 2:
                        act.wait_ge(o_ready, t - 1)
                    act.activation(m_hi[t % 2][:], m[:, t % 2], ACT.Copy).then_inc(m_hi_ready, 1)

                def squares(t):
                    act.wait_ge(x_ready, t + 1)
                    if t >= 2:
                        act.wait_ge(rstd_ready, t - 1)
                    if t >= 1:
                        act.wait_ge(ss_ready, t)
                    act.activation(junk, x[:, t % 2, :].rearrange("p (a n) -> p a n", a=2), ACT.Square,
                                   accum_out=ss[:, t % 2:t % 2 + 1]).then_inc(ss_ready, 1)

                def hT_split(t):
                    for half in range(2):
                        act.wait_ge(hT_raw, 2 * t + half + 1)
                        act.activation(hT[0][:, 4 * half:4 * half + 4, cols(t)],
                                       psum[:, half, :].rearrange("p (k n) -> p k n", k=4),
                                       ACT.Copy).then_inc(hT_hi_ready, 1)

                m_split(0)
                for k in range(KT):
                    w_split(k)
                for slot in range(TT + 2):
                    if slot + 1 < TT:
                        m_split(slot + 1)
                    if 0 <= slot - 1 < TT:
                        squares(slot - 1)
                    if 0 <= slot - 2 < TT:
                        hT_split(slot - 2)

            @block.gpsimd
            def _(pool):
                step = Steps(pool, pool_step)
                pool.memset(power[:], -0.5).then_inc(const_set, 1)
                pool.wait_ge(const_set, 1)
                for t in range(TT):
                    c = slice(t % 2, t % 2 + 1)
                    pool.wait_ge(ss_ready, t + 1)
                    step.run(pool.tensor_scalar(ms[:, c], ss[:, c], 1.0 / D, EPS, ALU.mult, ALU.add))
                    if t >= 2:
                        pool.wait_ge(xn_ready, t - 1)
                    pool.tensor_tensor(rstd[:, c], ms[:, c], power[:], ALU.pow).then_inc(rstd_ready, 1)

            @block.vector
            def _(dve):
                def w_split(k):
                    dve.wait_ge(w_hi_ready, k + 1)
                    dve.tensor_tensor(w_lo[:, k, :], raw[k % WR], f(w_hi[:, k, :]), ALU.subtract
                                      ).then_inc(w_ready, 1)

                def m_split(t):
                    dve.wait_ge(m_hi_ready, t + 1)
                    dve.tensor_tensor(m_lo[t % 2][:], m[:, t % 2], f(m_hi[t % 2][:]), ALU.subtract).then_inc(m_ready, 1)

                def update(t):
                    if t == 0:
                        dve.wait_ge(stab_in, 16 * N_TAB * NB)
                    if t == 1:
                        dve.wait_ge(gate_in, 16)
                    dve.wait_ge(o_ready, t + 1)
                    dve.tensor_tensor(upd[:].rearrange("p (a n) -> p a n", a=2), psum[:, o_bank(t):o_bank(t) + 2, :],
                                      gate_t[:].rearrange("p (a n) -> p a n", a=2), ALU.mult).then_inc(upd_ready, 1)
                    dve.wait_ge(upd_ready, t + 1)
                    dve.wait_ge(x_in[t % 2], 16 * (t // 2 + 1))
                    dve.tensor_tensor(x[:, t % 2, :], x[:, t % 2, :], upd[:], ALU.add).then_inc(x_ready, 1)

                def norm(t):
                    dve.wait_ge(rstd_ready, t + 1)
                    if t == 1:
                        dve.wait_ge(tab_in, 32)
                    if t >= 2:
                        dve.wait_ge(hT_raw, 2 * t - 2)
                    dve.scalar_tensor_tensor(h[:, t % 2, :], x[:, t % 2, :], rstd[:, t % 2:t % 2 + 1], scale_t[:],
                                             ALU.mult, ALU.mult).then_inc(xn_ready, 1)
                    dve.wait_ge(xn_ready, t + 1)
                    dve.tensor_tensor(h[:, t % 2, :], h[:, t % 2, :], shift_t[:], ALU.add).then_inc(h_ready, 1)

                def hT_split(t):
                    for half in range(2):
                        dve.wait_ge(hT_hi_ready, 2 * t + half + 1)
                        part = (slice(None), slice(4 * half, 4 * half + 4), cols(t))
                        dve.tensor_tensor(hT[1][part], psum[:, half, :].rearrange("p (k n) -> p k n", k=4),
                                          f(hT[0][part]), ALU.subtract).then_inc(hT_ready, 1)

                m_split(0)
                for k in range(KT):
                    w_split(k)
                for slot in range(TT + 2):
                    if 0 <= slot - 1 < TT:
                        update(slot - 1)
                    if slot + 1 < TT:
                        m_split(slot + 1)
                    if 0 <= slot - 1 < TT:
                        norm(slot - 1)
                    if 0 <= slot - 2 < TT:
                        hT_split(slot - 2)

            @block.tensor
            def _(pe):
                def product(t):
                    pe.wait_ge(m_ready, t + 1)
                    if t >= 2:
                        pe.wait_ge(upd_ready, t - 1)
                    for half in range(2):
                        for k in range(KT):
                            if t == 0 and half == 0:
                                pe.wait_ge(w_ready, k + 1)
                            half_cols = slice(half * 512, half * 512 + 512)
                            mm = mm3(pe, psum[:, o_bank(t) + half, :], m_hi[t % 2][:, k, :], m_lo[t % 2][:, k, :],
                                     w_hi[:, k, half_cols], w_lo[:, k, half_cols], k == 0, k == KT - 1)
                    mm.then_inc(o_ready, 1)

                def transposes(t):
                    pe.wait_ge(h_ready, t + 1)
                    if t >= 1:
                        pe.wait_ge(hT_ready, 2 * t)
                    for k in range(KT):
                        mm = pe.transpose(psum[:, k // 4, (k % 4) * P:(k % 4 + 1) * P],
                                          h[:, t % 2, k * P:(k + 1) * P], ident[:])
                        if k % 4 == 3:
                            mm.then_inc(hT_raw, 1)

                for slot in range(TT + 2):
                    if 0 <= slot - 2 < TT:
                        transposes(slot - 2)
                    if slot < TT:
                        product(slot)


def ffn_phase(nc, psum, io, layer, hT, x_to, c_silu):
    SF = 2
    SLABS = FT // SF
    GT = 3
    GN = NTOK // GT
    U = SF * GT
    V = 2 * TT
    H_BANKS, F_BANKS, UPDS = 2, 3, 3
    with Phase(nc, f"ffn{layer}") as ph:
        x = ph.sb("x", [P, TT, D])
        gate_t = ph.sb("gate_t", [P, 2, D])
        raw = ph.sb("raw", [P, 2 * SF, D])
        w1_hi = [ph.sb(f"w1_hi{i}", [P, KT, P], F32R) for i in range(SF)]
        w1_lo = [ph.sb(f"w1_lo{i}", [P, KT, P], F32R) for i in range(SF)]
        w2_hi = [ph.sb(f"w2_hi{i}", [P, D], F32R) for i in range(SF)]
        w2_lo = [ph.sb(f"w2_lo{i}", [P, D], F32R) for i in range(SF)]
        relu = ph.sb("relu", [P, 2, GN])
        sq = ph.sb("sq", [P, 2, GN])
        s_hi = ph.sb("s_hi", [P, SF, NTOK], F32R)
        s_lo = ph.sb("s_lo", [P, SF, NTOK], F32R)
        upd = ph.sb("upd", [P, UPDS, 512])
        makes_mod = layer == 0
        if makes_mod:
            mod_w = ph.sb("mod_w", [P, HK, 4 * FFN_N])
            mod_tab, mod = ph.sb("mod_tab", [P, 3, FFN_N]), ph.sb("mod", [P, FFN_N])
            mod_psum = psum[:, H_BANKS + F_BANKS, 0:FFN_N]
            assert FFN_STEPS == SLABS

        raw_in = ph.sems("raw_in", 2 * SF)
        x_in, tab_in = ph.sem("x_in"), ph.sem("tab_in")
        w1_hi_ready, w1_ready = ph.sem("w1_hi_ready"), ph.sem("w1_ready")
        w2_hi_ready, w2_ready = ph.sem("w2_hi_ready"), ph.sem("w2_ready")
        hid_ready = ph.sem("hid_ready")
        relu_ready = ph.sem("relu_ready")
        sq_ready = ph.sem("sq_ready")
        s_hi_ready = ph.sem("s_hi_ready")
        s_ready = ph.sem("s_ready")
        f_ready = ph.sem("f_ready")
        upd_ready = ph.sem("upd_ready")
        added = ph.sem("added")
        stored = ph.sem("stored")
        mod_w_in, mod_tab_in, mod_w_used = ph.sem("mod_w_in"), ph.sem("mod_tab_in"), ph.sem("mod_w_used")
        mod_ready = ph.sem("mod_ready")
        mod_stored = ph.sem("mod_stored")
        mod_step = ph.sem("mod_step")

        with nc.Block() as block:
            @block.sync
            def _(sp):
                def load_w1(s, i):
                    sp.dma_start(raw[:, i, :].rearrange("p (k n) -> p k n", k=KT), io["w1"][layer, s * SF + i]
                                 ).then_inc(raw_in[i], 16)

                def load_w2(s, i):
                    sp.dma_start(raw[:, SF + i, :], io["w2"][layer, s * SF + i]).then_inc(raw_in[SF + i], 16)

                for i in range(SF):
                    load_w1(0, i)
                for i in range(SF):
                    load_w2(0, i)
                load_table(sp, gate_t[:, 0, :], io["mod"], layer, GATE2, 0, tab_in)
                load_table(sp, gate_t[:, 1, :], io["mod"], layer, GATE2, SAMPLE, tab_in)
                sp.dma_start(x[:], io["x_res"].rearrange("t p n -> p t n")).then_inc(x_in, 16)

                def load_mod_w(s, half):
                    sp.dma_start(mod_w[:], io["ada_w_ffn"][s, half]).then_inc(mod_w_in, 16)

                def load_mod_tab(s):
                    sp.dma_start(mod_tab[:], mod_tables(io["ada_tab_ffn"][s], FFN_N)).then_inc(mod_tab_in, 16)

                def second_mod_w(s):
                    sp.wait_ge(mod_w_used, s * 2 + 1)
                    load_mod_w(s, 1)

                def store_mod(s):
                    sp.wait_ge(mod_ready, s + 2)
                    mod_store(sp, io, layer + 1, FFN_N, s, mod, mod_stored)

                if makes_mod:
                    sp.sem_inc(mod_stored, 64)
                    load_mod_w(0, 0)
                    load_mod_tab(0)
                with sp.Fori(0, SLABS - 1) as s:
                    for i in range(SF):
                        sp.wait_ge(w1_ready, s * SF + (i + 1))
                        load_w1(s + 1, i)
                    for i in range(SF):
                        sp.wait_ge(w2_ready, s * SF + (i + 1))
                        load_w2(s + 1, i)
                    if makes_mod:
                        second_mod_w(s)
                        sp.wait_ge(mod_w_used, s * 2 + 2)
                        load_mod_w(s + 1, 0)
                        store_mod(s)
                        load_mod_tab(s + 1)
                if makes_mod:
                    second_mod_w(SLABS - 1)
                for t in range(TT):
                    if makes_mod and t == TT - 2:
                        store_mod(SLABS - 1)
                    sp.wait_ge(added, V * SLABS + 2 * (t + 1))
                    sp.dma_start(x_to[t], x[:, t, :]).then_inc(stored, 16)
                if makes_mod:
                    sp.wait_ge(mod_stored, 64 + 64 * SLABS)
                sp.wait_ge(stored, 16 * TT)

            @block.scalar
            def _(act):
                def split_w1(s, i):
                    act.wait_ge(raw_in[i], s * 16 + 16)
                    act.activation(w1_hi[i][:], raw[:, i, :].rearrange("p (k n) -> p k n", k=KT),
                                   ACT.Copy).then_inc(w1_hi_ready, 1)

                def slab(s, last):
                    act.wait_ge(f_ready, s * V + 1)
                    for i in range(SF):
                        act.wait_ge(raw_in[SF + i], s * 16 + 16)
                        act.activation(w2_hi[i][:], raw[:, SF + i, :], ACT.Copy).then_inc(w2_hi_ready, 1)

                    def square_hi(u):
                        act.wait_ge(sq_ready, s * U + (2 + u + 1))
                        act.activation(s_hi[:, u // GT, (u % GT) * GN:(u % GT + 1) * GN], sq[:, u % 2, :],
                                       ACT.Copy).then_inc(s_hi_ready, 1)

                    for u in range(U):
                        act.wait_ge(hid_ready, s * U + (u + 1))
                        act.wait_ge(sq_ready, s * U + (u + 1))
                        act.activation(relu[:, u % 2, :], psum[:, u % H_BANKS, 0:GN], ACT.Relu
                                       ).then_inc(relu_ready, 1)
                        if u >= 1:
                            square_hi(u - 1)
                    square_hi(U - 1)
                    if not last:
                        for i in range(SF):
                            act.wait_ge(hid_ready, s * U + GT * (i + 1))
                            split_w1(s + 1, i)

                act.sem_inc(relu_ready, H_BANKS)
                for i in range(SF):
                    split_w1(0, i)
                with act.Fori(0, SLABS - 1) as s:
                    slab(s, False)
                slab(SLABS - 1, True)

            @block.vector
            def _(dve):
                def split_w1(s, i):
                    dve.wait_ge(w1_hi_ready, s * SF + (i + 1))
                    dve.tensor_tensor(w1_lo[i][:], raw[:, i, :].rearrange("p (k n) -> p k n", k=KT),
                                      f(w1_hi[i][:]), ALU.subtract).then_inc(w1_ready, 1)

                def slab(s, last):
                    for i in range(SF):
                        dve.wait_ge(w2_hi_ready, s * SF + (i + 1))
                        dve.tensor_tensor(w2_lo[i][:], raw[:, SF + i, :], f(w2_hi[i][:]), ALU.subtract
                                          ).then_inc(w2_ready, 1)

                    def square_lo(u):
                        dve.wait_ge(s_hi_ready, s * U + (u + 1))
                        part = (slice(None), u // GT, slice((u % GT) * GN, (u % GT + 1) * GN))
                        dve.tensor_tensor(s_lo[part], sq[:, u % 2, :], f(s_hi[part]), ALU.subtract
                                          ).then_inc(s_ready, 1)

                    for u in range(U):
                        dve.wait_ge(relu_ready, s * U + (H_BANKS + u + 1))
                        dve.wait_ge(s_ready, s * U + (u + 1))
                        dve.tensor_tensor(sq[:, u % 2, :], relu[:, u % 2, :], relu[:, u % 2, :], ALU.mult
                                          ).then_inc(sq_ready, 1)
                        if u >= 1:
                            square_lo(u - 1)
                    square_lo(U - 1)
                    for v in range(V):
                        t, half = v // 2, v % 2
                        dve.wait_ge(f_ready, s * V + (1 + v + 1))
                        dve.wait_ge(added, s * V + (V + v + 1 - UPDS))
                        dve.tensor_tensor(upd[:, v % UPDS, :], psum[:, H_BANKS + v % F_BANKS, :],
                                          gate_t[:, int(t == SAMPLE), half * 512:half * 512 + 512], ALU.mult
                                          ).then_inc(upd_ready, 1)
                        if not last and v in (2, 5):
                            split_w1(s + 1, (v - 2) // 3)
                        if makes_mod and v == 14:
                            step = Steps(dve, mod_step)
                            step.base = s * 2
                            dve.wait_ge(mod_w_used, s * 2 + 2)
                            dve.wait_ge(mod_tab_in, s * 16 + 16)
                            dve.wait_ge(mod_stored, s * 64 + 64)
                            mod_finish(dve, step, mod[:], mod_psum, mod_tab[:, BIAS, :], mod_tab).then_inc(mod_ready, 1)

                dve.sem_inc(sq_ready, 2)
                dve.sem_inc(s_ready, 2)
                dve.sem_inc(upd_ready, F_BANKS)
                if makes_mod:
                    dve.sem_inc(mod_ready, 1)
                for i in range(SF):
                    split_w1(0, i)
                dve.wait_ge(tab_in, 16 * (1 + NB))
                with dve.Fori(0, SLABS - 1) as s:
                    slab(s, False)
                slab(SLABS - 1, True)

            @block.gpsimd
            def _(pool):
                pool.sem_inc(added, V)
                pool.wait_ge(x_in, 16)
                with pool.Fori(0, SLABS) as s:
                    for v in range(V):
                        part = x[:, v // 2, (v % 2) * 512:(v % 2) * 512 + 512]
                        pool.wait_ge(upd_ready, s * V + (F_BANKS + v + 1))
                        pool.wait_ge(added, s * V + (v + 1))
                        pool.tensor_tensor(part, part, upd[:, v % UPDS, :], ALU.add).then_inc(added, 1)

            @block.tensor
            def _(pe):
                def mod_half(s, half):
                    pe.wait_ge(mod_w_in, s * 32 + 16 * (half + 1))
                    if half == 0:
                        pe.wait_ge(mod_ready, s + 1)
                    mod_products(pe, mod_psum, c_silu, mod_w, half * HK, HK, FFN_N, half == 0, half == 1
                                 ).then_inc(mod_w_used, 1)

                def slab(s):
                    for u in range(U):
                        i, g = u // GT, u % GT
                        pe.wait_ge(w1_ready, s * SF + (i + 1))
                        pe.wait_ge(relu_ready, s * U + (u + 1))
                        for k in range(KT):
                            mm = mm3(pe, psum[:, u % H_BANKS, 0:GN], w1_hi[i][:, k, :], w1_lo[i][:, k, :],
                                     hT[0][:, k, g * GN:(g + 1) * GN], hT[1][:, k, g * GN:(g + 1) * GN],
                                     k == 0, k == KT - 1)
                        mm.then_inc(hid_ready, 1)
                    for v in range(V):
                        if makes_mod and v in (2, 12):
                            mod_half(s, int(v == 12))
                        t, half = v // 2, v % 2
                        pe.wait_ge(s_ready, s * U + (2 + U - GT + t // GT + 1))
                        pe.wait_ge(w2_ready, s * SF + SF)
                        pe.wait_ge(upd_ready, s * V + (v + 1))
                        for i in range(SF):
                            toks, cols = slice(t * P, (t + 1) * P), slice(half * 512, half * 512 + 512)
                            mm = mm3(pe, psum[:, H_BANKS + v % F_BANKS, :], s_hi[:, i, toks], s_lo[:, i, toks],
                                     w2_hi[i][:, cols], w2_lo[i][:, cols], i == 0, i == SF - 1)
                        mm.then_inc(f_ready, 1)

                pe.sem_inc(f_ready, 1)
                with pe.Fori(0, SLABS) as s:
                    slab(s)


def prompt_attention_phase(nc, psum, io, ident, c_silu, cqT, ckvT, krT):
    PAIRS = H // 2
    QT = QL // P
    T = SEQ // P
    GR = T // 2
    N = 2 * 2 * GR
    GN = 2 * GR
    QW = 2 * (DN + DR)
    SPLIT = (13, 14)

    def unit(n):
        return n // (2 * GR), n // 2 % GR, n % 2

    def key_tiles(n):
        return 2 * unit(n)[1] + 2

    chunks = [[(k, min(k + 4, key_tiles(n))) for k in range(0, key_tiles(n), 4)] for n in range(N)]
    before = [sum(len(c) for c in chunks[:n]) for n in range(N + 1)]
    C = before[N]
    assert C % 2 == 0

    with Phase(nc, "patt") as ph:
        q_raw, kv_raw = ph.sb("q_raw", [P, QT, QW]), ph.sb("kv_raw", [P, 2, 512])
        wq_hi, wq_lo = ph.sb("wq_hi", [P, QT, QW], F32R), ph.sb("wq_lo", [P, QT, QW], F32R)
        wkv_hi, wkv_lo = ph.sb("wkv_hi", [P, 2, 512], F32R), ph.sb("wkv_lo", [P, 2, 512], F32R)
        g_qn, g_qr, g_kn = ph.sb("g_qn", [P, DN]), ph.sb("g_qr", [P, DR]), ph.sb("g_kn", [P, DN])
        gg = ph.sb("gg", [P, DN])
        cos, sin = ph.sb("cos", [P, TT, DR]), ph.sb("sin", [P, TT, DR])
        ident_bf, mask = ph.sb("ident_bf", [P, P], BF16), ph.sb("mask", [P, 2, 2 * P], BF16)
        junk = ph.sb("junk", [P, QW + 2 * DN])
        inv_n, eps, power = ph.sb("inv_n", [P, 6]), ph.sb("eps", [P, 6]), ph.sb("power", [P, 6])
        ss, ms, rs = ph.sb("ss", [P, 2, 6]), ph.sb("ms", [P, 2, 6]), ph.sb("rs", [P, 2, 6])
        q_tok = ph.sb("q_tok", [P, 2, 4, P])
        k_tok = ph.sb("k_tok", [P, 2, 2, DN])
        qr, qr_cos, qr_sin = ph.sb("qr", [P, 2, DR]), ph.sb("qr_cos", [P, 2, DR]), ph.sb("qr_sin", [P, 2, DR])
        qT_hi = ph.sb("qT_hi", [P, 4, SEQ], F32R)
        qT_lo = ph.sb("qT_lo", [P, 2, SEQ], F32R)
        kT_hi, kT_lo = ph.sb("kT_hi", [P, 2, SEQ], F32R), ph.sb("kT_lo", [P, 2, SEQ], F32R)
        v_hi, v_lo = ph.sb("v_hi", [P, T, 2 * DN], F32R), ph.sb("v_lo", [P, T, 2 * DN], F32R)
        mx, neg, total, inv = (ph.sb(n, [P, 2]) for n in ("mx", "neg", "total", "inv"))
        pr = ph.sb("pr", [P, 2, SEQ])
        pT_hi = [ph.sb(f"pT_hi{i}", [P, T, 2 * P], F32R) for i in range(2)]
        pT_lo = [ph.sb(f"pT_lo{i}", [P, T, 2 * P], F32R) for i in range(2)]
        o = ph.sb("o", [P, 2, 2 * P])
        mod_w = ph.sb("mod_w", [P, HK, 4 * ATT_N])
        mod_tab, mod = ph.sb("mod_tab", [P, 3, ATT_N]), ph.sb("mod", [P, ATT_N])
        mod_psum = psum[:, 7, 3 * P:]
        assert ATT_STEPS == 2 * PAIRS and T == 8 and ATT_N == P

        const_in, const_set = ph.sem("const_in"), ph.sem("const_set")
        raw_in = ph.sem("raw_in")
        w_hi_ready, w_ready = ph.sem("w_hi_ready"), ph.sem("w_ready")
        proj_ready = ph.sem("proj_ready")
        ss_ready = ph.sem("ss_ready")
        r_ready = ph.sem("r_ready")
        tok_ready = ph.sem("tok_ready")
        ktok_ready = ph.sem("ktok_ready")
        tokT_raw = ph.sem("tokT_raw")
        tokT_hi_ready = ph.sem("tokT_hi_ready")
        tokT_ready = ph.sem("tokT_ready")
        s_ready = ph.sem("s_ready")
        max_ready = ph.sem("max_ready")
        exp_ready = ph.sem("exp_ready")
        pr_ready = ph.sem("pr_ready")
        pT_raw = ph.sem("pT_raw")
        pT_hi_ready = ph.sem("pT_hi_ready")
        pT_ready = ph.sem("pT_ready")
        pv_ready = ph.sem("pv_ready")
        o_ready = ph.sem("o_ready")
        stored = ph.sems("stored", 2)
        gg_ready = ph.sem("gg_ready")
        mod_w_in, mod_tab_in = ph.sem("mod_w_in"), ph.sem("mod_tab_in")
        mod_w_used = ph.sem("mod_w_used")
        mod_ready = ph.sem("mod_ready")
        mod_stored = ph.sem("mod_stored")
        dve_step, pool_step = ph.sem("dve_step"), ph.sem("pool_step")

        def flat(bank, width):
            return psum[:, bank:bank + 2, :].rearrange("p a n -> p (a n)")[:, 0:width]

        with nc.Block() as block:
            @block.sync
            def _(sp):
                for i in range(2):
                    sp.sem_inc(stored[i], 16)
                for dst, src in ((g_qn, "g_qn"), (g_qr, "g_qr"), (g_kn, "g_kn")):
                    sp.dma_start(dst[:], io[src].partition_broadcast(P)).then_inc(const_in, 16)
                for dst, src in ((cos, "cos"), (sin, "sin"), (ident_bf, "ident_bf"), (mask, "mask")):
                    sp.dma_start(dst[:], io[src]).then_inc(const_in, 16)

                def load_mod_w(p, i):
                    sp.wait_ge(mod_w_used, p * 4 + (i + 1))
                    sp.dma_start(mod_w[:], io["ada_w_att"][p * 2 + i // 2, i % 2]).then_inc(mod_w_in, 16)

                def load_mod_tab(p, n):
                    sp.wait_ge(mod_ready, p * 2 + (n + 1))
                    sp.dma_start(mod_tab[:], mod_tables(io["ada_tab_att"][p * 2 + n], ATT_N)).then_inc(mod_tab_in, 16)

                def store_mod(p, n):
                    sp.wait_ge(mod_ready, p * 2 + (1 + n + 1))
                    mod_store(sp, io, 0, ATT_N, p * 2 + (FRONT // (4 * ATT_N) + n), mod, mod_stored)

                sp.sem_inc(mod_stored, 64)
                with sp.Fori(0, PAIRS) as p:
                    load_mod_w(p, 0)
                    load_mod_tab(p, 0)
                    load_mod_w(p, 1)
                    load_mod_w(p, 2)
                    store_mod(p, 0)
                    load_mod_tab(p, 1)
                    load_mod_w(p, 3)
                    store_mod(p, 1)
                    for g in range(GN):
                        j, grp = g // GR, g % GR
                        sp.wait_ge(o_ready, p * GN + (2 + g + 1))
                        sp.dma_start(io["mixT"][p * 2 + j, :, 2 * P * grp:2 * P * (grp + 1)], o[:, g % 2, :]
                                     ).then_inc(stored[g % 2], 16)
                for i in range(2):
                    sp.wait_ge(stored[i], 16 + 16 * PAIRS * GN // 2)
                sp.wait_ge(mod_stored, 64 + 64 * ATT_STEPS)

            @block.gpsimd
            def _(pool):
                def load(p):
                    pool.dma_start(q_raw[:], io["w_q_pair"][p]).then_inc(raw_in, 16)
                    pool.dma_start(kv_raw[:], io["w_kv_pair"][p]).then_inc(raw_in, 16)

                def pair(p, step):
                    for t in range(T):
                        s = t % 2
                        pool.wait_ge(ss_ready, p * T + (1 + t + 1))
                        step.run(pool.tensor_tensor(ms[:, s, :], ss[:, s, :], inv_n[:], ALU.mult))
                        step.run(pool.tensor_tensor(ms[:, s, :], ms[:, s, :], eps[:], ALU.add))
                        pool.wait_ge(tok_ready, p * T + (t + 2))
                        pool.tensor_tensor(rs[:, s, :], ms[:, s, :], power[:], ALU.pow).then_inc(r_ready, 1)

                load(0)
                pool.sem_inc(r_ready, 2)
                pool.memset(inv_n[:, 0:2], 1.0 / DN)
                pool.memset(inv_n[:, 2:4], 1.0 / DR)
                pool.memset(inv_n[:, 4:6], 1.0 / DN)
                pool.memset(eps[:], EPS)
                pool.memset(power[:], -0.5).then_inc(const_set, 1)
                pool.wait_ge(const_set, 1)
                step = Steps(pool, pool_step)
                with pool.Fori(0, PAIRS - 1) as p:
                    step.n, step.base = 0, p * (2 * T)
                    pool.wait_ge(w_ready, p * 2 + 2)
                    load(p + 1)
                    pair(p, step)
                step.n, step.base = 0, (PAIRS - 1) * 2 * T
                pair(PAIRS - 1, step)

            @block.scalar
            def _(act):
                def tile(p, t):
                    b, s = 2 * (t % 3), t % 2
                    act.wait_ge(proj_ready, p * T + (1 + t + 1))
                    act.wait_ge(r_ready, p * T + (t + 1))
                    act.wait_ge(ss_ready, p * T + (t + 1))
                    q, kv = psum[:, b, :], psum[:, b + 1, :]
                    HW = DN + DR
                    act.activation(v_hi[:, t, :], kv[:, 2 * DN:], ACT.Copy)
                    for n, (src, c) in enumerate((
                            (q[:, 0:DN], 0), (q[:, HW:HW + DN], HW), (q[:, DN:HW], DN), (q[:, HW + DN:2 * HW], HW + DN),
                            (kv[:, 0:DN], QW), (kv[:, DN:2 * DN], QW + DN))):
                        last = act.activation(junk[:, c:c + src.shape[1]], src, ACT.Square, accum_out=ss[:, s, n:n + 1])
                    last.then_inc(ss_ready, 1)

                def keys(p, t):
                    b, s = 2 * (t % 3), t % 2
                    act.wait_ge(r_ready, p * T + (2 + t + 1))
                    act.wait_ge(tokT_raw, p * T + (t + 1))
                    for j in range(2):
                        last = act.activation(k_tok[:, s, j, :], psum[:, b + 1, j * DN:(j + 1) * DN], ACT.Copy,
                                              scale=rs[:, s, 4 + j:5 + j])
                    last.then_inc(ktok_ready, 1)

                def tileT(p, t):
                    b, toks = 6, slice(t * P, (t + 1) * P)
                    act.wait_ge(tokT_raw, p * T + (2 + t + 1))
                    act.activation(qT_hi[:, :, toks], psum[:, b, :].rearrange("p (k n) -> p k n", k=4), ACT.Copy)
                    act.activation(kT_hi[:, :, toks], psum[:, b + 1, 0:2 * P].rearrange("p (k n) -> p k n", k=2),
                                   ACT.Copy).then_inc(tokT_hi_ready, 1)

                def exps(p, n):
                    s, width = n % 2, key_tiles(n) * P
                    act.wait_ge(max_ready, p * N + (n + 1))
                    act.wait_ge(pT_raw, p * C + (1 + before[max(n - 1, 0)]))
                    act.activation(pr[:, s, 0:width], flat(2 * s, width), ACT.Exp, bias=neg[:, s:s + 1], scale=SCALE,
                                   accum_out=total[:, s:s + 1]).then_inc(exp_ready, 1)

                def probsT(p, n):
                    g, i = n // 2, n % 2
                    for c, (k0, k1) in enumerate(chunks[n]):
                        m = before[n] + c
                        act.wait_ge(pT_raw, p * C + (1 + m + 1))
                        act.wait_ge(pv_ready, p * GN + (g + 1))
                        act.activation(pT_hi[g % 2][:, k0:k1, i * P:(i + 1) * P],
                                       psum[:, 4 + m % 2, 0:(k1 - k0) * P].rearrange("p (k n) -> p k n", n=P),
                                       ACT.Copy).then_inc(pT_hi_ready, 1)

                def out(p, g):
                    act.wait_ge(pv_ready, p * GN + (2 + g + 1))
                    act.wait_ge(stored[g % 2], p * (16 * GN // 2) + 16 * (g // 2 + 1))
                    act.activation(o[:, g % 2, :], psum[:, 6 + g % 2, 0:2 * P], ACT.Copy).then_inc(o_ready, 1)

                def w_split(p, i):
                    hi, raw = ((wq_hi, q_raw), (wkv_hi, kv_raw))[i]
                    act.wait_ge(raw_in, p * 32 + 32)
                    act.wait_ge(proj_ready, p * T + 1)
                    act.activation(hi[:], raw[:], ACT.Copy).then_inc(w_hi_ready, 1)

                def pair(p, last):
                    for t in range(T + 1):
                        if t < T:
                            tile(p, t)
                        if t >= 1:
                            keys(p, t - 1)
                        if t >= 2:
                            tileT(p, t - 2)
                    exps(p, 0)
                    tileT(p, T - 1)
                    for n in range(1, N + 1):
                        if n < N:
                            exps(p, n)
                        probsT(p, n - 1)
                        if n >= 4 and n % 2 == 0:
                            out(p, n // 2 - 2)
                        if n in SPLIT and not last:
                            w_split(p + 1, SPLIT.index(n))
                    out(p, GN - 1)

                act.sem_inc(ss_ready, 1)
                act.sem_inc(exp_ready, 2)
                act.sem_inc(o_ready, 2)
                for i in range(2):
                    w_split(0, i)
                with act.Fori(0, PAIRS - 1) as p:
                    pair(p, False)
                pair(PAIRS - 1, True)

            @block.vector
            def _(dve):
                def tile(p, t, step):
                    b, s, HW, hr = 2 * (t % 3), t % 2, DN + DR, DR // 2
                    dve.wait_ge(r_ready, p * T + (2 + t + 1))
                    dve.wait_ge(tokT_raw, p * T + (t + 1))
                    for j in range(2):
                        q = psum[:, b, j * HW:(j + 1) * HW]
                        dve.scalar_tensor_tensor(qr[:, j, :], q[:, DN:], rs[:, s, 2 + j:3 + j], g_qr[:],
                                                 ALU.mult, ALU.mult)
                        last = dve.scalar_tensor_tensor(q_tok[:, s, j, :], q[:, 0:DN], rs[:, s, j:j + 1], gg[:],
                                                        ALU.mult, ALU.mult)
                    step.run(last)
                    cos_t = cos[:, t, :].unsqueeze(1).to_broadcast([P, 2, DR])
                    sin_t = sin[:, t, :].unsqueeze(1).to_broadcast([P, 2, DR])
                    dve.tensor_tensor(qr_cos[:], qr[:], cos_t, ALU.mult)
                    dve.tensor_tensor(qr_sin[:, :, 0:hr], qr[:, :, hr:], sin_t[:, :, 0:hr], ALU.mult)
                    step.run(dve.tensor_tensor(qr_sin[:, :, hr:], qr[:, :, 0:hr], sin_t[:, :, hr:], ALU.mult))
                    for i in range(2):
                        dve.tensor_tensor(q_tok[:, s, 2:4, i * DR:(i + 1) * DR], qr_cos[:], qr_sin[:], ALU.add)
                    dve.wait_ge(ktok_ready, p * T + (t + 1))
                    dve.tensor_tensor(v_lo[:, t, :], psum[:, b + 1, 2 * DN:], f(v_hi[:, t, :]), ALU.subtract
                                      ).then_inc(tok_ready, 1)

                def tileT(p, t, step):
                    b, toks = 6, slice(t * P, (t + 1) * P)
                    dve.wait_ge(tokT_hi_ready, p * T + (t + 1))
                    if t % 4 == 1:
                        dve.wait_ge(mod_tab_in, p * 32 + 16 * (t // 4 + 1))
                        dve.wait_ge(mod_stored, p * 128 + 64 * (t // 4 + 1))
                        step.run(dve.tensor_tensor(mod[:], mod_psum, mod_tab[:, BIAS, :], ALU.add))
                    if t % 4 == 3:
                        mod_finish(dve, step, mod[:], mod_psum, mod[:], mod_tab).then_inc(mod_ready, 1)
                    q = psum[:, b, :].rearrange("p (k n) -> p k n", k=4)
                    dve.tensor_tensor(qT_lo[:, :, toks], q[:, 0:2, :], f(qT_hi[:, 0:2, toks]), ALU.subtract)
                    dve.tensor_tensor(qT_hi[DR:, 2:4, toks], q[DR:, 2:4, :], f(qT_hi[DR:, 2:4, toks]), ALU.subtract)
                    dve.tensor_tensor(kT_lo[:, :, toks], psum[:, b + 1, 0:2 * P].rearrange("p (k n) -> p k n", k=2),
                                      f(kT_hi[:, :, toks]), ALU.subtract).then_inc(tokT_ready, 1)

                def maxes(p, n, step):
                    s, width = n % 2, key_tiles(n) * P
                    dve.wait_ge(s_ready, p * N + (n + 1))
                    dve.wait_ge(exp_ready, p * N + (n + 1))
                    step.run(dve.reduce_max(mx[:, s:s + 1], flat(2 * s, width), AX.X))
                    dve.tensor_scalar(neg[:, s:s + 1], mx[:, s:s + 1], -SCALE, None, ALU.mult).then_inc(max_ready, 1)

                def normalise(p, n, step):
                    s, width = n % 2, key_tiles(n) * P
                    dve.wait_ge(exp_ready, p * N + (2 + n + 1))
                    step.run(dve.reciprocal(inv[:, s:s + 1], total[:, s:s + 1]))
                    dve.tensor_scalar(pr[:, s, 0:width], pr[:, s, 0:width], inv[:, s:s + 1], None, ALU.mult
                                      ).then_inc(pr_ready, 1)

                def probsT(p, n):
                    g, i = n // 2, n % 2
                    for c, (k0, k1) in enumerate(chunks[n]):
                        m = before[n] + c
                        part = (slice(None), slice(k0, k1), slice(i * P, (i + 1) * P))
                        dve.wait_ge(pT_hi_ready, p * C + (m + 1))
                        dve.tensor_tensor(pT_lo[g % 2][part],
                                          psum[:, 4 + m % 2, 0:(k1 - k0) * P].rearrange("p (k n) -> p k n", n=P),
                                          f(pT_hi[g % 2][part]), ALU.subtract).then_inc(pT_ready, 1)

                def w_split(p, i):
                    lo, raw, hi = ((wq_lo, q_raw, wq_hi), (wkv_lo, kv_raw, wkv_hi))[i]
                    dve.wait_ge(w_hi_ready, p * 2 + (i + 1))
                    dve.tensor_tensor(lo[:], raw[:], f(hi[:]), ALU.subtract).then_inc(w_ready, 1)

                def pair(p, last):
                    step = Steps(dve, dve_step)
                    step.base = p * (2 * T + 2 * N + 6)
                    for t in range(T + 1):
                        if t >= 2:
                            tileT(p, t - 2, step)
                        if t < T:
                            tile(p, t, step)
                    maxes(p, 0, step)
                    tileT(p, T - 1, step)
                    for n in range(N + 1):
                        if n + 1 < N:
                            maxes(p, n + 1, step)
                        if n < N:
                            normalise(p, n, step)
                        if n >= 1:
                            probsT(p, n - 1)
                        if n in SPLIT and not last:
                            w_split(p + 1, SPLIT.index(n))
                    assert step.n == 2 * T + 2 * N + 6

                dve.sem_inc(mod_ready, 1)
                dve.sem_inc(tok_ready, 3)
                dve.sem_inc(tokT_ready, 2)
                dve.sem_inc(pT_ready, 2)
                for i in range(2):
                    w_split(0, i)
                dve.wait_ge(const_in, 16 * 7)
                dve.tensor_tensor(gg[:], g_qn[:], g_kn[:], ALU.mult).then_inc(gg_ready, 1)
                dve.wait_ge(gg_ready, 1)
                with dve.Fori(0, PAIRS - 1) as p:
                    pair(p, False)
                pair(PAIRS - 1, True)

            @block.tensor
            def _(pe):
                def proj(p, t):
                    b, toks = 2 * (t % 3), slice(t * P, (t + 1) * P)
                    pe.wait_ge(tok_ready, p * T + (t + 1))
                    if t == 0:
                        pe.wait_ge(w_ready, p * 2 + 1)
                    for k in range(QT):
                        mm3(pe, psum[:, b, 0:QW], cqT[0][:, k, toks], cqT[1][:, k, toks],
                            wq_hi[:, k, :], wq_lo[:, k, :], k == 0, k == QT - 1)
                    if t == 0:
                        pe.wait_ge(w_ready, p * 2 + 2)
                    for k in range(2):
                        mm = mm3(pe, psum[:, b + 1, :], ckvT[0][:, k, toks], ckvT[1][:, k, toks],
                                 wkv_hi[:, k, :], wkv_lo[:, k, :], k == 0, k == 1)
                    mm.then_inc(proj_ready, 1)

                def tokT(p, t):
                    b, s = 6, t % 2
                    pe.wait_ge(tok_ready, p * T + (3 + t + 1))
                    pe.wait_ge(tokT_ready, p * T + (t + 2))
                    if t == 0:
                        pe.wait_ge(o_ready, p * GN + 2)
                    if t % 2 == 1:
                        i = t // 2
                        pe.wait_ge(mod_w_in, p * 64 + 16 * (i + 1))
                        mod_products(pe, mod_psum, c_silu, mod_w, (i % 2) * HK, HK, ATT_N, True, True
                                     ).then_inc(mod_w_used, 1)
                    for k in range(4):
                        pe.transpose(psum[:, b, k * P:(k + 1) * P], q_tok[:, s, k, :], ident[:])
                    for k in range(2):
                        mm = pe.transpose(psum[:, b + 1, k * P:(k + 1) * P], k_tok[:, s, k, :], ident[:])
                    mm.then_inc(tokT_raw, 1)

                def scores(p, n):
                    j, g, i = unit(n)
                    width, toks = key_tiles(n) * P, slice((2 * g + i) * P, (2 * g + i + 1) * P)
                    pe.wait_ge(exp_ready, p * N + (n + 1))
                    for c in range(0, width, 512):
                        keys = slice(c, min(c + 512, width))
                        bank = 2 * (n % 2) + c // 512
                        out = psum[:, bank, 0:keys.stop - c]
                        mm3(pe, out, qT_hi[:, j, toks], qT_lo[:, j, toks], kT_hi[:, j, keys], kT_lo[:, j, keys],
                            True, False)
                        if keys.stop == width:
                            m0 = width - 2 * P - c
                            pe.matmul(psum[:, bank, m0:m0 + 2 * P], ident_bf[:], mask[:, i, :], start=False, stop=False)
                        pe.matmul(out, qT_hi[:, 2 + j, toks], krT[0][:, keys], start=False, stop=False)
                        mm = pe.matmul(out, qT_hi[:, 2 + j, toks], krT[1][:, keys], start=False, stop=True)
                    mm.then_inc(s_ready, 1)

                def probsT(p, n):
                    pe.wait_ge(pr_ready, p * N + (n + 1))
                    for c, (k0, k1) in enumerate(chunks[n]):
                        m = before[n] + c
                        pe.wait_ge(pT_ready, p * C + (m + 1))
                        for k in range(k0, k1):
                            mm = pe.transpose(psum[:, 4 + m % 2, (k - k0) * P:(k - k0 + 1) * P],
                                              pr[:, n % 2, k * P:(k + 1) * P], ident[:])
                        mm.then_inc(pT_raw, 1)

                def values(p, g):
                    j, s = g // GR, g % 2
                    pe.wait_ge(pT_ready, p * C + (2 + before[2 * g + 2]))
                    pe.wait_ge(o_ready, p * GN + (g + 1))
                    tiles = key_tiles(2 * g)
                    for k in range(tiles):
                        mm = mm3(pe, psum[:, 6 + s, 0:2 * P], v_hi[:, k, j * DN:(j + 1) * DN],
                                 v_lo[:, k, j * DN:(j + 1) * DN], pT_hi[s][:, k, :], pT_lo[s][:, k, :],
                                 k == 0, k == tiles - 1)
                    mm.then_inc(pv_ready, 1)

                pe.sem_inc(mod_w_used, 1)
                pe.sem_inc(proj_ready, 1)
                pe.sem_inc(tokT_raw, 2)
                pe.sem_inc(pT_raw, 1)
                pe.sem_inc(pv_ready, 2)
                with pe.Fori(0, PAIRS) as p:
                    for t in range(T + 1):
                        if t < T:
                            proj(p, t)
                        if t >= 2:
                            tokT(p, t - 2)
                    pe.wait_ge(const_in, 16 * 7)
                    scores(p, 0)
                    tokT(p, T - 1)
                    scores(p, 1)
                    pe.wait_ge(tokT_ready, p * T + (2 + T))
                    for n in range(N):
                        if n + 2 < N:
                            scores(p, n + 2)
                        probsT(p, n)
                        if n >= 2 and n % 2 == 0:
                            values(p, n // 2 - 1)
                    values(p, GN - 1)


def sample_query_phase(nc, psum, io, ident, cqT, ckvT, krT, wuk, qe, qrT, s_new):
    QT, HW, hr = QL // P, DN + DR, DR // 2
    toks = slice(SAMPLE * P, NTOK)
    with Phase(nc, "sq") as ph:
        wq_raw = ph.sb("wq_raw", [P, QT, H * HW])
        wq_hi, wq_lo = ph.sb("wq_hi", [P, QT, H * HW], F32R), ph.sb("wq_lo", [P, QT, H * HW], F32R)
        wuk_raw = ph.sb("wuk_raw", [P, 2, D])
        wukT = ph.sb("wukT", [P, H, KL])
        g_qn, g_kn, g_qr = ph.sb("g_qn", [P, DN]), ph.sb("g_kn", [P, DN]), ph.sb("g_qr", [P, DR])
        gg = ph.sb("gg", [P, DN])
        cos, sin = ph.sb("cos", [P, DR]), ph.sb("sin", [P, DR])
        sq, ksq = ph.sb("sq", [P, 4, 2 * HW]), ph.sb("ksq", [P, 3, 384])
        inv_n, eps, power = ph.sb("inv_n", [P, 3 * H]), ph.sb("eps", [P, 3 * H]), ph.sb("power", [P, 3 * H])
        ss, ms, rs = ph.sb("ss", [P, 3, H]), ph.sb("ms", [P, 3, H]), ph.sb("rs", [P, 3, H])
        qn = ph.sb("qn", [P, H, DN])
        qr, qr_cos, qr_sin = ph.sb("qr", [P, H, DR]), ph.sb("qr_cos", [P, H, DR]), ph.sb("qr_sin", [P, H, DR])
        qnT = ph.sb("qnT", [P, H, P])
        qe_f = ph.sb("qe_f", [P, 2, NB, H, TS])
        kr_f, ckv_f = ph.sb("kr_f", [P, P]), ph.sb("ckv_f", [P, 2, P])
        rn_wide, rn_keys = ph.sb("rn_wide", [P, H, TS]), ph.sb("rn_keys", [P, P])
        s_nope = ph.sb("s_nope", [P, P])

        wq_in, wuk_in = ph.sems("wq_in", 4), ph.sems("wuk_in", 2)
        wukT_in, const_in = ph.sem("wukT_in"), ph.sem("const_in")
        const_set = ph.sem("const_set")
        w_hi, w_ready = ph.sem("w_hi"), ph.sem("w_ready")
        q_ready, sq_ready, ss_ready, r_ready = ph.sem("q_ready"), ph.sem("sq_ready"), ph.sem("ss_ready"), ph.sem("r_ready")
        qtok_ready, qT_raw, qT_ready = ph.sem("qtok_ready"), ph.sem("qT_raw"), ph.sem("qT_ready")
        qe_raw, qe_f_ready, qe_ready = ph.sem("qe_raw"), ph.sem("qe_f_ready"), ph.sem("qe_ready")
        k_ready, ksq_ready, kss_ready, kr_ready = ph.sem("k_ready"), ph.sem("ksq_ready"), ph.sem("kss_ready"), ph.sem("kr_ready")
        lat_f_ready, wide_ready, s_raw, done = ph.sem("lat_f_ready"), ph.sem("wide_ready"), ph.sem("s_raw"), ph.sem("done")
        dve_step, pool_step = ph.sem("dve_step"), ph.sem("pool_step")

        def chunk(c):
            return slice(c * 2 * HW, (c + 1) * 2 * HW)

        with nc.Block() as block:
            @block.sync
            def _(sp):
                for i in range(2):
                    sp.dma_start(wuk_raw[:, i, :], io["w_uk"][:, i, :]).then_inc(wuk_in[i], 16)
                for c in range(4):
                    sp.dma_start(wq_raw[:, :, chunk(c)], io["w_q"][:, :, chunk(c)]).then_inc(wq_in[c], 16)
                sp.dma_start(wukT[:], io["w_ukT"]).then_inc(wukT_in, 16)
                for dst, src in ((g_qn, "g_qn"), (g_kn, "g_kn"), (g_qr, "g_qr")):
                    sp.dma_start(dst[:], io[src].partition_broadcast(P)).then_inc(const_in, 16)
                for dst, src in ((cos, "cos"), (sin, "sin")):
                    sp.dma_start(dst[:], io[src][:, SAMPLE, :]).then_inc(const_in, 16)

            @block.gpsimd
            def _(pool):
                step = Steps(pool, pool_step)
                pool.memset(inv_n[:, 0:H], 1.0 / DN)
                pool.memset(inv_n[:, H:2 * H], 1.0 / DR)
                pool.memset(inv_n[:, 2 * H:], 1.0 / DN)
                pool.memset(eps[:], EPS)
                pool.memset(power[:], -0.5).then_inc(const_set, 1)
                pool.wait_ge(const_set, 1)
                pool.memset(qrT[DR:, :, :], 0.0).then_inc(const_set, 1)
                pool.wait_ge(const_set, 2)

                def rms(parts, signal):
                    a, b = parts.start * H, parts.stop * H
                    flat = [t[:].rearrange("p a h -> p (a h)")[:, a:b] for t in (ss, ms, rs)]
                    step.run(pool.tensor_tensor(flat[1], flat[0], inv_n[:, a:b], ALU.mult))
                    step.run(pool.tensor_tensor(flat[1], flat[1], eps[:, a:b], ALU.add))
                    pool.tensor_tensor(flat[2], flat[1], power[:, a:b], ALU.pow).then_inc(signal, 1)

                pool.wait_ge(kss_ready, 1)
                rms(slice(2, 3), kr_ready)
                pool.wait_ge(ss_ready, 4)
                rms(slice(0, 2), r_ready)

            @block.scalar
            def _(act):
                for i in range(2):
                    act.wait_ge(wuk_in[i], 16)
                    act.activation(wuk[0][:, i, :], wuk_raw[:, i, :], ACT.Copy).then_inc(w_hi, 1)
                for c in range(4):
                    act.wait_ge(wq_in[c], 16)
                    act.activation(wq_hi[:, :, chunk(c)], wq_raw[:, :, chunk(c)], ACT.Copy).then_inc(w_hi, 1)
                act.wait_ge(k_ready, 1)
                act.activation(ksq[:, 0:2, :], psum[:, 4:6, 0:384], ACT.Square)
                act.activation(ksq[:, 2, 0:256], psum[:, 6, 0:256], ACT.Square).then_inc(ksq_ready, 1)
                for c in range(4):
                    act.wait_ge(q_ready, c + 1)
                    act.activation(sq[:, c, :], psum[:, c, 0:2 * HW], ACT.Square).then_inc(sq_ready, 1)
                act.wait_ge(qT_raw, 1)
                act.activation(qnT[:], psum[:, 4:6, :].rearrange("p a (h n) -> p (a h) n", n=P), ACT.Copy)
                act.activation(qrT[0:DR, :, :].rearrange("p b (h t) -> p b h t", t=TS),
                               psum[0:DR, 6:8, :].rearrange("p a (h b t) -> p b (a h) t", b=NB, t=TS),
                               ACT.Copy).then_inc(qT_ready, 1)
                act.wait_ge(qe_raw, 1)
                for k in range(2):
                    last = act.activation(qe_f[:, k], psum[:, 2 * k:2 * k + 2, :].rearrange(
                        "p a (h b t) -> p b (a h) t", b=NB, t=TS), ACT.Copy)
                last.then_inc(qe_f_ready, 1)
                act.wait_ge(qe_f_ready, 1)
                act.activation(qe[0][:], qe_f[:].rearrange("p k b h t -> p k b (h t)"), ACT.Copy).then_inc(qe_ready, 1)

            @block.vector
            def _(dve):
                step = Steps(dve, dve_step)
                for i in range(2):
                    dve.wait_ge(w_hi, i + 1)
                    dve.tensor_tensor(wuk[1][:, i, :], wuk_raw[:, i, :], f(wuk[0][:, i, :]), ALU.subtract
                                      ).then_inc(w_ready, 1)
                for c in range(4):
                    dve.wait_ge(w_hi, 2 + c + 1)
                    dve.tensor_tensor(wq_lo[:, :, chunk(c)], wq_raw[:, :, chunk(c)], f(wq_hi[:, :, chunk(c)]),
                                      ALU.subtract).then_inc(w_ready, 1)
                dve.tensor_tensor(ckv_f[:], f(ckvT[0][:, :, toks]), f(ckvT[1][:, :, toks]), ALU.add)
                dve.tensor_tensor(kr_f[:], f(krT[0][:, toks]), f(krT[1][:, toks]), ALU.add).then_inc(lat_f_ready, 1)
                dve.wait_ge(const_in, 16 * 5)
                step.then(dve.tensor_tensor(gg[:], g_qn[:], g_kn[:], ALU.mult))
                dve.wait_ge(ksq_ready, 1)
                dve.reduce_sum(ss[:, 2, :], ksq[:].rearrange("p a n -> p (a n)")[:, 0:D].rearrange(
                    "p (h x) -> p h x", x=DN), AX.X).then_inc(kss_ready, 1)
                for c in range(4):
                    dve.wait_ge(sq_ready, c + 1)
                    heads = sq[:, c, :].rearrange("p (j x) -> p j x", j=2)
                    dve.reduce_sum(ss[:, 0, 2 * c:2 * c + 2], heads[:, :, 0:DN], AX.X)
                    dve.reduce_sum(ss[:, 1, 2 * c:2 * c + 2], heads[:, :, DN:], AX.X).then_inc(ss_ready, 1)
                dve.wait_ge(kr_ready, 1)
                dve.wait_ge(r_ready, 1)
                q = psum[:, 0:4, 0:2 * HW].rearrange("p a (j x) -> p a j x", j=2)

                def per_head(t, width):
                    return t.rearrange("p (a j) -> p a j", j=2).unsqueeze(3).to_broadcast([P, 4, 2, width])

                dve.tensor_tensor(qn[:].rearrange("p (a j) x -> p a j x", j=2), q[:, :, :, 0:DN],
                                  per_head(rs[:, 0, :], DN), ALU.mult)
                step.run(dve.tensor_tensor(qr[:].rearrange("p (a j) x -> p a j x", j=2), q[:, :, :, DN:],
                                           per_head(rs[:, 1, :], DR), ALU.mult))
                step.then(dve.tensor_tensor(qn[:], qn[:], gg[:].unsqueeze(1).to_broadcast([P, H, DN]), ALU.mult))
                step.run(dve.tensor_tensor(qr[:], qr[:], g_qr[:].unsqueeze(1).to_broadcast([P, H, DR]), ALU.mult))
                cos_h = cos[:].unsqueeze(1).to_broadcast([P, H, DR])
                sin_h = sin[:].unsqueeze(1).to_broadcast([P, H, DR])
                dve.tensor_tensor(qr_cos[:], qr[:], cos_h, ALU.mult)
                dve.tensor_tensor(qr_sin[:, :, 0:hr], qr[:, :, hr:], sin_h[:, :, 0:hr], ALU.mult)
                step.run(dve.tensor_tensor(qr_sin[:, :, hr:], qr[:, :, 0:hr], sin_h[:, :, hr:], ALU.mult))
                dve.tensor_tensor(qr[:], qr_cos[:], qr_sin[:], ALU.add).then_inc(qtok_ready, 1)
                dve.tensor_copy(rn_wide[:], rs[:, 2, :].unsqueeze(2).to_broadcast([P, H, TS])).then_inc(wide_ready, 1)
                dve.wait_ge(qe_ready, 1)
                dve.tensor_tensor(qe[1][:], qe_f[:].rearrange("p k b h t -> p k b (h t)"), f(qe[0][:]), ALU.subtract)
                dve.wait_ge(s_raw, 1)
                step.run(dve.tensor_copy(rn_keys[:], psum[:, 4, 0:P]))
                step.run(dve.tensor_tensor(s_nope[:], psum[:, 5, 0:P], rn_keys[:], ALU.mult))
                dve.tensor_tensor(s_new[:], psum[:, 6, 0:P], s_nope[:], ALU.add).then_inc(done, 1)

            @block.tensor
            def _(pe):
                pe.wait_ge(w_ready, 2)
                for c, (c0, c1) in enumerate(((0, 384), (384, 768), (768, D))):
                    for k in range(2):
                        mm = mm3(pe, psum[:, 4 + c, 0:c1 - c0], ckvT[0][:, k, toks], ckvT[1][:, k, toks],
                                 wuk[0][:, k, c0:c1], wuk[1][:, k, c0:c1], k == 0, k == 1)
                mm.then_inc(k_ready, 1)
                for c in range(4):
                    pe.wait_ge(w_ready, 2 + c + 1)
                    for k in range(QT):
                        mm = mm3(pe, psum[:, c, 0:2 * HW], cqT[0][:, k, toks], cqT[1][:, k, toks],
                                 wq_hi[:, k, chunk(c)], wq_lo[:, k, chunk(c)], k == 0, k == QT - 1)
                    mm.then_inc(q_ready, 1)
                pe.wait_ge(qtok_ready, 1)
                pe.wait_ge(ksq_ready, 1)
                for h in range(H):
                    pe.transpose(psum[:, 4 + h // 4, (h % 4) * P:(h % 4 + 1) * P], qn[:, h, :], ident[:])
                    mm = pe.transpose(psum[0:DR, 6 + h // 4, (h % 4) * P:(h % 4 + 1) * P], qr[:, h, :], ident[:])
                mm.then_inc(qT_raw, 1)
                pe.wait_ge(qT_ready, 1)
                pe.wait_ge(wukT_in, 16)
                for k in range(2):
                    for h in range(H):
                        mm = pe.matmul(psum[:, 2 * k + h // 4, (h % 4) * P:(h % 4 + 1) * P],
                                       wukT[:, h, k * P:(k + 1) * P], qnT[:, h, :], start=True, stop=True)
                mm.then_inc(qe_raw, 1)
                pe.wait_ge(wide_ready, 1)
                pe.matmul(psum[:, 4, 0:P], rn_wide[:].rearrange("p h t -> p (h t)"), ident[:], start=True, stop=True)
                pe.wait_ge(qe_f_ready, 1)
                pe.wait_ge(lat_f_ready, 1)
                for b in range(NB):
                    own = slice(b * TS, (b + 1) * TS)
                    for k in range(2):
                        pe.matmul(psum[:, 5, own], qe_f[:, k, b].rearrange("p h t -> p (h t)"), ckv_f[:, k, own],
                                  start=(k == 0), stop=(k == 1))
                    mm = pe.matmul(psum[:, 6, own], qrT[:, b, :], kr_f[:, own], start=True, stop=True)
                mm.then_inc(s_raw, 1)


def sample_attention_phase(nc, psum, io, ident, wuk, qe, qrT, s_new):
    T = PAST // P
    CW = 384
    LAST = D - 2 * CW
    KEYS = PAST + TS
    PT, SB = 7, 6
    with Phase(nc, "satt") as ph:
        lT_raw = ph.sb("lT_raw", [P, 2, PAST])
        lT_hi, lT_lo = ph.sb("lT_hi", [P, 2, PAST], F32R), ph.sb("lT_lo", [P, 2, PAST], F32R)
        kpeT = ph.sb("kpeT", [P, PAST])
        l_raw = ph.sb("l_raw", [P, T, KL])
        l_hi, l_lo = ph.sb("l_hi", [P, T, KL], F32R), ph.sb("l_lo", [P, T, KL], F32R)
        l_new = ph.sb("l_new", [P, NB, KL])
        wc_hi, wc_lo = ph.sb("wc_hi", [P, 2, CW], F32R), ph.sb("wc_lo", [P, 2, CW], F32R)
        sq = ph.sb("sq", [P, 2, D])
        ss, ms, rn = ph.sb("ss", [P, 2, H]), ph.sb("ms", [P, 2, H]), ph.sb("rn", [P, 2, H])
        power, eps = ph.sb("power", [P, H]), ph.sb("eps", [P, H])
        st_nope = ph.sb("st_nope", [P, H, TS])
        st = ph.sb("st", [P, 2, P])
        s = ph.sb("s", [P, KEYS])
        pr = ph.sb("pr", [P, (T + 1) * P])
        mx, neg, total, inv = (ph.sb(n, [P, 1]) for n in ("mx", "neg", "total", "inv"))
        pT_hi, pT_lo = ph.sb("pT_hi", [P, T, P], F32R), ph.sb("pT_lo", [P, T, P], F32R)
        pT_new = ph.sb("pT_new", [P, P])
        o = ph.sb("o", [P, KL])
        oT = ph.sb("oT", [P, 2, H, NB, TS])
        wuv = ph.sb("wuv", [P, 2, H * DN])
        out = ph.sb("out", [P, H, P])

        const_in, const_set, wc_set = ph.sem("const_in"), ph.sem("const_set"), ph.sem("wc_set")
        l_new_in = ph.sem("l_new_in")
        lT_in, kpe_in, l_in = ph.sems("lT_in", 4), ph.sems("kpe_in", 4), ph.sems("l_in", 4)
        lT_hi_ready, lT_ready = ph.sem("lT_hi_ready"), ph.sem("lT_ready")
        wc_ready = ph.sem("wc_ready")
        k_ready = ph.sem("k_ready")
        sq_ready = ph.sem("sq_ready")
        ss_ready = ph.sem("ss_ready")
        rn_ready = ph.sem("rn_ready")
        st_ready = ph.sem("st_ready")
        sb_raw = ph.sem("sb_raw")
        s_ready = ph.sem("s_ready")
        max_ready = ph.sem("max_ready")
        exp_ready = ph.sem("exp_ready")
        inv_ready = ph.sem("inv_ready")
        l_hi_ready, l_ready = ph.sem("l_hi_ready"), ph.sem("l_ready")
        pT_raw = ph.sem("pT_raw")
        pT_hi_ready, pT_ready = ph.sem("pT_hi_ready"), ph.sem("pT_ready")
        pv_ready = ph.sem("pv_ready")
        o_ready, oT_raw = ph.sem("o_ready"), ph.sem("oT_raw")
        oT_ready = ph.sem("oT_ready")
        out_raw, out_ready, stored = ph.sem("out_raw"), ph.sem("out_ready"), ph.sem("stored")
        dve_step, pool_step = ph.sem("dve_step"), ph.sem("pool_step")

        def quarter(q):
            return slice(q * PAST // 4, (q + 1) * PAST // 4)

        def banks(t):
            return 3 * (t % 2)

        def streams(eng, body, tail):
            body(0, False, True)
            with eng.Fori(1, NB - 1) as b:
                body(b, True, True)
            body(NB - 1, True, False)
            tail(NB - 1)

        with nc.Block() as block:
            @block.sync
            def _(sp):
                def load_lT(b, q):
                    sp.dma_start(lT_raw[:, :, quarter(q)], io["cacheT"][b, :, :, quarter(q)]).then_inc(lT_in[q], 16)

                def load_kpe(b, q):
                    sp.dma_start(kpeT[0:DR, quarter(q)], io["kpeT"][b, :, quarter(q)]).then_inc(kpe_in[q], 16)

                for q in range(4):
                    load_lT(0, q)
                    load_kpe(0, q)
                sp.dma_start(wuv[:], io["w_uv"]).then_inc(const_in, 16)
                with sp.Fori(0, NB - 1) as b:
                    for q in range(4):
                        sp.wait_ge(lT_ready, b * T + (2 * q + 2))
                        load_lT(b + 1, q)
                        sp.wait_ge(k_ready, b * T + (8 + 2 * q + 2))
                        load_kpe(b + 1, q)
                sp.wait_ge(out_ready, 2)
                sp.dma_start(io["mixT"].rearrange("k p n -> p k n")[:, :, SEQ:], out[:]).then_inc(stored, 16)
                sp.wait_ge(stored, 16)

            @block.gpsimd
            def _(pool):
                def load_l(b, q):
                    pool.dma_start(l_raw[:, 2 * q:2 * q + 2, :], io["cache"][b, :, 2 * q:2 * q + 2, :]
                                   ).then_inc(l_in[q], 16)

                def rms(b, t, step):
                    c = t % 2
                    pool.wait_ge(ss_ready, b * T + (2 + t + 1))
                    step.run(pool.tensor_tensor(ms[:, c, :], ss[:, c, :], eps[:], ALU.add))
                    pool.wait_ge(st_ready, b * T + (t + 1))
                    pool.tensor_tensor(rn[:, c, :], ms[:, c, :], power[:], ALU.pow).then_inc(rn_ready, 1)

                def tail(b, q):
                    pool.wait_ge(l_hi_ready, b * 4 + (q + 1))
                    part = (slice(None), slice(2 * q, 2 * q + 2))
                    pool.tensor_tensor(l_lo[part], l_raw[part], f(l_hi[part]), ALU.subtract).then_inc(l_ready, 1)

                def body(b, prev, nxt):
                    step = Steps(pool, pool_step)
                    step.base = b * T
                    for t in range(T):
                        if prev and t < 4:
                            tail(b - 1, t)
                            pool.wait_ge(l_ready, b * 4 + (t + 1 - 4))
                            load_l(b, t)
                        rms(b, t, step)

                pool.memset(l_new[:], 0.0)
                pool.memset(pr[:, KEYS:], 0.0)
                pool.memset(eps[:], DN * EPS)
                pool.memset(power[:], -0.5).then_inc(const_set, 1)
                pool.wait_ge(const_set, 1)
                pool.memset(kpeT[DR:, :], 0.0).then_inc(const_set, 1)
                pool.wait_ge(const_set, 2)
                for q in range(4):
                    load_l(0, q)
                pool.dma_start(l_new[0:TS, :, :], io["ckv_new"][SAMPLE].rearrange("(b t) l -> t b l", t=TS)
                               ).then_inc(l_new_in, 16)
                streams(pool, body, lambda b: [tail(b, q) for q in range(4)])

            @block.scalar
            def _(act):
                def lT_split(b, t):
                    if t % 2 == 0:
                        act.wait_ge(lT_in[t // 2], b * 16 + 16)
                    act.wait_ge(k_ready, b * T + (t + 1))
                    keys = slice(t * P, (t + 1) * P)
                    act.activation(lT_hi[:, :, keys], lT_raw[:, :, keys], ACT.Copy).then_inc(lT_hi_ready, 1)

                def squares(b, t):
                    act.wait_ge(k_ready, b * T + (8 + t + 1))
                    act.wait_ge(ss_ready, b * T + (t + 1))
                    k, c = banks(t), t % 2
                    act.activation(sq[:, c, 2 * CW:], psum[:, k + 2, 0:LAST], ACT.Square)
                    act.activation(sq[:, c, 0:2 * CW].rearrange("p (a n) -> p a n", a=2), psum[:, k:k + 2, 0:CW],
                                   ACT.Square).then_inc(sq_ready, 1)

                def evict_scores(b, half):
                    act.wait_ge(sb_raw, b * T + (2 + 4 * half + 4))
                    act.wait_ge(exp_ready, b + 1)
                    act.activation(s[:, half * 512:half * 512 + 512], psum[:, SB, :], ACT.Copy).then_inc(s_ready, 1)

                def before(b, slot):
                    if slot < 4:
                        part = (slice(None), slice(2 * slot, 2 * slot + 2))
                        act.wait_ge(l_in[slot], b * 16 + 16)
                        act.wait_ge(pv_ready, b + 1)
                        act.activation(l_hi[part], l_raw[part], ACT.Copy).then_inc(l_hi_ready, 1)
                    if slot in (4, 5):
                        c = slot - 4
                        act.wait_ge(pT_raw, b * 3 + (1 + c + 1))
                        act.activation(pT_hi[:, 4 * c:4 * c + 4, :], psum[:, PT, :].rearrange("p (k n) -> p k n", n=P),
                                       ACT.Copy).then_inc(pT_hi_ready, 1)
                    if slot == 6:
                        act.wait_ge(pT_raw, b * 3 + 4)
                        act.activation(pT_new[:], psum[:, PT, 0:P], ACT.Copy).then_inc(pT_hi_ready, 1)
                    if slot == 7:
                        act.wait_ge(pv_ready, b + 2)
                        act.wait_ge(inv_ready, b + 1)
                        act.activation(o[:], psum[:, PT, 0:KL], ACT.Copy, scale=inv[:]).then_inc(o_ready, 1)

                def after(b, slot):
                    if slot == 1:
                        evict_scores(b, 1)
                    if slot == 2:
                        act.wait_ge(max_ready, b + 1)
                        act.wait_ge(pT_raw, b * 3 + 1)
                        act.activation(pr[:, 0:KEYS], s[:], ACT.Exp, bias=neg[:], scale=SCALE,
                                       accum_out=total[:]).then_inc(exp_ready, 1)
                    if slot == 7:
                        act.wait_ge(oT_raw, b + 1)
                        for k in range(2):
                            last = act.activation(oT[:, k, :, b, :], psum[:, PT, k * P:(k + 1) * P].rearrange(
                                "p (h t) -> p h t", t=TS), ACT.Copy)
                        last.then_inc(oT_ready, 1)

                def body(b, prev, nxt):
                    for t in range(T):
                        if t + 2 < T:
                            lT_split(b, t + 2)
                        elif nxt:
                            lT_split(b + 1, t + 2 - T)
                        if prev:
                            before(b - 1, t)
                        squares(b, t)
                        if prev:
                            after(b - 1, t)
                        if t == 5:
                            evict_scores(b, 0)

                def tail(b):
                    for slot in range(T):
                        before(b, slot)
                        after(b, slot)

                act.sem_inc(s_ready, 1)
                act.sem_inc(sq_ready, 2)
                act.sem_inc(exp_ready, 1)
                act.sem_inc(oT_ready, 1)
                act.activation(wc_hi[:, :, 0:LAST], f(wuk[0][:, :, 2 * CW:]), ACT.Copy).then_inc(wc_set, 1)
                lT_split(0, 0)
                lT_split(0, 1)
                act.wait_ge(const_set, 2)
                streams(act, body, tail)
                act.wait_ge(out_raw, 1)
                for half in range(2):
                    act.activation(out[:, 4 * half:4 * half + 4, :], psum[:, half, :].rearrange("p (h n) -> p h n", n=P),
                                   ACT.Copy).then_inc(out_ready, 1)

            @block.vector
            def _(dve):
                def lT_split(b, t):
                    keys = slice(t * P, (t + 1) * P)
                    dve.wait_ge(lT_hi_ready, b * T + (t + 1))
                    dve.tensor_tensor(lT_lo[:, :, keys], lT_raw[:, :, keys], f(lT_hi[:, :, keys]), ALU.subtract
                                      ).then_inc(lT_ready, 1)

                def place_queries(b):
                    dve.wait_ge(k_ready, b * T + 8)
                    dve.tensor_copy(wc_hi[:, :, LAST:], f(qe[0][:, :, b, :]))
                    dve.tensor_copy(wc_lo[:, :, LAST:], f(qe[1][:, :, b, :])).then_inc(wc_ready, 1)

                def sums(b, t):
                    dve.wait_ge(sq_ready, b * T + (2 + t + 1))
                    dve.reduce_sum(ss[:, t % 2, :], sq[:, t % 2, :].rearrange("p (h x) -> p h x", x=DN), AX.X
                                   ).then_inc(ss_ready, 1)

                def scores(b, t, step):
                    bank = psum[:, banks(t) + 2, :]
                    dve.wait_ge(rn_ready, b * T + (t + 1))
                    step.run(dve.scalar_tensor_tensor(
                        st_nope[:], bank[:, LAST:CW].rearrange("p (h t) -> p h t", t=TS), DN ** 0.5,
                        rn[:, t % 2, :].unsqueeze(2).to_broadcast([P, H, TS]), ALU.mult, ALU.mult))
                    dve.wait_ge(sb_raw, b * T + (t + 1))
                    dve.tensor_tensor(st[:, t % 2, :], bank[:, CW:CW + P], st_nope[:].rearrange("p h t -> p (h t)"),
                                      ALU.add).then_inc(st_ready, 1)

                def tail(b, slot, step):
                    if slot == 2:
                        dve.wait_ge(s_ready, b * 2 + 3)
                        step.run(dve.tensor_copy(s[:, PAST:], s_new[:, bass.ts(b, TS)]))
                        step.run(dve.reduce_max(mx[:], s[:], AX.X))
                        dve.tensor_scalar(neg[:], mx[:], -SCALE, None, ALU.mult).then_inc(max_ready, 1)
                    if slot == 3:
                        dve.wait_ge(exp_ready, b + 2)
                        dve.reciprocal(inv[:], total[:]).then_inc(inv_ready, 1)
                    if slot in (4, 5):
                        c = slot - 4
                        part = (slice(None), slice(4 * c, 4 * c + 4))
                        dve.wait_ge(pT_hi_ready, b * 3 + (c + 1))
                        dve.tensor_tensor(pT_lo[part], psum[:, PT, :].rearrange("p (k n) -> p k n", n=P), f(pT_hi[part]),
                                          ALU.subtract).then_inc(pT_ready, 1)

                def body(b, prev, nxt):
                    step = Steps(dve, dve_step)
                    step.base = b * (T + 2) - (2 if prev else 0)
                    for t in range(T):
                        sums(b, t)
                        if prev:
                            tail(b - 1, t + 1, step)
                        if t + 2 < T:
                            lT_split(b, t + 2)
                        elif nxt:
                            lT_split(b + 1, t + 2 - T)
                        if t == T - 1 and nxt:
                            place_queries(b + 1)
                        scores(b, t, step)

                def last_tail(b):
                    step = Steps(dve, dve_step)
                    step.base = b * (T + 2) + T
                    for slot in range(T):
                        tail(b, slot, step)

                dve.sem_inc(ss_ready, 2)
                dve.sem_inc(st_ready, 2)
                dve.tensor_copy(wc_lo[:, :, 0:LAST], f(wuk[1][:, :, 2 * CW:])).then_inc(wc_set, 1)
                place_queries(0)
                lT_split(0, 0)
                lT_split(0, 1)
                streams(dve, body, last_tail)

            @block.tensor
            def _(pe):
                def keys(b, t):
                    k, tile = banks(t), slice(t * P, (t + 1) * P)
                    pe.wait_ge(lT_ready, b * T + (t + 1))
                    pe.wait_ge(sq_ready, b * T + (t + 1))
                    for c in range(3):
                        if c == 2:
                            pe.wait_ge(st_ready, b * T + (t + 1))
                        if c == 2 and t == 0:
                            pe.wait_ge(wc_ready, b + 1)
                        for i in range(2):
                            hi, lo = (w[:, i, c * CW:(c + 1) * CW] for w in wuk) if c < 2 else (wc_hi[:, i, :], wc_lo[:, i, :])
                            mm3(pe, psum[:, k + c, 0:CW], lT_hi[:, i, tile], lT_lo[:, i, tile], hi, lo, i == 0, i == 1)
                    if t % 2 == 0:
                        pe.wait_ge(kpe_in[t // 2], b * 16 + 16)
                    pe.matmul(psum[:, k + 2, CW:CW + P], kpeT[:, tile], qrT[:, b, :], start=True, stop=True
                              ).then_inc(k_ready, 1)

                def turn(b, t):
                    pe.wait_ge(st_ready, b * T + (2 + t + 1))
                    if t % 4 == 0:
                        pe.wait_ge(s_ready, b * 2 + (t // 4 + 1))
                    pe.transpose(psum[:, SB, (t % 4) * P:(t % 4 + 1) * P], st[:, t % 2, :], ident[:]).then_inc(sb_raw, 1)

                def before(b, slot):
                    if slot in (4, 5, 6):
                        c = slot - 4
                        if c == 0:
                            pe.wait_ge(exp_ready, b + 2)
                            pe.wait_ge(oT_ready, b + 1)
                        else:
                            pe.wait_ge(pT_ready, b * 2 + c)
                        for k in range(4 * c, min(4 * c + 4, T + 1)):
                            mm = pe.transpose(psum[:, PT, (k % 4) * P:(k % 4 + 1) * P], pr[:, k * P:(k + 1) * P], ident[:])
                        mm.then_inc(pT_raw, 1)

                def after(b, slot):
                    if slot < 2:
                        turn(b, T - 2 + slot)
                    if slot == 6:
                        pe.wait_ge(pT_hi_ready, b * 3 + 3)
                        pe.wait_ge(l_ready, b * 4 + 4)
                        pe.wait_ge(l_new_in, 16)
                        for k in range(T):
                            mm3(pe, psum[:, PT, 0:KL], pT_hi[:, k, :], pT_lo[:, k, :], l_hi[:, k, :], l_lo[:, k, :],
                                k == 0, False)
                        pe.matmul(psum[:, PT, 0:KL], pT_new[:], l_new[:, b, :], start=False, stop=True
                                  ).then_inc(pv_ready, 1)
                    if slot == 7:
                        pe.wait_ge(o_ready, b + 1)
                        for k in range(2):
                            mm = pe.transpose(psum[:, PT, k * P:(k + 1) * P], o[:, k * P:(k + 1) * P], ident[:])
                        mm.then_inc(oT_raw, 1)

                def body(b, prev, nxt):
                    for t in range(T):
                        if prev:
                            before(b - 1, t)
                        keys(b, t)
                        if prev:
                            after(b - 1, t)
                        if t >= 2:
                            turn(b, t - 2)

                def tail(b):
                    for slot in range(T):
                        before(b, slot)
                        after(b, slot)

                pe.sem_inc(k_ready, 8)
                pe.sem_inc(sb_raw, 2)
                pe.sem_inc(pT_raw, 1)
                pe.sem_inc(pv_ready, 1)
                pe.wait_ge(const_set, 2)
                pe.wait_ge(wc_set, 2)
                streams(pe, body, tail)
                pe.wait_ge(const_in, 16)
                pe.wait_ge(oT_ready, 1 + NB)
                for h in range(H):
                    for k in range(2):
                        mm = pe.matmul(psum[:, h // 4, (h % 4) * P:(h % 4 + 1) * P], wuv[:, k, h * DN:(h + 1) * DN],
                                       oT[:, k, h].rearrange("p b t -> p (b t)"), start=(k == 0), stop=(k == 1))
                mm.then_inc(out_raw, 1)


def gating_phase(nc, psum, io, ident):
    NA = 3
    WR = 4
    CHUNKS = (2, 3, 0, 1)
    with Phase(nc, "gate") as ph:
        w_hi, w_lo = ph.sb("w_hi", [P, KT, 2 * D], F32R), ph.sb("w_lo", [P, KT, 2 * D], F32R)
        w_raw = ph.sb("w_raw", [P, 2, D])
        x = ph.sb("x", [P, 3, D])
        hT_hi = [ph.sb(f"hT_hi{i}", [P, KT, P], F32R) for i in range(2)]
        hT_lo = [ph.sb(f"hT_lo{i}", [P, KT, P], F32R) for i in range(2)]
        scale_t, shift_t, g_v = ph.sb("scale_t", [P, D]), ph.sb("shift_t", [P, D]), ph.sb("g_v", [P, D])
        z = ph.sb("z", [P, 2, 2 * D])
        ws = ph.sb("ws", [P, 2, G, P])
        bs = ph.sb("bs", [P, 2, G])
        gT = ph.sb("gT", [P, KT, P])
        junk = ph.sb("junk", [P, D], BF16)
        ss, ms, rstd = ph.sb("ss", [P, 2]), ph.sb("ms", [P, 2]), ph.sb("rstd", [P, 2])
        vss, vms, vr = ph.sb("vss", [P, 2]), ph.sb("vms", [P, 2]), ph.sb("vr", [P, 2])
        power = ph.sb("power", [P, 1])

        raw = [w_raw[:, 0, :], w_raw[:, 1, :], z[:, 1, 0:D], z[:, 1, D:]]

        raw_in, x_in = ph.sems("raw_in", WR), ph.sems("x_in", 3)
        tab_in, stab_in, const_in = ph.sem("tab_in"), ph.sem("stab_in"), ph.sem("const_in")
        ws_in, ws_zero, blocks_in, ws_ready = ph.sem("ws_in"), ph.sem("ws_zero"), ph.sem("blocks_in"), ph.sem("ws_ready")
        const_set = ph.sem("const_set")
        w_hi_ready, w_ready = ph.sem("w_hi_ready"), ph.sem("w_ready")
        ss_ready, rstd_ready, xn_ready, h_ready = (ph.sem(n) for n in ("ss_ready", "rstd_ready", "xn_ready", "h_ready"))
        hT_raw, hT_hi_ready, hT_ready = ph.sem("hT_raw"), ph.sem("hT_hi_ready"), ph.sem("hT_ready")
        z_raw, z_ready = ph.sem("z_raw"), ph.sem("z_ready")
        vss_ready, vr_ready, v_ready = ph.sem("vss_ready"), ph.sem("vr_ready"), ph.sem("v_ready")
        mix_raw, g_ready, gT_raw, gT_ready = (ph.sem(n) for n in ("mix_raw", "g_ready", "gT_raw", "gT_ready"))
        gT_stored, v_stored = ph.sem("gT_stored"), ph.sem("v_stored")
        pool_step = ph.sem("pool_step")

        with nc.Block() as block:
            @block.sync
            def _(sp):
                def load_x(t):
                    if t >= 3:
                        sp.wait_ge(hT_raw, 2 * (t - 2))
                    sp.dma_start(x[:, t % 3, :], io["x_mid"][t]).then_inc(x_in[t % 3], 16)

                load_x(0)
                load_table(sp, scale_t, io["mod"], 1, SCALE1, 0, tab_in)
                load_table(sp, shift_t, io["mod"], 1, SHIFT1, 0, tab_in)
                for n in range(2 * KT):
                    if n >= WR:
                        sp.wait_ge(w_ready, n - WR + 1)
                    half, k = 1 - n // KT, n % KT
                    sp.dma_start(raw[n % WR], io["cm_w_in"][k, :, half * D:(half + 1) * D]
                                 ).then_inc(raw_in[n % WR], 16)
                    if n == 3:
                        load_x(1)
                        load_x(2)
                        sp.dma_start(ws[:, 0], io["w_sT"]).then_inc(ws_in, 16)
                        sp.dma_start(bs[:, 0, :], io["b_sT"]).then_inc(const_in, 16)
                        for b in range(NB):
                            sp.dma_start(bs[b * TS:(b + 1) * TS, 1, :], io["b_sT"][0:TS, :]).then_inc(const_in, 16)
                        sp.dma_start(g_v[:], io["cm_g_v"].partition_broadcast(P)).then_inc(const_in, 16)
                    if n == 6:
                        sp.wait_ge(ws_zero, 1)
                        for b in range(NB):
                            rows = slice(b * TS, (b + 1) * TS)
                            sp.dma_start(ws[rows, 1, :, rows], io["w_sT"][0:TS, :, 0:TS]).then_inc(blocks_in, 16)
                for t in range(TT + 2):
                    if 3 <= t + 1 < TT:
                        load_x(t + 1)
                    if t == SAMPLE - 1:
                        sp.wait_ge(h_ready, SAMPLE)
                        load_table(sp, scale_t, io["mod"], 1, SCALE1, SAMPLE, stab_in)
                        load_table(sp, shift_t, io["mod"], 1, SHIFT1, SAMPLE, stab_in)
                    if t >= 2:
                        u = t - 2
                        sp.wait_ge(gT_ready, 2 * u + 2)
                        sp.dma_start(io["mixT"].rearrange("k p n -> p k n")[:, :, u * P:(u + 1) * P], gT[:]
                                     ).then_inc(gT_stored, 16)
                    if t == SAMPLE + 1:
                        sp.wait_ge(v_ready, TT)
                        sp.dma_start(io["v_new"], z[:, SAMPLE % 2, D:]).then_inc(v_stored, 16)
                sp.wait_ge(gT_stored, 16 * TT)
                sp.wait_ge(v_stored, 16)

            @block.gpsimd
            def _(pool):
                step = Steps(pool, pool_step)
                pool.memset(power[:], -0.5).then_inc(const_set, 1)
                pool.wait_ge(const_set, 1)

                def rms(t):
                    c = slice(t % 2, t % 2 + 1)
                    pool.wait_ge(ss_ready, t + 1)
                    step.run(pool.tensor_scalar(ms[:, c], ss[:, c], 1.0 / D, EPS, ALU.mult, ALU.add))
                    if t >= 2:
                        pool.wait_ge(xn_ready, t - 1)
                    pool.tensor_tensor(rstd[:, c], ms[:, c], power[:], ALU.pow).then_inc(rstd_ready, 1)

                def v_rms(t):
                    c = slice(t % 2, t % 2 + 1)
                    pool.wait_ge(vss_ready, t + 1)
                    step.run(pool.tensor_scalar(vms[:, c], vss[:, c], 1.0 / D, EPS, ALU.mult, ALU.add))
                    if t >= 2:
                        pool.wait_ge(v_ready, t - 1)
                    pool.tensor_tensor(vr[:, c], vms[:, c], power[:], ALU.pow).then_inc(vr_ready, 1)

                rms(0)
                pool.memset(ws[:, 1], 0.0).then_inc(ws_zero, 1)
                pool.wait_ge(ws_in, 16)
                pool.wait_ge(ws_zero, 1)
                pool.memset(ws[64:, 0, :, 0:64], 0.0).then_inc(ws_ready, 1)
                pool.wait_ge(ws_ready, 1)
                for slot in range(-1, TT + 1):
                    if 0 <= slot < TT:
                        v_rms(slot)
                    if 0 <= slot + 2 < TT:
                        rms(slot + 2)

            @block.scalar
            def _(act):
                def squares(t):
                    act.wait_ge(x_in[t % 3], 16 * (t // 3 + 1))
                    if t >= 2:
                        act.wait_ge(rstd_ready, t - 1)
                    if t >= 1:
                        act.wait_ge(ss_ready, t)
                    if t >= 2:
                        act.wait_ge(vss_ready, t - 1)
                    act.activation(junk[:], x[:, t % 3, :], ACT.Square, accum_out=ss[:, t % 2:t % 2 + 1]
                                   ).then_inc(ss_ready, 1)

                def w_split(n):
                    half, k = 1 - n // KT, n % KT
                    act.wait_ge(raw_in[n % WR], 16 * (n // WR + 1))
                    act.activation(w_hi[:, k, half * D:(half + 1) * D], raw[n % WR], ACT.Copy).then_inc(w_hi_ready, 1)

                def hT_split(t):
                    for half in range(2):
                        act.wait_ge(hT_raw, 2 * t + half + 1)
                        if t >= 2:
                            act.wait_ge(z_raw, 4 * (t - 1))
                        act.activation(hT_hi[t % 2][:, 4 * half:4 * half + 4, :],
                                       psum[:, half, :].rearrange("p (k n) -> p k n", k=4),
                                       ACT.Copy).then_inc(hT_hi_ready, 1)

                def gelu(t, n):
                    act.wait_ge(z_raw, 4 * t + n + 1)
                    c = CHUNKS[n]
                    if n == 0 and t >= 2:
                        act.wait_ge(mix_raw, t - 1)
                    if n == 2 and t >= 2:
                        act.wait_ge(gT_raw, 2 * (t - 1))
                    act.activation(z[:, t % 2, c * 512:(c + 1) * 512], psum[:, 2 + n, :], ACT.Gelu_apprx_tanh
                                   ).then_inc(z_ready, 1)

                def v_squares(t):
                    act.wait_ge(z_ready, 4 * t + 2)
                    if t >= 2:
                        act.wait_ge(vr_ready, t - 1)
                    act.wait_ge(ss_ready, min(t + 2, TT))
                    act.activation(junk[:], z[:, t % 2, D:], ACT.Square,
                                   accum_out=vss[:, t % 2:t % 2 + 1]).then_inc(vss_ready, 1)

                def gT_out(t):
                    for half in range(2):
                        act.wait_ge(gT_raw, 2 * t + half + 1)
                        if t >= 1:
                            act.wait_ge(gT_stored, 16 * t)
                        act.activation(gT[:, 4 * half:4 * half + 4, :],
                                       psum[:, half, :].rearrange("p (k n) -> p k n", k=4), ACT.Copy
                                       ).then_inc(gT_ready, 1)

                squares(0)
                for n in range(NA):
                    w_split(n)
                hT_split(0)
                for n in range(NA, 2 * KT):
                    w_split(n)
                    if n == 4:
                        squares(1)
                for slot in range(TT + 2):
                    if slot < TT:
                        gelu(slot, 0)
                        gelu(slot, 1)
                        v_squares(slot)
                    if 0 <= slot - 2 < TT:
                        gT_out(slot - 2)
                    if slot < TT:
                        gelu(slot, 2)
                    if slot + 1 < TT:
                        hT_split(slot + 1)
                    if slot < TT:
                        gelu(slot, 3)
                    if slot + 2 < TT:
                        squares(slot + 2)

            @block.vector
            def _(dve):
                def norm(t):
                    if t == 0:
                        dve.wait_ge(tab_in, 32)
                    if t == SAMPLE:
                        dve.wait_ge(stab_in, 32 * NB)
                    dve.wait_ge(rstd_ready, t + 1)
                    dve.scalar_tensor_tensor(x[:, t % 3, :], x[:, t % 3, :], rstd[:, t % 2:t % 2 + 1], scale_t[:],
                                             ALU.mult, ALU.mult).then_inc(xn_ready, 1)
                    dve.wait_ge(xn_ready, t + 1)
                    dve.tensor_tensor(x[:, t % 3, :], x[:, t % 3, :], shift_t[:], ALU.add).then_inc(h_ready, 1)

                def w_split(n):
                    half, k = 1 - n // KT, n % KT
                    cols = slice(half * D, (half + 1) * D)
                    dve.wait_ge(w_hi_ready, n + 1)
                    dve.tensor_tensor(w_lo[:, k, cols], raw[n % WR], f(w_hi[:, k, cols]), ALU.subtract
                                      ).then_inc(w_ready, 1)

                def hT_split(t):
                    for half in range(2):
                        dve.wait_ge(hT_hi_ready, 2 * t + half + 1)
                        ks = slice(4 * half, 4 * half + 4)
                        dve.tensor_tensor(hT_lo[t % 2][:, ks, :], psum[:, half, :].rearrange("p (k n) -> p k n", k=4),
                                          f(hT_hi[t % 2][:, ks, :]), ALU.subtract).then_inc(hT_ready, 1)

                def norm_v(t):
                    if t == 0:
                        dve.wait_ge(const_in, 16 * (2 + NB))
                    dve.wait_ge(vr_ready, t + 1)
                    v = z[:, t % 2, D:]
                    dve.scalar_tensor_tensor(v, v, vr[:, t % 2:t % 2 + 1], g_v[:], ALU.mult, ALU.mult).then_inc(v_ready, 1)

                def gated(t):
                    dve.wait_ge(mix_raw, t + 1)
                    dve.wait_ge(z_ready, 4 * t + 4)
                    for g in range(G):
                        u = z[:, t % 2, g * P:(g + 1) * P]
                        last = dve.scalar_tensor_tensor(u, psum[:, 6 + g // 4, (g % 4) * P:(g % 4 + 1) * P],
                                                        bs[:, int(t == SAMPLE), g:g + 1], u, ALU.add, ALU.mult)
                    last.then_inc(g_ready, 1)

                norm(0)
                for n in range(NA):
                    w_split(n)
                hT_split(0)
                for n in range(NA, 2 * KT):
                    w_split(n)
                    if n == 8:
                        norm(1)
                for slot in range(TT + 1):
                    if slot < TT:
                        norm_v(slot)
                    if slot + 1 < TT:
                        hT_split(slot + 1)
                    if 0 <= slot - 1 < TT:
                        gated(slot - 1)
                    if slot + 2 < TT:
                        norm(slot + 2)

            @block.tensor
            def _(pe):
                def transposes(t):
                    pe.wait_ge(h_ready, t + 1)
                    if t >= 1:
                        pe.wait_ge(hT_ready, 2 * t)
                    if t >= 3:
                        pe.wait_ge(gT_ready, 2 * (t - 2))
                    for k in range(KT):
                        mm = pe.transpose(psum[:, k // 4, (k % 4) * P:(k % 4 + 1) * P],
                                          x[:, t % 3, k * P:(k + 1) * P], ident[:])
                        if k % 4 == 3:
                            mm.then_inc(hT_raw, 1)

                def product(t, n):
                    c = CHUNKS[n]
                    cols = slice(c * 512, (c + 1) * 512)
                    pe.wait_ge(hT_ready, 2 * t + 2)
                    if t >= 1:
                        pe.wait_ge(z_ready, 4 * (t - 1) + n + 1)
                    for k in range(KT):
                        if t == 0:
                            pe.wait_ge(w_ready, (n // 2) * KT + k + 1)
                        mm = mm3(pe, psum[:, 2 + n, :], hT_hi[t % 2][:, k, :], hT_lo[t % 2][:, k, :],
                                 w_hi[:, k, cols], w_lo[:, k, cols], k == 0, k == KT - 1)
                    mm.then_inc(z_raw, 1)

                def mix(t):
                    if t == 0:
                        pe.wait_ge(ws_ready, 1)
                        pe.wait_ge(blocks_in, 16 * NB)
                    pe.wait_ge(v_ready, t + 1)
                    if t >= 1:
                        pe.wait_ge(g_ready, t)
                    for g in range(G):
                        mm = pe.matmul(psum[:, 6 + g // 4, (g % 4) * P:(g % 4 + 1) * P], ws[:, int(t == SAMPLE), g, :],
                                       z[:, t % 2, D + g * P:D + (g + 1) * P], start=True, stop=True)
                    mm.then_inc(mix_raw, 1)

                def turn(t):
                    pe.wait_ge(g_ready, t + 1)
                    if t + 1 < TT:
                        pe.wait_ge(hT_ready, min(2 * (t + 3), 2 * TT))
                    if t >= 1:
                        pe.wait_ge(gT_ready, 2 * t)
                    for k in range(KT):
                        mm = pe.transpose(psum[:, k // 4, (k % 4) * P:(k % 4 + 1) * P],
                                          z[:, t % 2, k * P:(k + 1) * P], ident[:])
                        if k % 4 == 3:
                            mm.then_inc(gT_raw, 1)

                transposes(0)
                for slot in range(TT + 2):
                    if slot < TT:
                        product(slot, 0)
                        product(slot, 1)
                    if 0 <= slot - 2 < TT:
                        turn(slot - 2)
                    if slot < TT:
                        product(slot, 2)
                    if slot + 1 < TT:
                        transposes(slot + 1)
                    if slot < TT:
                        product(slot, 3)
                    if 0 <= slot - 1 < TT:
                        mix(slot - 1)


def build_program(nc, io):
    Phase.semaphores = []
    with ExitStack() as ctx:
        psum = ctx.enter_context(nc.psum_tensor("psum", [P, 8, 512], F32))
        ident = ctx.enter_context(nc.sbuf_tensor("ident", [P, P], F32))
        load_constants(nc, io, ident)
        c_silu = ctx.enter_context(nc.sbuf_tensor("c_silu", [P, KT, 32], F32))
        with ExitStack() as latents:
            def split(name, shape):
                return [latents.enter_context(nc.sbuf_tensor(f"{name}_{part}", shape, F32R)) for part in ("hi", "lo")]
            cqT = split("cqT", [P, QL // P, NTOK])
            ckvT = split("ckvT", [P, KL // P, NTOK])
            krT = split("krT", [P, NTOK])
            latent_phase(nc, psum, io, ident, c_silu, cqT, ckvT, krT)
            prompt_attention_phase(nc, psum, io, ident, c_silu, cqT, ckvT, krT)
            sample_phases(nc, psum, io, ident, cqT, ckvT, krT)
        Phase.recycle_semaphores(nc)
        mlp_half(nc, psum, io, ident, c_silu, 0, io["x"], io["x_mid"])
        gating_phase(nc, psum, io, ident)
        mlp_half(nc, psum, io, ident, c_silu, 1, io["x_mid"], io["y"])


def sample_phases(nc, psum, io, ident, cqT, ckvT, krT):
    with ExitStack() as ctx:
        def sb(name, shape, dt=F32):
            return ctx.enter_context(nc.sbuf_tensor(f"sample_{name}", shape, dt))
        wuk = [sb(f"wuk_{part}", [P, 2, D], F32R) for part in ("hi", "lo")]
        qe = [sb(f"qe_{part}", [P, 2, NB, P], F32R) for part in ("hi", "lo")]
        qrT = sb("qrT", [P, NB, P])
        s_new = sb("s_new", [P, P])
        sample_query_phase(nc, psum, io, ident, cqT, ckvT, krT, wuk, qe, qrT, s_new)
        sample_attention_phase(nc, psum, io, ident, wuk, qe, qrT, s_new)


def mlp_half(nc, psum, io, ident, c_silu, layer, x_from, x_to):
    with ExitStack() as ctx:
        hT = [ctx.enter_context(nc.sbuf_tensor(f"h2T{layer}_{part}", [P, KT, NTOK], F32R)) for part in ("hi", "lo")]
        project_phase(nc, psum, io, ident, layer, x_from, hT)
        ffn_phase(nc, psum, io, layer, hT, x_to, c_silu)


def load_constants(nc, io, ident):
    with Phase(nc, "const") as ph:
        loaded = ph.sem("loaded")
        with nc.Block() as block:
            @block.sync
            def _(sp):
                sp.dma_start(ident[:], io["ident"]).then_inc(loaded, 16)
                sp.wait_ge(loaded, 16)


SCRATCH = {
    "mod": (2, 1 + NB, 6 * D),
    "mixT": (KT, P, NTOK),
    "x_res": (TT, P, D),
    "x_mid": (TT, P, D),
}
OUTPUTS = {
    "y": (TT, P, D), "ckv_new": (TT, P, KL), "kpe_new": (TT, P, DR), "v_new": (P, D),
}


def lay_out(v):
    def a(name):
        return np.asarray(v[name])

    def rows(w):
        return w.reshape(-1, P, w.shape[-1])

    ada_w = a("ada_w")

    def steps(w, n):
        return w.reshape(2, HK, P, -1, 4 * n).transpose(3, 0, 2, 1, 4)

    def tables(layer, n):
        zeros, ones = np.zeros(D, np.float32), np.ones(D, np.float32)
        plus = np.concatenate([zeros, ones, zeros, zeros, ones, zeros])
        gain = np.concatenate([ones, a("norm1_g")[layer], ones, ones, a("norm2_g")[layer], ones])
        return np.stack([a("ada_b")[layer], plus, gain]).reshape(3, -1, 4, n).transpose(1, 2, 0, 3)

    pair = 2 * (DN + DR)
    uk, uv = a("mla_w_uk")[0], a("mla_w_uv")[0]
    kv = np.concatenate([uk.reshape(2, P, 4, 2 * DN), uv.reshape(2, P, 4, 2 * DN)], axis=3)
    cq = a("mla_w_q_up")[0].reshape(QL // P, P, 4, pair)
    c = np.concatenate([a("c_prompt"), a("c_sample")])
    cache = a("cache_ckv")[0]
    out = {
        "x": np.concatenate([a("x_prompt").reshape(SEQ, D), a("x_sample").reshape(NB * TS, D)]).reshape(TT, P, D),
        "c_cols": c.T.reshape(KT, P, 1 + NB).transpose(1, 0, 2),
        "ada_w_front": ada_w[0][:, :FRONT].reshape(KT, P, FRONT),
        "ada_w_att": steps(ada_w[0][:, FRONT:], ATT_N),
        "ada_w_ffn": steps(ada_w[1], FFN_N),
        "ada_tab_front": tables(0, FRONT // 4)[0],
        "ada_tab_att": tables(0, ATT_N)[FRONT // (4 * ATT_N):],
        "ada_tab_ffn": tables(1, FFN_N),
        "w1": a("ffn_w1").reshape(2, KT, P, FT, P).transpose(0, 3, 2, 1, 4),
        "w2": a("ffn_w2").reshape(2, FT, P, D),
        "w_in": rows(a("mla_w_in")[0]).transpose(1, 0, 2),
        "g_qa": a("mla_g_qa")[0], "g_kva": a("mla_g_kva")[0], "g_kr": a("mla_g_kr")[0],
        "g_qn": a("mla_g_qn")[0], "g_qr": a("mla_g_qr")[0], "g_kn": a("mla_g_kn")[0],
        "w_q_pair": cq.transpose(2, 1, 0, 3),
        "w_kv_pair": kv.transpose(2, 1, 0, 3),
        "w_q": rows(a("mla_w_q_up")[0]).transpose(1, 0, 2),
        "w_uk": uk.reshape(2, P, H * DN).transpose(1, 0, 2),
        "w_ukT": uk.transpose(2, 1, 0),
        "w_uv": uv.reshape(2, P, H * DN).transpose(1, 0, 2),
        "w_o0": rows(a("mla_w_o")[0]), "w_o1": rows(a("cm_w_o")[0]),
        "cache": cache.reshape(NB, PAST // P, P, KL).transpose(0, 2, 1, 3),
        "cacheT": cache.reshape(NB, PAST, 2, P).transpose(0, 3, 2, 1),
        "kpeT": a("cache_kpe")[0].transpose(0, 2, 1),
        "cm_w_in": rows(a("cm_w_in")[0]),
        "cm_g_v": a("cm_g_v")[0],
        "w_sT": a("cm_w_s")[0].transpose(2, 0, 1),
        "b_sT": a("cm_b_s")[0].T,
    }
    return {k: np.ascontiguousarray(x) for k, x in out.items()}


def constants():
    half = DR // 2
    pos = np.concatenate([np.arange(SEQ), np.tile(PAST + np.arange(TS), NB)]).astype(np.float32)
    inv = (np.float32(1.0) / (np.float32(10000.0) ** (np.arange(half, dtype=np.float32) / np.float32(half)))).astype(np.float32)
    ang = pos[:, None] * inv[None, :]
    cos, sin = np.cos(ang), np.sin(ang)

    def tiles(t):
        return np.ascontiguousarray(t.reshape(TT, P, DR).transpose(1, 0, 2)).astype(np.float32)

    r, key = np.arange(P)[:, None, None], np.arange(2 * P)[None, None, :]
    seen = key < P * np.arange(2)[None, :, None] + 64 * (r // 64 + 1)
    rows = np.stack([np.zeros(P, int), 1 + np.arange(P) // TS])
    sel = np.arange(P)[:, None, None, None] == 32 * np.arange(4)[None, None, :, None] + rows[None, :, None, :]
    sel = sel.astype(np.float32)
    return {
        "ident": np.eye(P, dtype=np.float32),
        "mod_sel": np.ascontiguousarray(sel),
        "ident_bf": np.eye(P, dtype=np.float32).astype(mybir.dt.np(BF16)),
        "mask": np.where(seen, 0.0, -1e30).astype(mybir.dt.np(BF16)),
        "cos": tiles(np.concatenate([cos, cos], axis=1)),
        "sin": tiles(np.concatenate([-sin, sin], axis=1)),
    }


def kernel(**inputs):
    from concourse import bacc
    from concourse.bass_utils import run_bass_kernel_spmd

    arrays = {**lay_out(inputs), **constants()}
    nc = bacc.Bacc("TRN2", target_bir_lowering=False, num_devices=1)
    io = {k: nc.dram_tensor(f"in_{k}", v.shape, mybir.dt.from_np(v.dtype), kind="ExternalInput").ap()
          for k, v in arrays.items()}
    io |= {k: nc.dram_tensor(f"out_{k}", s, F32, kind="ExternalOutput").ap() for k, s in OUTPUTS.items()}
    io |= {k: nc.dram_tensor(f"scratch_{k}", s, F32).ap() for k, s in SCRATCH.items()}
    build_program(nc, io)
    r = run_bass_kernel_spmd(nc, [{f"in_{k}": v for k, v in arrays.items()}], core_ids=[0]).results[0]
    y, ckv, kpe, v = (r[f"out_{k}"] for k in ("y", "ckv_new", "kpe_new", "v_new"))
    return (y[:SAMPLE].reshape(1, SEQ, D), y[SAMPLE].reshape(NB, TS, D),
            ckv[:SAMPLE].reshape(1, 1, SEQ, KL), kpe[:SAMPLE].reshape(1, 1, SEQ, DR),
            ckv[SAMPLE].reshape(1, NB, TS, KL), kpe[SAMPLE].reshape(1, NB, TS, DR),
            v.reshape(1, NB, TS, D))
```
